# Optimizing a Trainium2 kernel written in Bass

```python
import jax
import jax.numpy as jnp
from jax import lax
import numpy as np
import math
import jax, jax.numpy as jnp

D_MODEL = 1024
BATCH = 1
SEQ = 256
DEPTH = 2

CONV_WIDTH = 512
CONV_GROUPS = 8
CONV_K = 3
MLA_HEADS = 8
MLA_Q_LORA = 256
MLA_KV_LORA = 128
MLA_NOPE = 64
MLA_ROPE = 32
MLA_V = 64
MLA_QK = MLA_NOPE + MLA_ROPE
ROPE_THETA = 10000.0
DIL_PATTERNS = ((128, 1), (512, 4), (2048, 16))
DIL_GROUPS = len(DIL_PATTERNS)
DIL_HEADS = 8
DIL_HEAD_DIM = 64
DIL_WIDTH = DIL_HEADS * DIL_HEAD_DIM
N_BRANCH = 3
Q_BLOCK = 128
EPS = 1e-6

SPLIT_SIZES = ((CONV_WIDTH,) * 4
               + (MLA_Q_LORA, MLA_KV_LORA, MLA_ROPE, MLA_HEADS * MLA_V)
               + (DIL_GROUPS * DIL_WIDTH,) * 3 + (DIL_WIDTH,)
               + (N_BRANCH * D_MODEL,))
SPLIT_POINTS = tuple(int(v) for v in np.cumsum(SPLIT_SIZES)[:-1])
N_IN = int(sum(SPLIT_SIZES))


def rmsnorm(x, g):
    xf = x.astype(jnp.float32)
    y = xf * lax.rsqrt(jnp.mean(xf * xf, axis=-1, keepdims=True) + EPS)
    return (y * g.astype(jnp.float32)).astype(x.dtype)

def rope_tables(S):
    inv = ROPE_THETA ** (-jnp.arange(0, MLA_ROPE, 2, dtype=jnp.float32) / MLA_ROPE)
    ang = jnp.arange(S, dtype=jnp.float32)[:, None] * inv[None, :]
    return jnp.cos(ang), jnp.sin(ang)

def apply_rope(t, cos, sin):
    tf = t.astype(jnp.float32)
    t1, t2 = jnp.split(tf, 2, axis=-1)
    c = cos[None, :, None, :]
    s = sin[None, :, None, :]
    return jnp.concatenate([t1 * c - t2 * s, t2 * c + t1 * s], axis=-1).astype(t.dtype)

def alibi_slopes():
    n = DIL_GROUPS * DIL_HEADS
    m = 2.0 ** (-8.0 * jnp.arange(1, n + 1, dtype=jnp.float32) / n)
    return m.reshape(DIL_GROUPS, DIL_HEADS)

def causal_block_attention(q, k, v, scale):
    B, H, S, Dk = q.shape
    Dv = v.shape[-1]
    nqb = S // Q_BLOCK
    qb = q.reshape(B, H, nqb, Q_BLOCK, Dk).transpose(2, 0, 1, 3, 4)
    kf = k.astype(jnp.float32)
    vf = v.astype(jnp.float32)
    kpos = jnp.arange(S)

    def one_block(args):
        qblk, i = args
        s = jnp.einsum('bhqc,bhkc->bhqk', qblk.astype(jnp.float32), kf) * scale
        qpos = i * Q_BLOCK + jnp.arange(Q_BLOCK)
        s = jnp.where(kpos[None, :] <= qpos[:, None], s, -jnp.inf)
        p = jax.nn.softmax(s, axis=-1)
        return jnp.einsum('bhqk,bhkc->bhqc', p, vf)

    o = lax.map(one_block, (qb, jnp.arange(nqb)))
    return o.transpose(1, 2, 0, 3, 4).reshape(B, H, S, Dv)

def dilated_group_attention(q, k, v, slopes, dilation, n_back):
    B, S, H, hd = q.shape
    L = S // dilation
    nb = -(-L // Q_BLOCK)
    Lp = nb * Q_BLOCK

    def to_sub(t):
        return t.reshape(B, L, dilation, H, hd).transpose(0, 2, 3, 1, 4)

    qs = jnp.pad(to_sub(q).astype(jnp.float32), ((0, 0), (0, 0), (0, 0), (0, Lp - L), (0, 0)))
    qs = qs.reshape(B, dilation, H, nb, Q_BLOCK, hd)

    def windows(t):
        tp = jnp.pad(to_sub(t).astype(jnp.float32), ((0, 0), (0, 0), (0, 0), (Q_BLOCK, Lp - L), (0, 0)))
        tb = tp.reshape(B, dilation, H, nb + 1, Q_BLOCK, hd)
        return jnp.concatenate([tb[:, :, :, :-1], tb[:, :, :, 1:]], axis=4)

    kw = windows(k)
    vw = windows(v)
    qq = jnp.arange(Q_BLOCK)[:, None]
    kk = jnp.arange(2 * Q_BLOCK)[None, :]
    j = Q_BLOCK + qq - kk
    key_idx = (jnp.arange(nb)[:, None, None] - 1) * Q_BLOCK + kk[None]
    valid = (j >= 0) & (j <= n_back) & (key_idx >= 0)
    dist = (dilation * j).astype(jnp.float32)
    bias = -slopes.reshape(1, 1, H, 1, 1, 1) * dist
    scale = DIL_HEAD_DIM ** -0.5
    s = jnp.einsum('bdhnqc,bdhnkc->bdhnqk', qs, kw) * scale + bias
    s = jnp.where(valid, s, -jnp.inf)
    lse = jax.nn.logsumexp(s, axis=-1)
    p = jnp.exp(s - lse[..., None])
    o = jnp.einsum('bdhnqk,bdhnkc->bdhnqc', p, vw)
    o = o.reshape(B, dilation, H, Lp, hd)[:, :, :, :L]
    lse = lse.reshape(B, dilation, H, Lp)[:, :, :, :L]
    o = o.transpose(0, 3, 1, 2, 4).reshape(B, S, H, hd)
    lse = lse.transpose(0, 3, 1, 2).reshape(B, S, H)
    return o, lse

def hybrid_layer(x, norm_g, w_in, b_gate, conv_w, conv_b, q_a_norm_g, w_uq, kv_a_norm_g, w_ukv,
                 mla_q_norm_g, mla_k_norm_g, dil_q_norm_g, dil_k_norm_g,
                 w_out_a, w_out_b, w_out_c, w_o, cos, sin, slopes):
    B, S, _ = x.shape
    h = rmsnorm(x, norm_g)
    proj = h @ w_in
    (a_b, a_c, a_x, a_z, c_q, c_kv, k_pe, b_z, dq, dk, dv, c_z, gate_pre) = jnp.split(proj, SPLIT_POINTS, axis=-1)

    u = a_c * a_x
    up = jnp.pad(u, ((0, 0), (CONV_K - 1, 0), (0, 0)))
    conv = conv_b
    for tap in range(CONV_K):
        conv = conv + up[:, tap:tap + S] * conv_w[tap]
    y_a = a_b * conv * jax.nn.silu(a_z)

    q = (rmsnorm(c_q, q_a_norm_g) @ w_uq).reshape(B, S, MLA_HEADS, MLA_QK)
    kv = (rmsnorm(c_kv, kv_a_norm_g) @ w_ukv).reshape(B, S, MLA_HEADS, MLA_NOPE + MLA_V)
    k_nope, v = jnp.split(kv, [MLA_NOPE], axis=-1)
    k = jnp.concatenate([k_nope, jnp.broadcast_to(k_pe[:, :, None, :], (B, S, MLA_HEADS, MLA_ROPE))], axis=-1)
    q = rmsnorm(q, mla_q_norm_g)
    k = rmsnorm(k, mla_k_norm_g)
    q = jnp.concatenate([q[..., :MLA_NOPE], apply_rope(q[..., MLA_NOPE:], cos, sin)], axis=-1)
    k = jnp.concatenate([k[..., :MLA_NOPE], apply_rope(k[..., MLA_NOPE:], cos, sin)], axis=-1)
    o_b = causal_block_attention(q.transpose(0, 2, 1, 3), k.transpose(0, 2, 1, 3), v.transpose(0, 2, 1, 3),
                                 MLA_QK ** -0.5)
    o_b = o_b.transpose(0, 2, 1, 3).reshape(B, S, MLA_HEADS * MLA_V).astype(x.dtype)
    y_b = o_b * jax.nn.silu(b_z)

    dq = rmsnorm(dq.reshape(B, S, DIL_GROUPS, DIL_HEADS, DIL_HEAD_DIM), dil_q_norm_g[:, None, :])
    dk = rmsnorm(dk.reshape(B, S, DIL_GROUPS, DIL_HEADS, DIL_HEAD_DIM), dil_k_norm_g[:, None, :])
    dv = dv.reshape(B, S, DIL_GROUPS, DIL_HEADS, DIL_HEAD_DIM)
    outs = []
    lses = []
    for gi, (window, dilation) in enumerate(DIL_PATTERNS):
        o_g, lse_g = dilated_group_attention(dq[:, :, gi], dk[:, :, gi], dv[:, :, gi], slopes[gi],
                                             dilation, window // dilation)
        outs.append(o_g)
        lses.append(lse_g)
    alpha = jax.nn.softmax(jnp.stack(lses, axis=0), axis=0)
    o_c = jnp.sum(alpha[..., None] * jnp.stack(outs, axis=0), axis=0)
    o_c = o_c.reshape(B, S, DIL_WIDTH).astype(x.dtype)
    y_c = o_c * jax.nn.silu(c_z)

    g_a, g_b, g_c = jnp.split(jax.nn.sigmoid(gate_pre + b_gate), N_BRANCH, axis=-1)
    merged = g_a * (y_a @ w_out_a) + g_b * (y_b @ w_out_b) + g_c * (y_c @ w_out_c)
    return x + merged @ w_o

def first_inputs(seed: int = 0) -> dict:
    key = jax.random.key(seed)
    ks = jax.random.split(key, 18)
    f32 = jnp.float32

    def nrm(k, shape, scale):
        return jax.random.normal(k, shape, f32) * scale

    def gain(k, shape):
        return 1.0 + 0.02 * jax.random.normal(k, shape, f32)

    Ld = DEPTH
    return {
        'x': jax.random.normal(ks[0], (BATCH, SEQ, D_MODEL), f32),
        'norm_g': gain(ks[1], (Ld, D_MODEL)),
        'w_in': nrm(ks[2], (Ld, D_MODEL, N_IN), D_MODEL ** -0.5),
        'b_gate': nrm(ks[3], (Ld, N_BRANCH * D_MODEL), 0.1),
        'conv_w': nrm(ks[4], (Ld, CONV_K, CONV_WIDTH), CONV_K ** -0.5),
        'conv_b': nrm(ks[5], (Ld, CONV_WIDTH), 0.02),
        'q_a_norm_g': gain(ks[6], (Ld, MLA_Q_LORA)),
        'w_uq': nrm(ks[7], (Ld, MLA_Q_LORA, MLA_HEADS * MLA_QK), MLA_Q_LORA ** -0.5),
        'kv_a_norm_g': gain(ks[8], (Ld, MLA_KV_LORA)),
        'w_ukv': nrm(ks[9], (Ld, MLA_KV_LORA, MLA_HEADS * (MLA_NOPE + MLA_V)), MLA_KV_LORA ** -0.5),
        'mla_q_norm_g': gain(ks[10], (Ld, MLA_QK)),
        'mla_k_norm_g': gain(ks[11], (Ld, MLA_QK)),
        'dil_q_norm_g': gain(ks[12], (Ld, DIL_GROUPS, DIL_HEAD_DIM)),
        'dil_k_norm_g': gain(ks[13], (Ld, DIL_GROUPS, DIL_HEAD_DIM)),
        'w_out_a': nrm(ks[14], (Ld, CONV_WIDTH, D_MODEL), CONV_WIDTH ** -0.5),
        'w_out_b': nrm(ks[15], (Ld, MLA_HEADS * MLA_V, D_MODEL), (MLA_HEADS * MLA_V) ** -0.5),
        'w_out_c': nrm(ks[16], (Ld, DIL_WIDTH, D_MODEL), DIL_WIDTH ** -0.5),
        'w_o': nrm(ks[17], (Ld, D_MODEL, D_MODEL), D_MODEL ** -0.5),
    }

def first_block(x, norm_g, w_in, b_gate, conv_w, conv_b, q_a_norm_g, w_uq, kv_a_norm_g, w_ukv,
              mla_q_norm_g, mla_k_norm_g, dil_q_norm_g, dil_k_norm_g, w_out_a, w_out_b, w_out_c, w_o):
    cos, sin = rope_tables(x.shape[1])
    slopes = alibi_slopes()
    for l in range(DEPTH):
        x = hybrid_layer(x, norm_g[l], w_in[l], b_gate[l], conv_w[l], conv_b[l], q_a_norm_g[l], w_uq[l],
                         kv_a_norm_g[l], w_ukv[l], mla_q_norm_g[l], mla_k_norm_g[l], dil_q_norm_g[l],
                         dil_k_norm_g[l], w_out_a[l], w_out_b[l], w_out_c[l], w_o[l], cos, sin, slopes)
    return x


DEPTH_2 = 1

CTX_LEN = 256
GRID_W = 64
HEAD_DIM = 64
GQA_HEADS = 8
GQA_KV_HEADS = 2
GQA_GROUP = GQA_HEADS // GQA_KV_HEADS
DIFF_HEADS = 4
DIFF_V_DIM = 2 * HEAD_DIM
MIX_WIDTH = GQA_HEADS * HEAD_DIM + DIFF_HEADS * DIFF_V_DIM
A_Q_COLS = GQA_HEADS * HEAD_DIM
A_KV_COLS = GQA_KV_HEADS * HEAD_DIM
B_QK_COLS = DIFF_HEADS * 2 * HEAD_DIM
B_V_COLS = DIFF_HEADS * DIFF_V_DIM
QKV_COLS = A_Q_COLS + 2 * A_KV_COLS + 2 * B_QK_COLS + B_V_COLS
N_EXPERTS = 32
TOP_K = 4
D_FF = D_MODEL
SWIGLU_ALPHA = 1.702
SWIGLU_LIMIT = 7.0
EXPERT_BLOCK = 128
N_MOD = 6


def rms_norm(x, g):
    xf = x.astype(jnp.float32)
    y = xf * lax.rsqrt(jnp.mean(xf * xf, axis=-1, keepdims=True) + EPS)
    return (y * g.astype(jnp.float32)).astype(x.dtype)

def modulate(h, shift, scale):
    return h * (1 + scale) + shift

def axial_rope_tables(n_tokens):
    rows = n_tokens // GRID_W
    row = jnp.broadcast_to(jnp.arange(rows, dtype=jnp.float32)[:, None], (rows, GRID_W)).reshape(-1)
    col = jnp.broadcast_to(jnp.arange(GRID_W, dtype=jnp.float32)[None, :], (rows, GRID_W)).reshape(-1)
    n_freq = HEAD_DIM // 4
    inv_freq = ROPE_THETA ** (-jnp.arange(n_freq, dtype=jnp.float32) / n_freq)
    ang = jnp.stack([row[:, None] * inv_freq, col[:, None] * inv_freq], axis=1)
    return jnp.cos(ang), jnp.sin(ang)

def apply_axial_rope(x, cos, sin):
    b, t, h, _ = x.shape
    xr = x.reshape(b, t, h, 2, 2, HEAD_DIM // 4)
    x1, x2 = xr[..., 0, :], xr[..., 1, :]
    cs = cos[None, :, None]
    sn = sin[None, :, None]
    out = jnp.stack([x1 * cs - x2 * sn, x2 * cs + x1 * sn], axis=-2)
    return out.reshape(x.shape).astype(x.dtype)

def split_projection(p):
    b, t, _ = p.shape
    offs = [A_Q_COLS, A_Q_COLS + A_KV_COLS, A_Q_COLS + 2 * A_KV_COLS,
            A_Q_COLS + 2 * A_KV_COLS + B_QK_COLS, A_Q_COLS + 2 * A_KV_COLS + 2 * B_QK_COLS]
    qa, ka, va, qb, kb, vb = jnp.split(p, offs, axis=-1)
    qa = qa.reshape(b, t, GQA_HEADS, HEAD_DIM)
    ka = ka.reshape(b, t, GQA_KV_HEADS, HEAD_DIM)
    va = va.reshape(b, t, GQA_KV_HEADS, HEAD_DIM)
    qb = qb.reshape(b, t, DIFF_HEADS, 2, HEAD_DIM)
    kb = kb.reshape(b, t, DIFF_HEADS, 2, HEAD_DIM)
    vb = vb.reshape(b, t, DIFF_HEADS, DIFF_V_DIM)
    return qa, ka, va, qb, kb, vb

def rope_diff(x, cos, sin):
    b, t, h, two, d = x.shape
    return apply_axial_rope(x.reshape(b, t, h * two, d), cos, sin).reshape(x.shape)

def gqa_attention(q, k, v, q_block):
    b, t, _, d = q.shape
    nb = t // q_block
    qb = q.reshape(b, nb, q_block, GQA_KV_HEADS, GQA_GROUP, d).transpose(1, 0, 3, 4, 2, 5)
    scale = d ** -0.5

    def block(qi):
        s = jnp.einsum('bhgqd,bkhd->bhgqk', qi, k, preferred_element_type=jnp.float32) * scale
        p = jax.nn.softmax(s, axis=-1)
        return jnp.einsum('bhgqk,bkhd->bqhgd', p.astype(v.dtype), v)

    o = lax.map(block, qb)
    return o.transpose(1, 0, 2, 3, 4, 5).reshape(b, t, GQA_HEADS * d)

def diff_attention(q, k, v, lam, sub_g, lambda_init, q_block):
    b, t, h, _, d = q.shape
    nb = t // q_block
    qb = q.reshape(b, nb, q_block, h, 2, d).transpose(1, 0, 3, 4, 2, 5)
    scale = d ** -0.5

    def block(qi):
        s = jnp.einsum('bhcqd,bkhcd->bhcqk', qi, k, preferred_element_type=jnp.float32) * scale
        p = jax.nn.softmax(s, axis=-1)
        a = p[:, :, 0] - lam * p[:, :, 1]
        return jnp.einsum('bhqk,bkhe->bqhe', a.astype(v.dtype), v)

    o = lax.map(block, qb).transpose(1, 0, 2, 3, 4).reshape(b, t, h, DIFF_V_DIM)
    o = rms_norm(o, sub_g) * (1.0 - lambda_init)
    return o.reshape(b, t, h * DIFF_V_DIM)

def moe_ffn(h, w_router, b_router, w_in, b_in, w_out, b_out):
    b, t, dm = h.shape
    n = b * t
    xt = h.reshape(n, dm)
    logits = (xt @ w_router + b_router).astype(jnp.float32)
    top_val, top_idx = lax.top_k(logits, TOP_K)
    gates = jax.nn.softmax(top_val, axis=-1)
    n_assign = n * TOP_K
    exp_flat = top_idx.reshape(-1).astype(jnp.int32)
    tok_flat = jnp.repeat(jnp.arange(n, dtype=jnp.int32), TOP_K)
    gate_flat = gates.reshape(-1)
    order = jnp.argsort(exp_flat)
    exp_sorted = exp_flat[order]
    counts = jax.ops.segment_sum(jnp.ones_like(exp_flat), exp_flat, num_segments=N_EXPERTS)
    starts = jnp.cumsum(counts) - counts
    padded = (counts + EXPERT_BLOCK - 1) // EXPERT_BLOCK * EXPERT_BLOCK
    pad_ends = jnp.cumsum(padded)
    pad_starts = pad_ends - padded
    dest = pad_starts[exp_sorted] + (jnp.arange(n_assign, dtype=jnp.int32) - starts[exp_sorted])
    n_blocks = -(-n_assign // EXPERT_BLOCK) + N_EXPERTS
    n_rows = n_blocks * EXPERT_BLOCK
    row_tok = jnp.full((n_rows,), n, jnp.int32).at[dest].set(tok_flat[order])
    row_gate = jnp.zeros((n_rows,), jnp.float32).at[dest].set(gate_flat[order])
    block_start = jnp.arange(n_blocks, dtype=jnp.int32) * EXPERT_BLOCK
    block_exp = jnp.minimum(jnp.searchsorted(pad_ends, block_start, side='right'), N_EXPERTS - 1)
    x_pad = jnp.concatenate([xt, jnp.zeros((1, dm), xt.dtype)], axis=0)
    xs = x_pad[row_tok].reshape(n_blocks, EXPERT_BLOCK, dm)

    def expert_block(args):
        xb, e = args
        hcat = xb @ w_in[e] + b_in[e]
        x_glu = jnp.minimum(hcat[:, :D_FF], SWIGLU_LIMIT)
        x_lin = jnp.clip(hcat[:, D_FF:], -SWIGLU_LIMIT, SWIGLU_LIMIT)
        act = x_glu * jax.nn.sigmoid(SWIGLU_ALPHA * x_glu) * (x_lin + 1)
        return act @ w_out[e] + b_out[e]

    ys = lax.map(expert_block, (xs, block_exp)).reshape(n_rows, dm)
    y = jax.ops.segment_sum(ys * row_gate[:, None].astype(ys.dtype), row_tok, num_segments=n + 1)[:n]
    return y.reshape(b, t, dm)

def second_inputs(seed: int = 0) -> dict:
    key = jax.random.key(seed)
    ks = jax.random.split(key, 21)
    f32 = jnp.float32
    nrm = lambda k, shape, s: jax.random.normal(k, shape, f32) * s
    return {
        'x': nrm(ks[0], (BATCH, SEQ, D_MODEL), 1.0),
        'c': nrm(ks[1], (BATCH, D_MODEL), 1.0),
        'ctx': nrm(ks[2], (BATCH, CTX_LEN, D_MODEL), 1.0),
        'c_ctx': nrm(ks[3], (D_MODEL,), 1.0),
        'w_ada': nrm(ks[4], (DEPTH_2, D_MODEL, N_MOD * D_MODEL), 0.5 * D_MODEL ** -0.5),
        'b_ada': nrm(ks[5], (DEPTH_2, N_MOD * D_MODEL), 0.02),
        'g_attn': 1.0 + nrm(ks[6], (DEPTH_2, D_MODEL), 0.05),
        'w_qkv': nrm(ks[7], (DEPTH_2, D_MODEL, QKV_COLS), D_MODEL ** -0.5),
        'gqa_q_norm': 1.0 + nrm(ks[8], (DEPTH_2, HEAD_DIM), 0.05),
        'gqa_k_norm': 1.0 + nrm(ks[9], (DEPTH_2, HEAD_DIM), 0.05),
        'diff_lambda': nrm(ks[10], (DEPTH_2, 4, HEAD_DIM), 0.1),
        'diff_subln': 1.0 + nrm(ks[11], (DEPTH_2, DIFF_V_DIM), 0.05),
        'w_o': nrm(ks[12], (DEPTH_2, MIX_WIDTH, D_MODEL), MIX_WIDTH ** -0.5),
        'g_ffn': 1.0 + nrm(ks[13], (DEPTH_2, D_MODEL), 0.05),
        'w_router': nrm(ks[14], (DEPTH_2, D_MODEL, N_EXPERTS), D_MODEL ** -0.5),
        'b_router': nrm(ks[15], (DEPTH_2, N_EXPERTS), 0.01),
        'w_in': nrm(ks[16], (DEPTH_2, N_EXPERTS, D_MODEL, 2 * D_FF), D_MODEL ** -0.5),
        'b_in': nrm(ks[17], (DEPTH_2, N_EXPERTS, 2 * D_FF), 0.02),
        'w_out': nrm(ks[18], (DEPTH_2, N_EXPERTS, D_FF, D_MODEL), D_FF ** -0.5),
        'b_out': nrm(ks[19], (DEPTH_2, N_EXPERTS, D_MODEL), 0.02),
        'g_final': 1.0 + nrm(ks[20], (D_MODEL,), 0.05),
    }

def second_block(x, c, ctx, c_ctx, w_ada, b_ada, g_attn, w_qkv, gqa_q_norm, gqa_k_norm, diff_lambda,
              diff_subln, w_o, g_ffn, w_router, b_router, w_in, b_in, w_out, b_out, g_final):
    n_tok = x.shape[1]
    cos, sin = axial_rope_tables(n_tok)
    for l in range(DEPTH_2):
        lambda_init = 0.8 - 0.6 * math.exp(-0.3 * l)
        mod_x = (jax.nn.silu(c) @ w_ada[l] + b_ada[l])[:, None, :]
        mod_c = (jax.nn.silu(c_ctx) @ w_ada[l] + b_ada[l])[None, None, :]
        sh1, sc1, gt1, sh2, sc2, gt2 = jnp.split(mod_x, N_MOD, axis=-1)
        csh1, csc1, cgt1, csh2, csc2, cgt2 = jnp.split(mod_c, N_MOD, axis=-1)

        h = modulate(rms_norm(x, g_attn[l]), sh1, sc1)
        hc = modulate(rms_norm(ctx, g_attn[l]), csh1, csc1)
        qa, ka, va, qb, kb, vb = split_projection(h @ w_qkv[l])
        qa_c, ka_c, va_c, qb_c, kb_c, vb_c = split_projection(hc @ w_qkv[l])
        qa = apply_axial_rope(rms_norm(qa, gqa_q_norm[l]), cos, sin)
        ka = apply_axial_rope(rms_norm(ka, gqa_k_norm[l]), cos, sin)
        ka_c = rms_norm(ka_c, gqa_k_norm[l])
        qb = rope_diff(qb, cos, sin)
        kb = rope_diff(kb, cos, sin)
        lamf = diff_lambda[l].astype(jnp.float32)
        lam = jnp.exp(jnp.sum(lamf[0] * lamf[1])) - jnp.exp(jnp.sum(lamf[2] * lamf[3])) + lambda_init
        ka_all = jnp.concatenate([ka_c, ka], axis=1)
        va_all = jnp.concatenate([va_c, va], axis=1)
        kb_all = jnp.concatenate([kb_c, kb], axis=1)
        vb_all = jnp.concatenate([vb_c, vb], axis=1)
        lat_mix = jnp.concatenate([
            gqa_attention(qa, ka_all, va_all, Q_BLOCK),
            diff_attention(qb, kb_all, vb_all, lam, diff_subln[l], lambda_init, Q_BLOCK),
        ], axis=-1)
        x = x + gt1 * (lat_mix @ w_o[l])
        x = x + gt2 * moe_ffn(modulate(rms_norm(x, g_ffn[l]), sh2, sc2),
                              w_router[l], b_router[l], w_in[l], b_in[l], w_out[l], b_out[l])

        if l < DEPTH_2 - 1:
            qa_c = rms_norm(qa_c, gqa_q_norm[l])
            ctx_len = ctx.shape[1]
            ctx_mix = jnp.concatenate([
                gqa_attention(qa_c, ka_c, va_c, ctx_len),
                diff_attention(qb_c, kb_c, vb_c, lam, diff_subln[l], lambda_init, ctx_len),
            ], axis=-1)
            ctx = ctx + cgt1 * (ctx_mix @ w_o[l])
            ctx = ctx + cgt2 * moe_ffn(modulate(rms_norm(ctx, g_ffn[l]), csh2, csc2),
                                       w_router[l], b_router[l], w_in[l], b_in[l], w_out[l], b_out[l])
    return rms_norm(x, g_final)


def setup_inputs(seed=0):
    out = dict(first_inputs(seed))
    for name, value in second_inputs(seed + 1).items():
        if name != "x":
            out[name + "_2"] = value
    return out


def reference(
    x, norm_g, w_in, b_gate, conv_w, conv_b, q_a_norm_g, w_uq, kv_a_norm_g, w_ukv, mla_q_norm_g,
    mla_k_norm_g, dil_q_norm_g, dil_k_norm_g, w_out_a, w_out_b, w_out_c, w_o, c_2, ctx_2,
    c_ctx_2, w_ada_2, b_ada_2, g_attn_2, w_qkv_2, gqa_q_norm_2, gqa_k_norm_2, diff_lambda_2,
    diff_subln_2, w_o_2, g_ffn_2, w_router_2, b_router_2, w_in_2, b_in_2, w_out_2, b_out_2,
    g_final_2,
):
    x = first_block(
        x, norm_g, w_in, b_gate, conv_w, conv_b, q_a_norm_g, w_uq, kv_a_norm_g, w_ukv,
        mla_q_norm_g, mla_k_norm_g, dil_q_norm_g, dil_k_norm_g, w_out_a, w_out_b, w_out_c, w_o,
    )
    return second_block(
        x, c_2, ctx_2, c_ctx_2, w_ada_2, b_ada_2, g_attn_2, w_qkv_2, gqa_q_norm_2, gqa_k_norm_2,
        diff_lambda_2, diff_subln_2, w_o_2, g_ffn_2, w_router_2, b_router_2, w_in_2, b_in_2,
        w_out_2, b_out_2, g_final_2,
    )


_drawn_inputs = setup_inputs


def setup_inputs(seed=0):
    import zlib

    import numpy as np

    out = dict(_drawn_inputs(seed))
    spreads = {}
    factors = {'conv_b': 3.55,
     'q_a_norm_g': 8.0,
     'kv_a_norm_g': 8.0,
     'mla_q_norm_g': 7.841,
     'mla_k_norm_g': 7.309,
     'dil_q_norm_g': 8.0,
     'dil_k_norm_g': 6.934,
     'g_attn_2': 4.295,
     'gqa_q_norm_2': 8.0,
     'gqa_k_norm_2': 8.0,
     'diff_subln_2': 22.935,
     'b_router_2': 42.808,
     'b_in_2': 52.11,
     'b_out_2': 64.0,
     'g_ffn_2': 7.562}
    for name, (base, spread) in spreads.items():
        noise = np.random.default_rng([zlib.crc32(name.encode()), seed]).standard_normal(out[name].shape)
        drawn = base * np.exp(spread * noise) if base else spread * noise
        out[name] = jnp.asarray(drawn.astype(out[name].dtype))
    for name, factor in factors.items():
        out[name] = (out[name] * factor).astype(out[name].dtype)
    return out
```

```python
from contextlib import ExitStack

import concourse.bass as bass
from concourse import mybir

F32 = mybir.dt.float32
I32 = mybir.dt.int32
ALU = mybir.AluOpType
ACT = mybir.ActivationFunctionType
AX = mybir.AxisListType

P = 128
T = 256
TT = T // P
D = 1024
DC = D // P
LAYERS = 2
EPS = 1e-6
W = 512
HALF = 64
MQK, MROPE, MHEADS = 96, 32, 8
GROUPS, DHEADS = 3, 8
NEXP = 32
TOPK = 4
SLOTS = 64
MAXJOBS = 16
MASKED = -1.0e30
RING = 4
MRING = 6
TILE = 8 * W

COL_AB, COL_AC, COL_AX, COL_AZ, COL_LORA = 0, 512, 1024, 1536, 2048
COL_BZ, COL_DQ, COL_DK, COL_DV, COL_CZ, COL_GATE = 2464, 2976, 4512, 6048, 7584, 8096
N_IN = 11168
LORA = 416
N_QKV = 2304

UNITS = [("lora", 0, (t,)) for t in range(TT)]
UNITS += [("dq", 1 + g, (g, t)) for g in range(GROUPS) for t in range(TT)]
UNITS += [("mq", 4, (h, t)) for h in range(2) for t in range(TT)]
UNITS += [("mkv", 4, (h, t)) for h in range(2) for t in range(TT)]
UNITS += [("dk", 5 + g, (g, t)) for g in range(GROUPS) for t in range(TT)]
UNITS += [("dv", 8 + g, (g, t)) for g in range(GROUPS) for t in range(TT)]
UNITS += [("z", 11 + b, (b, p)) for b in range(2) for p in range(2)]
PREP = len(UNITS)
UNITS += [("ac", 13, (p,)) for p in range(2)]
UNITS += [("ax", 14, (p,)) for p in range(2)]
UNITS += [("ab", 15, (p,)) for p in range(2)]
UNITS += [("az", 16, (p,)) for p in range(2)]
UNITS += [("gate", 17 + n, (n, p)) for n in range(6) for p in range(2)]
FILL = len(UNITS)
UNITS += [("merge", 23 + b, (p, b)) for p in range(4) for b in range(3)]
MERGED = len(UNITS)
UNITS += [("out", 26 + n, (n, p)) for n in range(2) for p in range(2)]
NU = len(UNITS)
NT = 28
BANKS = 4
PER_BANK = NU // BANKS
assert NU % BANKS == 0 and NT % RING == 0
NORMED = [u for u, x in enumerate(UNITS) if x[0] in ("lora", "dq", "mq", "mkv", "dk")]
NN = len(NORMED)
ZUNITS = [u for u, x in enumerate(UNITS) if x[0] in ("z", "az")]
LAG = 2

JOBS = [("mla", h) for h in range(MHEADS)] + [("dil", h, t) for h in range(DHEADS) for t in range(TT)]
NJ = len(JOBS)
ROUNDS = []
for job in JOBS:
    if job[0] == "mla":
        ROUNDS.append([[0, 1, 2]])
    elif job[2] == 0:
        ROUNDS.append([[0, 1, 2]])
    else:
        ROUNDS.append([[0, 1, 2], [3, 4, 5]])
NR = sum(map(len, ROUNDS))
FIRST_ROUND = [sum(map(len, ROUNDS[:j])) for j in range(NJ + 1)]
NTR = NN + NR
NS = NJ + 1

BUNITS = [("ada", i, (i,)) for i in range(12)]
BUNITS += [("qa", 12, (t,)) for t in range(TT)]
BUNITS += [("ka", 13, (t,)) for t in range(2 * TT)]
BUNITS += [("qb", 14, (t,)) for t in range(TT)]
BUNITS += [("kb", 15, (t,)) for t in range(2 * TT)]
BUNITS += [("vb", 16, (t,)) for t in range(2 * TT)]
BQKV = len(BUNITS)
BUNITS += [("out2", 17 + n, (n, p)) for n in range(2) for p in range(2)]
NBU = len(BUNITS)
BTURNED = [u for u, x in enumerate(BUNITS) if x[0] in ("qa", "ka", "qb", "kb")]
BNORMED = [u for u, x in enumerate(BUNITS) if x[0] in ("qa", "ka")]
AHEADS, DIFFS = 8, 4
BJOBS = [("gqa", h, t) for h in range(AHEADS) for t in range(TT)]
BJOBS += [("diff", h, t) for h in range(DIFFS) for t in range(TT)]
NBJ = len(BJOBS)
LAMBDA_INIT = 0.8 - 0.6 * 1.0
GLU_LIMIT = 7.0
GLU_ALPHA = 1.702
PAIRS = NEXP // 2

LAYER_PARAMS = dict(norm_g=DC, b_gate=3 * DC, conv_w=12, conv_b=4, q_a=2, kv_a=1, dil_q=3, dil_k=3,
                    mla_q=MQK, mla_k=MQK)
BLOCK_PARAMS = dict(b_ada=48, g_attn=DC, g_ffn=DC, g_final=DC, subln=1, c=2 * DC, gqa_q=HALF,
                    gqa_k=HALF, lam=4 * HALF, b_router=NEXP, w_router=DC * NEXP)
CONSTS = dict(ident=P, ones=P, cosm=2 * 32, sinm=2 * 32, mask=384, dist=GROUPS * 384, iota=2 * P,
              cosx=2 * 64, sinx=2 * 64, before=P, pick=2, expert=3 * NEXP, start=3 * NEXP, job=MAXJOBS)


def places(widths):
    at, out = 0, {}
    for name, n in widths.items():
        out[name] = (at, n)
        at += n
    return out, at


LP, NLP = places(LAYER_PARAMS)
BP, NBP = places(BLOCK_PARAMS)
CP, NCP = places(CONSTS)

CHAINED = dict(layer=176, pair=2, job=2)


def slope(g, h):
    return 2.0 ** (-8.0 * (g * DHEADS + h + 1) / (GROUPS * DHEADS))


def build(nc, xT, ctxT, consts, layer_params, block_params, w_in, w_uq, w_ukv, w_out_a, w_out_b, w_out_c,
          w_o, w_ada, w_qkv, w_o2, e_in, eb_in, e_out, eb_out, out, sizes=None, debug=None):
    PER = sizes or CHAINED
    with ExitStack() as ctx:
        def sb(name, shape, dt=F32):
            return ctx.enter_context(nc.sbuf_tensor(name, shape, dt))

        def sem(name):
            return ctx.enter_context(nc.semaphore(name))

        ring = sb("ring", [P, MRING, TILE])
        cst = sb("cst", [P, NCP])
        lpar = sb("lpar", [P, LAYERS, NLP])
        par = sb("par", [P, NLP])
        x = sb("x", [P, DC, T])
        h = sb("h", [P, DC, T])
        space = sb("space", [P, 20980])
        upper = ring[:, RING:MRING, :].rearrange("p s n -> p (s n)")
        gates = upper[:, 0:3 * DC * T].rearrange("p (c t) -> p c t", t=T)
        conv = upper[:, 6144:7168].rearrange("p (c t) -> p c t", t=T)
        tanh_z = upper[:, 7168:7680]
        square = upper[:, 7680:8192]
        top = [0]

        def take(*shape):
            n = 1
            for s in shape:
                n *= s
            v = space[:, top[0]:top[0] + n]
            top[0] += n
            if len(shape) == 2:
                return v.rearrange("p (a b) -> p a b", b=shape[1])
            if len(shape) == 3:
                return v.rearrange("p (a b c) -> p a b c", b=shape[1], c=shape[2])
            return v

        ssum = take(8)
        var = take(8)
        rs = take(8)
        varx, rsx = square[:, 0:T], square[:, T:2 * T]
        stat = take(2, 8)
        mc = take(4, MQK)
        probs = take(2, 1024)
        turned = take(2, W)
        qn = turned
        rope = probs[:, 0, :].rearrange("p (a n) -> p a n", a=2)
        cT = probs[:, 1, 0:3 * T].rearrange("p (a n) -> p a n", a=3)
        phase0 = top[0]
        kpe = take(TT, MROPE)
        dqT = take(12, T)
        dkT = take(12, T)
        dv = take(TT, 3 * W)
        mqT = take(MHEADS, T)
        mkT = take(MHEADS, T)
        mv = take(TT, W)
        yB = take(4, T)
        yC = take(4, T)
        up = take(4, T + 2)
        mtmp = square
        assert top[0] <= 20980, top[0]
        top[0] = phase0
        bpar = take(NBP)
        mod = take(48, 2)
        bvarx = take(T)
        brsx = take(T)
        silu = take(DC, 32)
        bsquare = take(W)
        modrow = take(2, W)
        ctx_x = take(DC, T)
        hc = take(DC, T)
        qaT = take(4, T)
        kaT = take(2, 2 * T)
        qbT = take(4, T)
        kbT = take(4, 2 * T)
        va = take(4, P)
        vb = take(4, W)
        mix = take(DC, T)
        gs = take(2, DC)
        kdup = take(2, 2 * HALF)
        lamt = take(2, HALF)
        lam = take(8)
        assert top[0] <= 20980, top[0]
        top[0] = phase0 + NBP + 96 + 2 * T
        hTM = take(TT, D)
        bin_sb = take(2 * D)
        xs = take(DC, P)
        onehot = take(2, SLOTS)
        sel = take(TT, P)
        selg = take(2, TT, P)
        spread0 = take(2, T)
        spread1 = take(2, T)
        glu_at = top[0]
        glu = take(2, W)
        tanh_g = take(2, W)
        lin = take(2, W)
        actT = take(2, W)
        ys = take(2, W)
        bout = take(D)
        logits = take(TT, NEXP)
        best = take(TT, 8)
        fill = take(TT, 8)
        ext = take(TT, 40)
        left = take(TT, 40)
        chosen = take(TT, NEXP)
        gate = take(TT, NEXP)
        gate_half = take(TT, NEXP)
        gateT = take(T)
        pos = take(TT, 40)
        gsum = take(TT, 4)
        cnt = take(NEXP)
        cand = take(2, 96)
        cand0 = take(96)
        jt = take(MAXJOBS, 96)
        jt2 = space[:, glu_at:glu_at + MAXJOBS * 96].rearrange("p (a b) -> p a b", b=96)
        jobe = take(MAXJOBS)
        jobs_ = take(MAXJOBS)
        posb = take(TT, 1)
        jobi = take(MAXJOBS + 1).bitcast(I32)
        assert top[0] <= 20980, top[0]

        def c_(name):
            a, n = CP[name]
            return cst[:, a:a + n]

        def l_(name, i=0, n=None):
            a, m = LP[name]
            return par[:, a + i:a + i + (n or m)]

        def b_(name, i=0, n=None):
            a, m = BP[name]
            return bpar[:, a + i:a + i + (n or m)]

        ident, ones = c_("ident"), c_("ones")

        bank = [ctx.enter_context(nc.psum_tensor(f"bank{i}", [P, W], F32)) for i in range(BANKS)]
        score = ctx.enter_context(nc.psum_tensor("score", [P, 2 * W], F32))
        flip = ctx.enter_context(nc.psum_tensor("flip", [P, W], F32))
        mixed = ctx.enter_context(nc.psum_tensor("mixed", [P, W], F32))

        loaded = sem("loaded")
        par_ready = sem("par_ready")
        landed = [sem(f"landed{i}") for i in range(RING)]
        squared = sem("squared")
        hready = sem("hready")
        unit_done = sem("unit_done")
        bank_free = [sem(f"bank_free{i}") for i in range(BANKS)]
        scored = sem("scored")
        score_free = sem("score_free")
        flipped = sem("flipped")
        flip_free = sem("flip_free")
        mixed_done = sem("mixed_done")
        mixed_free = sem("mixed_free")
        squares = sem("squares")
        squares_used = sem("squares_used")
        copied = sem("copied")
        var_ready = sem("var_ready")
        rs_ready = sem("rs_ready")
        rsx_ready = sem("rsx_ready")
        qn_ready = sem("qn_ready")
        z_tanh = sem("z_tanh")
        masked = sem("masked")
        exped = sem("exped")
        probs_ready = sem("probs_ready")
        conv_ready = sem("conv_ready")
        merged = sem("merged")
        chain = sem("chain")
        stored = sem("stored")
        asked = sem("asked")
        bpar_loaded = sem("bpar_loaded")
        ctanh = sem("ctanh")
        silu_ready = sem("silu_ready")
        modrow_ready = sem("modrow_ready")
        mod_done = sem("mod_done")
        bsquared = sem("bsquared")
        bvar = sem("bvar")
        broot = sem("broot")
        bh_ready = sem("bh_ready")
        bsquares = sem("bsquares")
        bvaru = sem("bvaru")
        brootu = sem("brootu")
        bqn_ready = sem("bqn_ready")
        lam_in = sem("lam_in")
        lam_exp = sem("lam_exp")
        bmasked = sem("bmasked")
        bexped = sem("bexped")
        bprobs = sem("bprobs")
        mix_ready = sem("mix_ready")
        logits_done = sem("logits_done")
        gate_in = sem("gate_in")
        gate_exp = sem("gate_exp")
        chosen_ready = sem("chosen_ready")
        pos_done = sem("pos_done")
        gateT_done = sem("gateT_done")
        gateT_ready = sem("gateT_ready")
        table_ready = sem("table_ready")
        mlanded = [sem(f"mlanded{i}") for i in range(MRING)]
        mused = sem("mused")
        sel_ready = sem("sel_ready")
        onehot_ready = sem("onehot_ready")
        selg_ready = sem("selg_ready")
        glu_done = sem("glu_done")
        glu_free = sem("glu_free")
        glu_in = sem("glu_in")
        glu_tanh = sem("glu_tanh")
        lin_done = sem("lin_done")
        lin_free = sem("lin_free")
        act_ready = sem("act_ready")
        eout_done = sem("eout_done")
        eout_free = sem("eout_free")
        scattered = sem("scattered")
        final_ready = sem("final_ready")
        block = ctx.enter_context(nc.Block())

        def freed(l, u):
            return l * PER_BANK + u // BANKS + 2

        def done(l, u):
            return (l + 1) * NU + u + 1

        def slot_left(l, n):
            last = max(u for u, x in enumerate(UNITS) if x[1] == (n - RING) % NT)
            return l * NU + last + 1 if n < RING else done(l, last)

        def first_flip(j):
            return NN + FIRST_ROUND[j]


        def bdone(u):
            return (LAYERS + 1) * NU + u + 1

        def bfreed(u):
            return LAYERS * PER_BANK + u // BANKS + 2

        SCORE0, FLIP0, MIXED0 = LAYERS * NS, LAYERS * NTR, LAYERS * NJ
        S_JOBS, S_SUB = 2, 2 + NBJ
        S_FFN, S_FINAL = S_SUB + 1, S_SUB + 2
        F_JOBS = len(BTURNED)
        F_TOK = F_JOBS + NBJ
        F_MOE = F_TOK + 4
        M_JOBS, M_LOGITS, M_POS, M_GATE = 1, 1 + NBJ, 2 + NBJ, 3 + NBJ
        M_END = M_GATE + 1

        def score_left(s):
            s1 = s - S_JOBS
            alone = not 1 <= s1 < 2 * AHEADS
            return SCORE0 + s + (1 if alone else 0)

        def half_of(j):
            return j % 2 if BJOBS[j][0] == "gqa" else 0

        def block_sync(sp):
            for b in range(BANKS):
                sp.wait_ge(bank_free[b], LAYERS * PER_BANK + 1)
            sp.wait_ge(mixed_free, MIXED0 + 1)
            sp.dma_start(bpar, block_params).then_inc(bpar_loaded, 16)
            sp.dma_start(ctx_x, ctxT).then_inc(bpar_loaded, 16)
            sources = [(w_ada, i * W, W) for i in range(12)]
            sources += [(w_qkv, 0, W), (w_qkv, W, 256), (w_qkv, 768, W), (w_qkv, 1280, W), (w_qkv, 1792, W)]
            sources += [(w_o2, 0, W), (w_o2, W, W)]
            for n, (src, a, width) in enumerate(sources):
                if n >= RING:
                    last = max(u for u, x_ in enumerate(BUNITS) if x_[1] == n - RING)
                    sp.wait_ge(unit_done, bdone(last))
                sp.dma_start(ring[:, n % RING, :].rearrange("p (c n) -> p c n", c=DC)[:, :, 0:width],
                             columns(src, a, width)).then_inc(landed[n % RING], 16)

            def expert(e, m):
                we = e_in[bass.ds(e, 1)].rearrange("a k n -> (a k) n")
                wo = e_out[bass.ds(e, 1)].rearrange("a k n -> (a k) n")
                for j in range(MRING):
                    sp.wait_ge(mused, m * MRING + j + 1)
                    sp.sem_inc(asked, 1)
                    rows_ = slice((j % 2) * W, (j % 2 + 1) * W)
                    src = wo[rows_, :] if j >= 4 else we[rows_, (j // 2) * D:(j // 2 + 1) * D]
                    sp.dma_start(ring[:, j, :].rearrange("p (c n) -> p c n", c=4),
                                 src.rearrange("(c p) n -> p c n", p=P)).then_inc(mlanded[j], 16)

            sp.wait_ge(unit_done, bdone(NBU - 1))
            sp.wait_ge(mix_ready, 1)
            sp.dma_start(bout[0:NEXP, :], eb_out).then_inc(bpar_loaded, 16)
            sp.wait_ge(table_ready, 1)
            sp.dma_start(bin_sb[0:NEXP, :], eb_in).then_inc(bpar_loaded, 16)
            with sp.Fori(0, NEXP) as e:
                expert(e, e)
            sp.wait_ge(table_ready, 2)
            n_jobs = sp.value_load(jobi[0:1, MAXJOBS:MAXJOBS + 1], min_val=0, max_val=MAXJOBS)
            with sp.If(n_jobs > 0):
                with sp.Fori(0, n_jobs) as i:
                    e = sp.value_load(jobi[0:1, bass.ds(i, 1)], min_val=0, max_val=NEXP - 1)
                    expert(e, i + NEXP)
            sp.wait_ge(final_ready, 1)
            sp.dma_start(out, h[:]).then_inc(stored, 16)
            sp.wait_ge(stored, 16)

        def block_tensor(pe):
            for b in range(BANKS):
                pe.wait_ge(bank_free[b], LAYERS * PER_BANK + 1)
            pe.sem_inc(mused, MRING)
            pe.wait_ge(bpar_loaded, 32)
            pe.wait_ge(silu_ready, 1)

            def start(u):
                tl = BUNITS[u][1]
                pe.wait_ge(landed[tl % RING], LAYERS * 16 * NT // RING + 16 * (tl // RING + 1))
                pe.wait_ge(bank_free[u % BANKS], bfreed(u) - 1)
                return bank[u % BANKS], ring[:, tl % RING, :].rearrange("p (c n) -> p c n", c=DC)

            def pick(i):
                pe.wait_ge(bank_free[i % BANKS], bfreed(i))
                for m in range(4):
                    cc = 4 * i + m
                    ins = pe.matmul(mixed[:, 2 * cc:2 * cc + 2], modrow[:, i % 2, m * P:(m + 1) * P], c_("pick"),
                                    start=True, stop=True)
                ins.then_inc(modrow_ready, 1)

            pe.wait_ge(mixed_free, MIXED0 + 1)
            for i in range(12):
                b, w8 = start(i)
                for k in range(2):
                    for g in range(4):
                        c = 4 * k + g
                        ins = pe.matmul(b[32 * g:32 * g + 32, :], silu[:, c, :], w8[:, c, :], start=k == 0, stop=k == 1,
                                        tile_position=(0, 32 * g))
                ins.then_inc(unit_done, 1)
                if i > 0:
                    pick(i - 1)
            pick(11)

            for s, src in ((0, h[:]), (1, hc)):
                pe.wait_ge(bsquared, s + 1)
                pe.wait_ge(score_free, score_left(s))
                for c in range(DC):
                    ins = pe.matmul(score[:, 0:T], ones, src[:, c, :], start=c == 0, stop=c == DC - 1)
                ins.then_inc(scored, 1)
            pe.wait_ge(bh_ready, 2)

            def project(u):
                kind, _, who = BUNITS[u]
                b, w8 = start(u)
                t = who[0]
                n = 256 if kind == "ka" else W
                if kind in ("qa", "qb"):
                    src, tt = h, t
                else:
                    src, tt = (hc, t) if t < TT else (h, t - TT)
                for c in range(DC):
                    ins = pe.matmul(b[:, 0:n], src[:, c, tt * P:(tt + 1) * P], w8[:, c, 0:n], start=c == 0,
                                    stop=c == DC - 1)
                ins.then_inc(unit_done, 1)

            def turn(u):
                r = BTURNED.index(u)
                pe.wait_ge(bqn_ready, r + 1)
                pe.wait_ge(flip_free, FLIP0 + r + 1)
                for i in range(2 if BUNITS[u][0] == "ka" else 4):
                    ins = pe.transpose(flip[:, i * P:(i + 1) * P], qn[:, r % 2, i * P:(i + 1) * P], ident)
                ins.then_inc(flipped, 1)

            for u in range(12, BQKV + LAG):
                if u < BQKV:
                    project(u)
                if u - LAG in BTURNED:
                    turn(u - LAG)
            pe.wait_ge(flip_free, FLIP0 + F_JOBS + 1)

            def scores(j):
                kind, hd, t = BJOBS[j]
                pe.wait_ge(score_free, score_left(S_JOBS + j))
                cols = slice(t * P, (t + 1) * P)
                if kind == "gqa":
                    lo = HALF * (hd % 2)
                    o = score[:, W * half_of(j):W * half_of(j) + W]
                    ins = pe.matmul(o, qaT[lo:lo + HALF, hd // 2, cols], kaT[lo:lo + HALF, hd // 4, :],
                                    start=True, stop=True)
                else:
                    for cp in range(2):
                        lo = HALF * cp
                        ins = pe.matmul(score[:, W * cp:W * cp + W], qbT[lo:lo + HALF, hd, cols],
                                        kbT[lo:lo + HALF, hd, :], start=True, stop=True)
                ins.then_inc(scored, 1)

            def values(j):
                kind, hd, t = BJOBS[j]
                pe.wait_ge(bprobs, j + 1)
                pe.wait_ge(flip_free, FLIP0 + F_JOBS + j + 1)
                for i in range(4):
                    ins = pe.transpose(flip[:, i * P:(i + 1) * P], probs[:, j % 2, i * P:(i + 1) * P], ident)
                ins.then_inc(flipped, 1)
                pe.wait_ge(flip_free, FLIP0 + F_JOBS + j + 2)
                pe.wait_ge(mixed_free, MIXED0 + M_JOBS + j + 1)
                for i in range(4):
                    pt = turned[:, j % 2, i * P:(i + 1) * P]
                    if kind == "gqa":
                        lo = HALF * (hd % 2)
                        kv = hd // 4
                        ins = pe.matmul(mixed[lo:lo + HALF, 0:P], va[:, i, kv * HALF:(kv + 1) * HALF], pt,
                                        start=i == 0, stop=i == 3)
                    else:
                        ins = pe.matmul(mixed[:, 0:P], vb[:, i, hd * P:(hd + 1) * P], pt, start=i == 0, stop=i == 3)
                ins.then_inc(mixed_done, 1)

            for b in range(BANKS):
                pe.wait_ge(bank_free[(BQKV - 1 - b) % BANKS], bfreed(BQKV - 1 - b))
            for j in range(NBJ + 1):
                if j < NBJ:
                    scores(j)
                if j > 0:
                    values(j - 1)
            pe.wait_ge(bsquared, 3)
            pe.wait_ge(score_free, score_left(S_SUB))
            for i in range(2):
                ins = pe.matmul(score[:, i * W:(i + 1) * W], ones, hc[:, 2 * i:2 * i + 2, :].rearrange("p a t -> p (a t)"),
                                start=True, stop=True)
            ins.then_inc(scored, 1)
            pe.wait_ge(mix_ready, 1)
            for u in range(BQKV, NBU):
                b, w8 = start(u)
                for i in range(2):
                    m = (2 * BUNITS[u][2][1] + i) * P
                    for c in range(DC):
                        ins = pe.matmul(b[:, i * T:(i + 1) * T], w8[:, c, m:m + P], mix[:, c, :], start=c == 0,
                                        stop=c == DC - 1)
                ins.then_inc(unit_done, 1)

            pe.wait_ge(bsquared, 4)
            pe.wait_ge(score_free, score_left(S_FFN))
            for c in range(DC):
                ins = pe.matmul(score[:, 0:T], ones, h[:, c, :], start=c == 0, stop=c == DC - 1)
            ins.then_inc(scored, 1)
            pe.wait_ge(bh_ready, 3)
            pe.wait_ge(mixed_free, MIXED0 + M_LOGITS + 1)
            wr = b_("w_router").rearrange("p (c e) -> p c e", c=DC)
            for t in range(TT):
                for c in range(DC):
                    ins = pe.matmul(mixed[:, t * NEXP:(t + 1) * NEXP], h[:, c, t * P:(t + 1) * P], wr[:, c, :],
                                    start=c == 0, stop=c == DC - 1)
            ins.then_inc(mixed_done, 1)
            for r in range(4):
                t, q = r // 2, r % 2
                pe.wait_ge(flip_free, FLIP0 + F_TOK + r + 1)
                for i in range(4):
                    ins = pe.transpose(flip[:, i * P:(i + 1) * P], h[:, 4 * q + i, t * P:(t + 1) * P], ident)
                ins.then_inc(flipped, 1)
            pe.wait_ge(chosen_ready, 1)
            pe.wait_ge(mixed_free, MIXED0 + M_POS + 1)
            pe.matmul(mixed[:, 0:32], c_("before"), chosen[:, 0, :], start=True, stop=True)
            pe.matmul(mixed[:, 32:64], c_("before"), chosen[:, 1, :], start=True, stop=False)
            pe.matmul(mixed[:, 32:64], ones, chosen[:, 0, :], start=False, stop=True)
            pe.matmul(mixed[:, 64:96], ones, chosen[:, 0, :], start=True, stop=False)
            pe.matmul(mixed[:, 64:96], ones, chosen[:, 1, :], start=False, stop=True).then_inc(mixed_done, 1)
            pe.wait_ge(gate_in, 2)
            pe.wait_ge(mixed_free, MIXED0 + M_GATE + 1)
            for t in range(TT):
                ins = pe.matmul(mixed[0:NEXP, t * P:(t + 1) * P], gate[:, t, :], ident, start=True, stop=True)
            ins.then_inc(mixed_done, 1)
            pe.wait_ge(mixed_free, MIXED0 + M_END + 1)
            pe.wait_ge(bpar_loaded, 64)
            for b in range(BANKS):
                pe.wait_ge(bank_free[b], bfreed(NBU - BANKS + b))
            for c in range(DC):
                pe.matmul(bank[c // 2][:, (c % 2) * T:(c % 2 + 1) * T], bout[0:NEXP, c * P:(c + 1) * P],
                          gateT[0:NEXP, :], start=c % 2 == 0, stop=False, skip_group_check=True)

            def gather(first_sel, first_flip_):
                pe.wait_ge(sel_ready, first_sel)
                for q in range(2):
                    pe.wait_ge(flip_free, first_flip_ + q)
                    for i in range(4):
                        c = 4 * q + i
                        for t in range(TT):
                            ins = pe.matmul(flip[:, i * P:(i + 1) * P], hTM[:, t, c * P:(c + 1) * P], sel[:, t, :],
                                            start=t == 0, stop=t == TT - 1)
                    ins.then_inc(flipped, 1)

            def expert_in(m, which, hh):
                pe.wait_ge((glu_free, lin_free)[which], m + 1)
                for k in range(DC):
                    j = 2 * which + k // 4
                    if k % 4 == 0:
                        pe.wait_ge(mlanded[j], m * 16 + 16)
                    wk = ring[:, j, (k % 4) * D:(k % 4 + 1) * D]
                    for blk in range(2):
                        ins = pe.matmul(score[HALF * blk:HALF * blk + HALF, which * W:(which + 1) * W],
                                        xs[:, k, HALF * hh:HALF * hh + HALF], wk[:, blk * W:(blk + 1) * W],
                                        start=k == 0, stop=False)
                    if k % 4 == 3:
                        ins.then_inc(mused, 1)
                for blk in range(2):
                    ins = pe.matmul(score[HALF * blk:HALF * blk + HALF, which * W:(which + 1) * W],
                                    onehot[:, hh, :], bin_sb[:, which * D + blk * W:which * D + (blk + 1) * W],
                                    start=False, stop=True)
                ins.then_inc((glu_done, lin_done)[which], 1)

            def expert_out(m, hh):
                pe.wait_ge(eout_free, m + 1)
                for k in range(DC):
                    j = 4 + k // 4
                    if k % 4 == 0:
                        pe.wait_ge(mlanded[j], m * 16 + 16)
                    wk = ring[:, j, (k % 4) * D:(k % 4 + 1) * D]
                    a0 = (k % 4) * P + HALF * (k // 4)
                    for blk in range(2):
                        ins = pe.matmul(mixed[HALF * blk:HALF * blk + HALF, :], actT[:, hh, a0:a0 + HALF],
                                        wk[:, blk * W:(blk + 1) * W], start=k == 0, stop=k == DC - 1)
                    if k == 3:
                        ins.then_inc(mused, 1)
                ins.then_inc(eout_done, 1)

            def turn_act(m, hh, f):
                pe.wait_ge(act_ready, m + 1)
                pe.wait_ge(flip_free, f)
                for i in range(4):
                    ins = pe.transpose(flip[:, i * P:(i + 1) * P], lin[:, hh, i * P:(i + 1) * P], ident)
                ins.then_inc(flipped, 1)
                pe.wait_ge(flip_free, f + 1)

            def turn_sel(hh, f):
                pe.wait_ge(flip_free, f)
                for t in range(TT):
                    ins = pe.transpose(flip[:, t * P:(t + 1) * P], selg[:, hh, t, :], ident)
                ins.then_inc(flipped, 1)

            def scatter(hh):
                for c in range(DC):
                    sp_ = (spread0, spread1)[c // 4]
                    ins = pe.matmul(bank[c // 2][:, (c % 2) * T:(c % 2 + 1) * T],
                                    ys[:, hh, (c % 4) * P:(c % 4 + 1) * P], sp_[:, hh, :], start=False, stop=False,
                                    skip_group_check=True)
                return ins

            pe.wait_ge(eout_free, 1)
            gather(1, FLIP0 + F_MOE + 1)
            pe.wait_ge(flip_free, FLIP0 + F_MOE + 3)
            base_f = FLIP0 + F_MOE + 2
            with pe.Fori(0, PAIRS) as i:
                pe.wait_ge(onehot_ready, i + 1)
                expert_in(i * 2, 0, 0)
                expert_in(i * 2, 1, 0)
                pe.wait_ge(eout_free, i * 2 + 1)
                scatter(1)
                pe.wait_ge(selg_ready, i + 1)
                turn_sel(0, i * 6 + base_f + 1)
                turn_sel(1, i * 6 + base_f + 2)
                turn_act(i * 2, 0, i * 6 + base_f + 3)
                expert_out(i * 2, 0)
                pe.wait_ge(eout_done, i * 2 + 1)
                pe.sem_inc(mused, 1)
                expert_in(i * 2 + 1, 0, 1)
                expert_in(i * 2 + 1, 1, 1)
                gather(i + 2, i * 6 + base_f + 4)
                pe.wait_ge(eout_free, i * 2 + 2)
                scatter(0)
                turn_act(i * 2 + 1, 1, i * 6 + base_f + 6)
                expert_out(i * 2 + 1, 1)
                pe.wait_ge(eout_done, i * 2 + 2)
                pe.sem_inc(mused, 1)
            pe.wait_ge(eout_free, NEXP + 1)
            scatter(1).then_inc(scattered, 1)
            base_f2 = base_f + 6 * PAIRS
            n_jobs = pe.value_load(jobi[0:1, MAXJOBS:MAXJOBS + 1], min_val=0, max_val=MAXJOBS)
            with pe.If(n_jobs > 0):
                with pe.Fori(0, n_jobs) as i:
                    pe.wait_ge(selg_ready, i + PAIRS + 1)
                    gather(i + PAIRS + 2, i * 4 + base_f2 + 1)
                    turn_sel(0, i * 4 + base_f2 + 3)
                    pe.wait_ge(flip_free, i * 4 + base_f2 + 4)
                    pe.wait_ge(onehot_ready, i + PAIRS + 1)
                    expert_in(i + NEXP, 0, 0)
                    expert_in(i + NEXP, 1, 0)
                    turn_act(i + NEXP, 0, i * 4 + base_f2 + 4)
                    expert_out(i + NEXP, 0)
                    pe.wait_ge(eout_free, i + NEXP + 2)
                    pe.sem_inc(mused, 1)
                    scatter(0).then_inc(scattered, 1)
            pe.wait_ge(bsquared, 5)
            for c in range(DC):
                ins = pe.matmul(score[:, 0:T], ones, h[:, c, :], start=c == 0, stop=c == DC - 1)
            ins.then_inc(scored, 1)

        def block_scalar(act):
            act.wait_ge(bpar_loaded, 32)
            act.activation(modrow[:, 0, 0:16], b_("c"), ACT.Tanh, scale=0.5).then_inc(ctanh, 1)
            act.wait_ge(lam_in, 1)
            act.activation(lam[:, 2:4], lam[:, 0:2], ACT.Exp).then_inc(lam_exp, 1)
            for i in range(12):
                act.wait_ge(unit_done, bdone(i))
                if i >= 2:
                    act.wait_ge(modrow_ready, i - 1)
                else:
                    act.wait_ge(silu_ready, 1)
                act.activation(modrow[:, i % 2, :], bank[i % BANKS][:, :], ACT.Copy).then_inc(bank_free[i % BANKS], 1)

            act.activation(h[:], x[:], ACT.Square).then_inc(bsquared, 1)
            act.activation(hc, ctx_x, ACT.Square).then_inc(bsquared, 1)

            def stream_root(n, s):
                act.wait_ge(bvar, n)
                act.activation(brsx, bvarx, ACT.Sqrt).then_inc(broot, 1)

            stream_root(1, 0)
            stream_root(2, 1)
            for u in range(12, BQKV + LAG):
                if u < BQKV:
                    kind, _, who = BUNITS[u]
                    b = bank[u % BANKS]
                    if kind in ("qa", "ka"):
                        n = BNORMED.index(u)
                        act.wait_ge(unit_done, bdone(u))
                        if n:
                            act.wait_ge(bvaru, n)
                        w = W if kind == "qa" else P
                        act.activation(bsquare[:, 0:w], b[:, 0:w], ACT.Square).then_inc(bsquares, 1)
                        act.wait_ge(bvaru, n + 1)
                        act.activation(rs, var, ACT.Sqrt).then_inc(brootu, 1)
                    elif kind == "vb":
                        act.wait_ge(unit_done, bdone(u))
                        act.activation(vb[:, who[0], :], b[:, :], ACT.Copy).then_inc(bank_free[u % BANKS], 1)
                if u - LAG in BTURNED:
                    r = BTURNED.index(u - LAG)
                    kind, _, who = BUNITS[u - LAG]
                    t = who[0]
                    act.wait_ge(flipped, FLIP0 + r + 1)
                    v = flip[:, :].rearrange("p (a t) -> p a t", t=P)
                    n = 2 if kind == "ka" else 4
                    dst = dict(qa=qaT, ka=kaT, qb=qbT, kb=kbT)[kind][:, 0:n, t * P:(t + 1) * P]
                    act.activation(dst, v[:, 0:n, :], ACT.Copy,
                                   scale=HALF ** -0.5 if kind in ("qa", "qb") else 1.0).then_inc(flip_free, 1)
            for j in range(NBJ + 1):
                if j < NBJ:
                    kind = BJOBS[j][0]
                    act.wait_ge(bmasked, j + 1)
                    if j >= 2:
                        act.wait_ge(flipped, FLIP0 + F_JOBS + j - 1)
                    st = stat[:, j % 2, :]
                    a = W * half_of(j)
                    ins = act.activation(probs[:, j % 2, 0:W], score[:, a:a + W], ACT.Exp, bias=st[:, 2:3],
                                         accum_out=st[:, 4:5])
                    if kind == "diff":
                        ins = act.activation(probs[:, j % 2, W:2 * W], score[:, W:2 * W], ACT.Exp, bias=st[:, 3:4],
                                             accum_out=st[:, 5:6])
                    ins.then_inc(score_free, 1)
                if j > 0:
                    act.wait_ge(flipped, FLIP0 + F_JOBS + j)
                    if j >= 3:
                        act.wait_ge(mixed_done, MIXED0 + j - 2)
                    act.activation(turned[:, (j - 1) % 2, :], flip[:, :], ACT.Copy).then_inc(flip_free, 1)
            act.wait_ge(mixed_free, MIXED0 + M_JOBS + NBJ + 1)
            act.activation(hc[:, 0:4, :], mix[:, 4:8, :], ACT.Square).then_inc(bsquared, 1)
            act.wait_ge(bvar, 3)
            act.activation(hc[:, 0:4, :], hc[:, 4:8, :], ACT.Sqrt).then_inc(broot, 1)
            act.wait_ge(bank_free[(NBU - 1) % BANKS], bfreed(NBU - 1))
            act.activation(h[:], x[:], ACT.Square).then_inc(bsquared, 1)
            stream_root(4, S_FFN)
            for r in range(4):
                t, q = r // 2, r % 2
                act.wait_ge(flipped, FLIP0 + F_TOK + r + 1)
                act.activation(hTM[:, t, q * W:(q + 1) * W], flip[:, :], ACT.Copy).then_inc(flip_free, 1)
            act.wait_ge(gate_in, 1)
            for t in range(TT):
                ins = act.activation(gate[:, t, :], ext[:, t, 0:NEXP], ACT.Exp, bias=gsum[:, t, 0:1])
            ins.then_inc(gate_exp, 1)

            def gathered(f):
                for q in range(2):
                    act.wait_ge(flipped, f + q)
                    act.activation(xs[:, 4 * q:4 * q + 4, :], flip[:, :].rearrange("p (a t) -> p a t", t=P),
                                   ACT.Copy).then_inc(flip_free, 1)

            def sel_turned(hh, f):
                act.wait_ge(flipped, f)
                act.activation(spread0[0:HALF, hh, :], flip[0:HALF, 0:T], ACT.Copy)
                act.activation(spread1[HALF:P, hh, :], flip[HALF:P, 0:T], ACT.Copy).then_inc(flip_free, 1)

            def tanh(m, hh):
                act.wait_ge(glu_free, m + 2)
                act.activation(tanh_g[:, hh, :], glu[:, hh, :], ACT.Tanh, scale=GLU_ALPHA / 2).then_inc(glu_tanh, 1)

            def act_turned(hh, f):
                act.wait_ge(flipped, f)
                act.activation(actT[:, hh, :], flip[:, :], ACT.Copy).then_inc(flip_free, 1)

            base_f = FLIP0 + F_MOE + 2
            gathered(FLIP0 + F_MOE + 1)
            with act.Fori(0, PAIRS) as i:
                tanh(i * 2, 0)
                sel_turned(0, i * 6 + base_f + 1)
                sel_turned(1, i * 6 + base_f + 2)
                act_turned(0, i * 6 + base_f + 3)
                tanh(i * 2 + 1, 1)
                gathered(i * 6 + base_f + 4)
                act_turned(1, i * 6 + base_f + 6)
            base_f2 = base_f + 6 * PAIRS
            n_jobs = act.value_load(jobi[0:1, MAXJOBS:MAXJOBS + 1], min_val=0, max_val=MAXJOBS)
            with act.If(n_jobs > 0):
                with act.Fori(0, n_jobs) as i:
                    gathered(i * 4 + base_f2 + 1)
                    sel_turned(0, i * 4 + base_f2 + 3)
                    tanh(i + NEXP, 0)
                    act_turned(0, i * 4 + base_f2 + 4)
            act.wait_ge(bh_ready, 4)
            act.activation(h[:], x[:], ACT.Square).then_inc(bsquared, 1)
            stream_root(5, S_FINAL)

        def block_vector(dve, link, steps, base):
            def to(shape, v, axis=1):
                return v.unsqueeze(axis).broadcast_to(shape)

            dve.wait_ge(bpar_loaded, 32)
            link(dve.memset(silu, 0.0))
            lv = b_("lam").rearrange("p (a n) -> p a n", a=4)
            for k in range(2):
                link(dve.tensor_tensor(lamt[:, k, :], lv[:, 2 * k, :], lv[:, 2 * k + 1, :], ALU.mult))
            dve.tensor_reduce(lam[:, 0:2], lamt, AX.X, ALU.add).then_inc(lam_in, 1)
            dve.wait_ge(ctanh, 1)
            cv = b_("c").rearrange("p (c two) -> p c two", two=2)
            tv = modrow[:, 0, 0:16].rearrange("p (c two) -> p c two", two=2)
            link(dve.scalar_tensor_tensor(out=silu[:, :, 0:2], in0=tv, scalar=1.0, in1=cv, op0=ALU.add,
                                          op1=ALU.mult))
            dve.tensor_scalar(silu[:, :, 0:2], silu[:, :, 0:2], 0.5, None, ALU.mult).then_inc(silu_ready, 1)
            dve.wait_ge(lam_exp, 1)
            link(dve.tensor_tensor(lam[:, 4:5], lam[:, 3:4], lam[:, 2:3], ALU.subtract))
            link(dve.tensor_scalar(lam[:, 4:5], lam[:, 4:5], -LAMBDA_INIT, None, ALU.add))
            link(dve.tensor_scalar(b_("subln"), b_("subln"), 1.0 - LAMBDA_INIT, None, ALU.mult))
            dve.wait_ge(modrow_ready, 12)
            dve.tensor_tensor(mod, mixed[:, 0:96].rearrange("p (c two) -> p c two", two=2),
                              to([P, 48, 2], b_("b_ada"), 2), ALU.add).then_inc(mixed_free, 1)
            dve.wait_ge(mixed_free, MIXED0 + 2)
            SH1, SC1, GT1, SH2, SC2, GT2 = (DC * i for i in range(6))

            def modulated(dst, src, n, gains, shift, scale_at, which, s):
                link(dve.scalar_tensor_tensor(out=gs[:, 0, :], in0=mod[:, scale_at:scale_at + DC, which], scalar=1.0,
                                              in1=gains, op0=ALU.add, op1=ALU.mult))
                dve.wait_ge(scored, SCORE0 + s + 1)
                dve.tensor_scalar(bvarx, score[:, 0:T], 1.0 / D, EPS, ALU.mult, ALU.add).then_inc(score_free, 1)
                dve.wait_ge(score_free, SCORE0 + s + 2)
                dve.sem_inc(bvar, 1)
                dve.wait_ge(broot, n)
                link(dve.reciprocal(brsx, brsx))
                for c in range(DC):
                    ins = dve.scalar_tensor_tensor(out=dst[:, c, :], in0=src[:, c, :], scalar=gs[:, 0, c:c + 1],
                                                   in1=brsx, op0=ALU.mult, op1=ALU.mult)
                link(ins)
                for c in range(DC):
                    ins = dve.tensor_scalar(dst[:, c, :], dst[:, c, :],
                                            mod[:, shift + c:shift + c + 1, which:which + 1].rearrange("p a b -> p (a b)"),
                                            None, ALU.add)
                return ins

            modulated(h, x, 1, b_("g_attn"), SH1, SC1, 0, 0).then_inc(bh_ready, 1)
            modulated(hc, ctx_x, 2, b_("g_attn"), SH1, SC1, 1, 1).then_inc(bh_ready, 1)

            def rotate(v, t):
                a = v.shape[1] // 2
                for ax in range(2):
                    def tab(name, hf):
                        at = t * 64 + ax * 32 + hf * 16
                        return c_(name)[:, at:at + 16].unsqueeze(1).broadcast_to([P, a, 16])
                    for hf in range(2):
                        s_ = v[:, ax::2, hf, :]
                        o_ = v[:, ax::2, 1 - hf, :]
                        r0 = rope[:, 0, :].rearrange("p (b n) -> p b n", n=16)[:, (2 * ax + hf) * 8:(2 * ax + hf) * 8 + a, :]
                        r1 = rope[:, 1, :].rearrange("p (b n) -> p b n", n=16)[:, (2 * ax + hf) * 8:(2 * ax + hf) * 8 + a, :]
                        dve.tensor_tensor(r0, s_, tab("cosx", hf), ALU.mult)
                        link(dve.tensor_tensor(r1, o_, tab("sinx", hf), ALU.mult))
                for ax in range(2):
                    for hf in range(2):
                        r0 = rope[:, 0, :].rearrange("p (b n) -> p b n", n=16)[:, (2 * ax + hf) * 8:(2 * ax + hf) * 8 + a, :]
                        r1 = rope[:, 1, :].rearrange("p (b n) -> p b n", n=16)[:, (2 * ax + hf) * 8:(2 * ax + hf) * 8 + a, :]
                        ins = dve.tensor_tensor(v[:, ax::2, hf, :], r0, r1, ALU.add)
                link(ins)

            for u in range(12, BQKV):
                kind, _, who = BUNITS[u]
                b = bank[u % BANKS]
                t = who[0]
                if kind == "vb":
                    continue
                r = BTURNED.index(u)
                q = qn[:, r % 2, :]
                xt = t if kind in ("qa", "qb") else t - TT
                if r >= 2:
                    dve.wait_ge(flipped, FLIP0 + r - 1)
                if kind in ("qa", "ka"):
                    n = BNORMED.index(u)
                    a = 8 if kind == "qa" else 2
                    dve.wait_ge(bsquares, n + 1)
                    link(dve.tensor_reduce(ssum[:, 0:a], bsquare[:, 0:a * HALF].rearrange("p (a b) -> p a b", b=HALF), AX.X,
                                           ALU.add))
                    dve.tensor_scalar(var[:, 0:a], ssum[:, 0:a], 1.0 / HALF, EPS, ALU.mult, ALU.add).then_inc(bvaru, 1)
                    dve.wait_ge(brootu, n + 1)
                    link(dve.reciprocal(rs, rs))
                    dst = q if kind == "qa" else kdup.rearrange("p a b -> p (a b)")[:, 0:P]
                    dv_ = dst.rearrange("p (a b) -> p a b", b=HALF)
                    if kind == "ka":
                        link(dve.tensor_copy(va[:, t, :], b[:, P:2 * P]))
                    dve.tensor_tensor(dv_, b[:, 0:a * HALF].rearrange("p (a b) -> p a b", b=HALF),
                                      to([P, a, HALF], rs[:, 0:a], 2), ALU.mult).then_inc(bank_free[u % BANKS], 1)
                    dve.wait_ge(bank_free[u % BANKS], bfreed(u))
                    g = b_("gqa_q" if kind == "qa" else "gqa_k")
                    link(dve.tensor_tensor(dv_, dv_, to([P, a, HALF], g), ALU.mult))
                else:
                    dst = q
                    dve.wait_ge(unit_done, bdone(u))
                    dve.tensor_copy(q, b[:, :]).then_inc(bank_free[u % BANKS], 1)
                    dve.wait_ge(bank_free[u % BANKS], bfreed(u))
                if xt >= 0:
                    rotate(dst.rearrange("p (a two n) -> p a two n", two=2, n=16), xt)
                if kind == "ka":
                    kd = kdup.rearrange("p a b -> p (a b)")[:, 0:P].rearrange("p (a b) -> p a b", b=HALF)
                    for cp in range(2):
                        ins = dve.tensor_copy(q[:, 0:256].rearrange("p (a two b) -> p a two b", two=2, b=HALF)[:, :, cp, :],
                                              kd)
                    link(ins)
                dve.sem_inc(bqn_ready, 1)

            for j in range(NBJ + 1):
                if j < NBJ:
                    kind, hd, t = BJOBS[j]
                    st = stat[:, j % 2, :]
                    dve.wait_ge(scored, SCORE0 + S_JOBS + j + 1)
                    a = W * half_of(j)
                    if kind == "gqa":
                        link(dve.tensor_reduce(st[:, 0:1], score[:, a:a + W], AX.X, ALU.max))
                        dve.tensor_scalar(st[:, 2:3], st[:, 0:1], -1.0, None, ALU.mult).then_inc(bmasked, 1)
                    else:
                        link(dve.tensor_reduce(st[:, 0:2], score[:, :].rearrange("p (a n) -> p a n", a=2), AX.X, ALU.max))
                        dve.tensor_scalar(st[:, 2:4], st[:, 0:2], -1.0, None, ALU.mult).then_inc(bmasked, 1)
                if j > 0:
                    kind, hd, t = BJOBS[j - 1]
                    lo = HALF * (hd % 2)
                    dve.wait_ge(mixed_done, MIXED0 + j)
                    cols = slice(t * P, (t + 1) * P)
                    if kind == "gqa":
                        dve.tensor_copy(mix[lo:lo + HALF, hd // 2, cols], mixed[lo:lo + HALF, 0:P]).then_inc(mixed_free, 1)
                    else:
                        dve.tensor_copy(mix[:, 4 + hd, cols], mixed[:, 0:P]).then_inc(mixed_free, 1)
                if j < NBJ:
                    kind, hd, t = BJOBS[j]
                    pr, st = probs[:, j % 2, :], stat[:, j % 2, :]
                    dve.wait_ge(score_free, SCORE0 + S_JOBS + j + 2)
                    if kind == "gqa":
                        link(dve.reciprocal(st[:, 6:7], st[:, 4:5]))
                        dve.tensor_scalar(pr[:, 0:W], pr[:, 0:W], st[:, 6:7], None, ALU.mult).then_inc(bprobs, 1)
                    else:
                        link(dve.reciprocal(st[:, 6:8], st[:, 4:6]))
                        link(dve.tensor_tensor(st[:, 7:8], st[:, 7:8], lam[:, 4:5], ALU.mult))
                        link(dve.tensor_scalar(pr[:, 0:W], pr[:, 0:W], st[:, 6:7], None, ALU.mult))
                        dve.scalar_tensor_tensor(out=pr[:, 0:W], in0=pr[:, W:2 * W], scalar=st[:, 7:8], in1=pr[:, 0:W],
                                                 op0=ALU.mult, op1=ALU.add).then_inc(bprobs, 1)
            dve.wait_ge(scored, SCORE0 + S_SUB + 1)
            dve.tensor_scalar(hc[:, 4:8, :].rearrange("p a t -> p (a t)"), score[:, :], 1.0 / P, EPS, ALU.mult,
                              ALU.add).then_inc(score_free, 1)
            dve.wait_ge(score_free, SCORE0 + S_SUB + 2)
            dve.sem_inc(bvar, 1)
            dve.wait_ge(broot, 3)
            link(dve.reciprocal(hc[:, 0:4, :], hc[:, 0:4, :]))
            m4 = mix[:, 4:8, :].rearrange("p a t -> p (a t)")
            dve.scalar_tensor_tensor(out=m4, in0=m4, scalar=b_("subln"), in1=hc[:, 0:4, :].rearrange("p a t -> p (a t)"),
                                     op0=ALU.mult, op1=ALU.mult).then_inc(mix_ready, 1)
            for u in range(BQKV, NBU):
                n, p = BUNITS[u][2]
                dve.wait_ge(unit_done, bdone(u))
                for i in range(2):
                    c = 4 * n + 2 * p + i
                    ins = dve.scalar_tensor_tensor(out=x[:, c, :], in0=bank[u % BANKS][:, i * T:(i + 1) * T],
                                                   scalar=mod[:, GT1 + c, 0:1], in1=x[:, c, :], op0=ALU.mult,
                                                   op1=ALU.add)
                ins.then_inc(bank_free[u % BANKS], 1)
            if debug == "attention":
                return

            dve.wait_ge(unit_done, bdone(NBU - 1))
            for v in (bin_sb, pos, ext, ys, spread0, spread1, sel):
                ins = dve.memset(v, -1.0 if v is pos else -2.0 ** 126 if v is ext else 0.0)
            link(ins)
            dve.sem_inc(table_ready, 1)
            modulated(h, x, 4, b_("g_ffn"), SH2, SC2, 0, S_FFN).then_inc(bh_ready, 1)
            dve.wait_ge(mixed_done, MIXED0 + NBJ + 1)
            dve.tensor_tensor(ext[:, :, 0:NEXP], mixed[:, 0:2 * NEXP].rearrange("p (a e) -> p a e", a=2),
                              to([P, TT, NEXP], b_("b_router")), ALU.add).then_inc(mixed_free, 1)
            dve.wait_ge(mixed_free, MIXED0 + M_LOGITS + 2)
            for t in range(TT):
                link(dve.max(best[:, t, :], ext[:, t, 0:NEXP]))
            link(dve.memset(fill, -2.0 ** 126))
            link(dve.tensor_copy(fill[:, :, 0:TOPK], best[:, :, 0:TOPK]))
            for t in range(TT):
                link(dve.match_replace(left[:, t, :], fill[:, t, :], ext[:, t, :], -2.0 ** 127))
            dve.tensor_scalar(chosen, left[:, :, 0:NEXP], -1.5 * 2.0 ** 126, None, ALU.is_lt).then_inc(chosen_ready, 1)
            dve.wait_ge(chosen_ready, 1)
            dve.tensor_scalar(gsum[:, :, 0:1], best[:, :, 0:1], -1.0, None, ALU.mult).then_inc(gate_in, 1)
            dve.wait_ge(gate_exp, 1)
            link(dve.tensor_tensor(gate, gate, chosen, ALU.mult))
            link(dve.tensor_reduce(gsum[:, :, 1], gate, AX.X, ALU.add))
            link(dve.reciprocal(gsum[:, :, 2], gsum[:, :, 1]))
            link(dve.tensor_tensor(gate, gate, to([P, TT, NEXP], gsum[:, :, 2], 2), ALU.mult))
            dve.tensor_scalar(gate_half, gate, 0.5, None, ALU.mult).then_inc(gate_in, 1)
            dve.wait_ge(mixed_done, MIXED0 + NBJ + 2)
            link(dve.tensor_copy(cnt, mixed[:, 64:96]))
            pv = pos[:, :, 0:NEXP]
            dve.scalar_tensor_tensor(out=pv, in0=mixed[:, 0:64].rearrange("p (a e) -> p a e", a=2), scalar=1.0,
                                     in1=chosen, op0=ALU.add, op1=ALU.mult).then_inc(mixed_free, 1)
            dve.wait_ge(mixed_free, MIXED0 + M_POS + 2)
            link(dve.tensor_scalar(pv, pv, -1.0, None, ALU.add))
            dve.wait_ge(mixed_done, MIXED0 + NBJ + 3)
            dve.tensor_copy(gateT[0:NEXP, :], mixed[0:NEXP, 0:T]).then_inc(mixed_free, 1)
            dve.wait_ge(gate_in, 2)

            def column(v, t, e):
                return v[:, t, bass.ds(e, 1)]

            iota = c_("iota")

            def select(hh, e):
                for t in range(TT):
                    ins = dve.tensor_scalar(sel[:, t, HALF * hh:HALF * hh + HALF], iota[:, 0:HALF], column(pos, t, e),
                                            None, ALU.is_equal)
                return ins

            select(0, 0)
            select(1, 1).then_inc(sel_ready, 1)
            for b in range(3):
                ins = dve.tensor_scalar(cand0[:, b * NEXP:(b + 1) * NEXP], cnt, SLOTS * (b + 1) + 0.5, None, ALU.is_gt)
            link(ins)
            src, s = cand0, 1
            k = 0
            while s < 96:
                dst = cand[:, k % 2, :]
                dve.tensor_copy(dst[:, 0:s], src[:, 0:s])
                link(dve.tensor_tensor(dst[:, s:96], src[:, s:96], src[:, 0:96 - s], ALU.add))
                src, s, k = dst, 2 * s, k + 1
            link(dve.tensor_copy(jobi[:, MAXJOBS:MAXJOBS + 1], src[:, 95:96]))
            link(dve.tensor_tensor(cand0, cand0, src, ALU.mult))
            jshape = [P, MAXJOBS, 96]
            link(dve.tensor_tensor(jt, to(jshape, cand0), to(jshape, c_("job"), 2), ALU.is_equal))
            for name, dst in (("expert", jobe), ("start", jobs_)):
                link(dve.tensor_tensor(jt2, jt, to(jshape, c_(name)), ALU.mult))
                link(dve.tensor_reduce(dst, jt2, AX.X, ALU.add))
            link(dve.tensor_copy(jobi[:, 0:MAXJOBS], jobe))
            for s_ in (glu_free, lin_free, eout_free, table_ready):
                dve.sem_inc(s_, 1)
            mark = steps[0]
            dve.wait_ge(bpar_loaded, 64)

            def onehots(hh, e):
                return dve.tensor_copy(onehot[:, hh, :], ident[:, bass.ds(e, 1)].broadcast_to([P, SLOTS]))

            def gates_of(hh, e, where):
                for t in range(TT):
                    ins = dve.tensor_scalar(selg[:, hh, t, :], iota[:, 0:P], where(t), column(gate_half, t, e),
                                            ALU.is_equal, ALU.mult)
                return ins

            def activate(m, hh):
                dve.wait_ge(glu_done, m + 1)
                dve.tensor_scalar(glu[:, hh, :], score[:, 0:W], GLU_LIMIT, None, ALU.min).then_inc(glu_free, 1)
                dve.wait_ge(glu_tanh, m + 1)
                link(dve.scalar_tensor_tensor(out=glu[:, hh, :], in0=tanh_g[:, hh, :], scalar=1.0, in1=glu[:, hh, :],
                                              op0=ALU.add, op1=ALU.mult))
                dve.wait_ge(lin_done, m + 1)
                dve.tensor_scalar(lin[:, hh, :], score[:, W:2 * W], GLU_LIMIT, -GLU_LIMIT, ALU.min,
                                  ALU.max).then_inc(lin_free, 1)
                dve.wait_ge(lin_free, m + 2)
                dve.scalar_tensor_tensor(out=lin[:, hh, :], in0=lin[:, hh, :], scalar=1.0, in1=glu[:, hh, :],
                                         op0=ALU.add, op1=ALU.mult).then_inc(act_ready, 1)

            def expert_rows(m, hh):
                dve.wait_ge(eout_done, m + 1)
                dve.tensor_copy(ys[:, hh, :], mixed[:, :]).then_inc(eout_free, 1)

            with dve.Fori(0, PAIRS) as i:
                base[0] = i * PER["pair"] + mark
                steps[0] = 0
                onehots(0, i * 2)
                onehots(1, i * 2 + 1).then_inc(onehot_ready, 1)
                gates_of(0, i * 2, lambda t: column(pos, t, i * 2))
                gates_of(1, i * 2 + 1, lambda t: column(pos, t, i * 2 + 1)).then_inc(selg_ready, 1)
                activate(i * 2, 0)
                select(0, i * 2 + 2)
                select(1, i * 2 + 3).then_inc(sel_ready, 1)
                expert_rows(i * 2, 0)
                activate(i * 2 + 1, 1)
                expert_rows(i * 2 + 1, 1)
                assert steps[0] == PER["pair"], steps[0]
            mark2 = mark + PAIRS * PER["pair"]
            n_jobs = dve.value_load(jobi[0:1, MAXJOBS:MAXJOBS + 1], min_val=0, max_val=MAXJOBS)
            with dve.If(n_jobs > 0):
                with dve.Fori(0, n_jobs) as i:
                    base[0] = i * PER["job"] + mark2
                    steps[0] = 0
                    e = dve.value_load(jobi[0:1, bass.ds(i, 1)], min_val=0, max_val=NEXP - 1)
                    dve.wait_ge(scattered, i + 1)
                    for t in range(TT):
                        ins = dve.tensor_tensor(posb[:, t, :], column(pos, t, e), jobs_[:, bass.ds(i, 1)], ALU.subtract)
                    link(ins)
                    onehots(0, e).then_inc(onehot_ready, 1)
                    gates_of(0, e, lambda t: posb[:, t, 0:1]).then_inc(selg_ready, 1)
                    for t in range(TT):
                        ins = dve.tensor_scalar(sel[:, t, 0:HALF], iota[:, 0:HALF], posb[:, t, 0:1], None, ALU.is_equal)
                    ins.then_inc(sel_ready, 1)
                    activate(i + NEXP, 0)
                    expert_rows(i + NEXP, 0)
                    assert steps[0] == PER["job"], steps[0]
            dve.wait_ge(scattered, n_jobs + 1)
            for c in range(DC):
                ins = dve.scalar_tensor_tensor(out=x[:, c, :], in0=bank[c // 2][:, (c % 2) * T:(c % 2 + 1) * T],
                                               scalar=mod[:, GT2 + c, 0:1], in1=x[:, c, :], op0=ALU.mult, op1=ALU.add)
            ins.then_inc(bh_ready, 1)
            dve.wait_ge(scored, SCORE0 + S_FINAL + 1)
            dve.tensor_scalar(bvarx, score[:, 0:T], 1.0 / D, EPS, ALU.mult, ALU.add).then_inc(bvar, 1)
            dve.wait_ge(broot, 5)
            dve.reciprocal(brsx, brsx).then_inc(bh_ready, 1)
            dve.wait_ge(bh_ready, 5)
            for c in range(DC):
                ins = dve.scalar_tensor_tensor(out=h[:, c, :], in0=x[:, c, :], scalar=b_("g_final", c, 1), in1=brsx,
                                               op0=ALU.mult, op1=ALU.mult)
            ins.then_inc(final_ready, 1)

        def columns(weights, a, n):
            return weights[:, a:a + n].rearrange("(c p) n -> p c n", p=P)

        @block.sync
        def _(sp):
            for dst, src in ((x[:], xT), (cst[:], consts), (lpar[:], layer_params)):
                sp.dma_start(dst, src).then_inc(loaded, 16)

            def tile(l, n, parts):
                sp.wait_ge(unit_done, slot_left(l, n))
                sp.sem_inc(asked, 1)
                dst, src = parts
                sp.dma_start(dst, src).then_inc(landed[n % RING], 16)

            def slot(n):
                return ring[:, n % RING, :].rearrange("p (c n) -> p c n", c=DC)

            with sp.Fori(0, LAYERS) as l:
                wl = w_in[bass.ds(l, 1)].rearrange("a k n -> (a k) n")
                tile(l, 0, (slot(0)[:, :, 0:LORA], columns(wl, COL_LORA, LORA)))
                for g in range(GROUPS):
                    tile(l, 1 + g, (slot(1 + g), columns(wl, COL_DQ + g * W, W)))
                sp.wait_ge(unit_done, slot_left(l, 4))
                sp.sem_inc(asked, 1)
                s4 = ring[:, 4 % RING, :]
                sp.dma_start(s4[:, 0:2 * 768].rearrange("p (c n) -> p c n", c=2),
                             w_uq[bass.ds(l, 1)].rearrange("a (c p) n -> p (a c) n", p=P)).then_inc(loaded, 16)
                sp.dma_start(s4[:, 2 * 768:2 * 768 + D],
                             w_ukv[bass.ds(l, 1)].rearrange("a p n -> p (a n)")).then_inc(landed[0], 16)
                for g in range(GROUPS):
                    tile(l, 5 + g, (slot(5 + g), columns(wl, COL_DK + g * W, W)))
                for g in range(GROUPS):
                    tile(l, 8 + g, (slot(8 + g), columns(wl, COL_DV + g * W, W)))
                for n, a in ((11, COL_BZ), (12, COL_CZ), (13, COL_AC), (14, COL_AX), (15, COL_AB), (16, COL_AZ)):
                    tile(l, n, (slot(n), columns(wl, a, W)))
                for i in range(6):
                    tile(l, 17 + i, (slot(17 + i), columns(wl, COL_GATE + i * W, W)))
                for b, wb in enumerate((w_out_a, w_out_b, w_out_c)):
                    tile(l, 23 + b, (ring[:, (23 + b) % RING, :].rearrange("p (c n) -> p c n", c=4),
                                     wb[bass.ds(l, 1)].rearrange("a (c p) n -> p (a c) n", p=P)))
                wol = w_o[bass.ds(l, 1)].rearrange("a k n -> (a k) n")
                for n in range(2):
                    tile(l, 26 + n, (slot(26 + n), columns(wol, n * W, W)))
            if debug == "layers":
                for b in range(BANKS):
                    sp.wait_ge(bank_free[b], LAYERS * PER_BANK + 1)
                sp.dma_start(out, x[:]).then_inc(stored, 16)
                sp.wait_ge(stored, 16)
            else:
                block_sync(sp)

        @block.tensor
        def _(pe):
            pe.wait_ge(loaded, 48)
            pe.sem_inc(unit_done, NU)

            def norm_sum(source, n_chunks, columns):
                for c in range(n_chunks):
                    ins = pe.matmul(score[:, 0:columns], ones, source[:, c, :], start=c == 0,
                                    stop=c == n_chunks - 1)
                return ins

            def unit(l, u):
                kind, tl, who = UNITS[u]
                pe.wait_ge(landed[tl % RING], l * (16 * NT // RING) + 16 * (tl // RING + 1))
                pe.wait_ge(bank_free[u % BANKS], freed(l, u) - 1)
                b = bank[u % BANKS]
                w8 = ring[:, tl % RING, :].rearrange("p (c n) -> p c n", c=DC)
                w4 = ring[:, tl % RING, :].rearrange("p (c n) -> p c n", c=4)
                if kind in ("lora", "dq", "dk", "dv"):
                    t = who[-1]
                    n = LORA if kind == "lora" else W
                    for c in range(DC):
                        ins = pe.matmul(b[:, 0:n], h[:, c, t * P:(t + 1) * P], w8[:, c, 0:n],
                                        start=c == 0, stop=c == DC - 1)
                elif kind == "mq":
                    half, t = who
                    pe.wait_ge(loaded, l * 16 + 64)
                    wq = ring[:, tl % RING, 0:1536].rearrange("p (c n) -> p c n", c=2)
                    for c in range(2):
                        ins = pe.matmul(b[:, 0:384], cT[:, c, t * P:(t + 1) * P],
                                        wq[:, c, half * 384:(half + 1) * 384], start=c == 0, stop=c == 1)
                elif kind == "mkv":
                    half, t = who
                    ins = pe.matmul(b[:, :], cT[:, 2, t * P:(t + 1) * P],
                                    ring[:, tl % RING, 1536 + half * W:1536 + (half + 1) * W],
                                    start=True, stop=True)
                elif kind == "merge":
                    p, br = who
                    y = (conv, yB, yC)[br]
                    for i in range(2):
                        m = (2 * p + i) * P
                        for c in range(4):
                            ins = pe.matmul(b[:, i * T:(i + 1) * T], w4[:, c, m:m + P], y[:, c, :],
                                            start=c == 0, stop=c == 3)
                else:
                    p = who[-1]
                    for i in range(2):
                        m = (2 * p + i) * P
                        for c in range(DC):
                            ins = pe.matmul(b[:, i * T:(i + 1) * T], w8[:, c, m:m + P], h[:, c, :],
                                            start=c == 0, stop=c == DC - 1)
                return ins

            def turn(l, u):
                kind = UNITS[u][0]
                n = NORMED.index(u)
                pe.wait_ge(qn_ready, l * NN + n + 1)
                pe.wait_ge(flip_free, l * NTR + n + 1)
                src = qn[:, n % 2, :]
                if kind == "lora":
                    blocks = [(P, src[:, i * P:(i + 1) * P]) for i in range(3)]
                elif kind in ("dq", "dk"):
                    blocks = [(P, src[:, i * P:(i + 1) * P]) for i in range(4)]
                else:
                    blocks = [(MQK, src[:, i * MQK:(i + 1) * MQK]) for i in range(4)]
                for i, (m, blk) in enumerate(blocks):
                    ins = pe.transpose(flip[0:m, i * P:(i + 1) * P], blk, ident)
                ins.then_inc(flipped, 1)

            def scores(l, j):
                pe.wait_ge(score_free, l * NS + j + 2)
                job = JOBS[j]
                if job[0] == "mla":
                    q, k = mqT[0:MQK, job[1], :], mkT[0:MQK, job[1], :]
                    pe.matmul(score[:, 0:P], q[:, 0:P], k[:, 0:P], start=True, stop=True)
                    ins = pe.matmul(score[:, P:P + T], q[:, P:T], k, start=True, stop=True)
                else:
                    _, hd, t = job
                    n = (t + 1) * P
                    lo = HALF * (hd % 2)
                    for g in range(GROUPS):
                        q = dqT[lo:lo + HALF, g * 4 + hd // 2, t * P:(t + 1) * P]
                        k = dkT[lo:lo + HALF, g * 4 + hd // 2, 0:n]
                        ins = pe.matmul(score[:, g * n:(g + 1) * n], q, k, start=True, stop=True)
                ins.then_inc(scored, 1)

            def values(l, j):
                job = JOBS[j]
                hd = job[1]
                lo = HALF * (hd % 2)
                pe.wait_ge(probs_ready, l * NJ + j + 1)
                pe.wait_ge(mixed_free, l * NJ + j + 1)
                blocks = 3 if job[0] == "mla" or job[2] == 0 else 6
                for r, cols in enumerate(ROUNDS[j]):
                    fr = first_flip(j) + r
                    pe.wait_ge(flip_free, l * NTR + fr + 1)
                    for i, c in enumerate(cols):
                        ins = pe.transpose(flip[:, i * P:(i + 1) * P], probs[:, j % 2, c * P:(c + 1) * P], ident)
                    ins.then_inc(flipped, 1)
                    pe.wait_ge(flip_free, l * NTR + fr + 2)
                    pt = turned[:, (FIRST_ROUND[j] + r) % 2, :]
                    for i, c in enumerate(cols):
                        if job[0] == "mla":
                            o = mixed[lo:lo + HALF, (0, P, P)[c]:(0, P, P)[c] + P]
                            v = mv[:, (0, 0, 1)[c], hd * HALF:(hd + 1) * HALF]
                            first, last = c < 2, c != 1
                        else:
                            t = job[2]
                            g, kt = c // (t + 1), c % (t + 1)
                            o = mixed[lo:lo + HALF, 0:P]
                            v = dv[:, kt, g * W + hd * HALF:g * W + (hd + 1) * HALF]
                            first, last = c == 0, c == blocks - 1
                        ins = pe.matmul(o, v, pt[:, i * P:(i + 1) * P], start=first, stop=last)
                ins.then_inc(mixed_done, 1)

            with pe.Fori(0, LAYERS) as l:
                pe.wait_ge(squared, l + 1)
                pe.wait_ge(score_free, l * NS + 1)
                norm_sum(h, DC, T).then_inc(scored, 1)
                pe.wait_ge(hready, l + 1)

                def step(u):
                    unit(l, u).then_inc(unit_done, 1)

                for u in range(PREP + LAG):
                    if u < PREP:
                        if UNITS[u][0] in ("mq",) and UNITS[u][2] == (0, 0):
                            pe.wait_ge(flip_free, l * NTR + 2 + 1)
                        step(u)
                    if u >= LAG and u - LAG in NORMED:
                        turn(l, u - LAG)
                pe.wait_ge(flip_free, l * NTR + NN + 1)
                pe.wait_ge(bank_free[(PREP - 1) % BANKS], freed(l, PREP - 1))
                for b in range(1, BANKS):
                    pe.wait_ge(bank_free[(PREP - 1 - b) % BANKS], freed(l, PREP - 1 - b))
                for j in range(NJ + 1):
                    if j < NJ:
                        scores(l, j)
                    if PREP + j < FILL:
                        step(PREP + j)
                    if j > 0:
                        values(l, j - 1)
                pe.wait_ge(conv_ready, l + 1)
                pe.wait_ge(mixed_free, l * NJ + NJ + 1)
                for u in range(FILL, MERGED):
                    step(u)
                pe.wait_ge(merged, l + 1)
                for u in range(MERGED, NU):
                    step(u)
            if debug != "layers":
                block_tensor(pe)

        @block.scalar
        def _(act):
            act.wait_ge(loaded, 48)
            act.sem_inc(flip_free, 1)

            def squares_of(l, n, src, width):
                act.wait_ge(squares_used, l * NN + n + 1)
                act.activation(square[:, 0:width], src, ACT.Square).then_inc(squares, 1)

            def root(l, n):
                act.wait_ge(var_ready, l * NN + n + 1)
                act.activation(rs, var, ACT.Sqrt).then_inc(rs_ready, 1)

            def unflip(l, n):
                kind, _, who = UNITS[NORMED[n]]
                act.wait_ge(flipped, l * NTR + n + 1)
                t = who[-1]
                cols = slice(t * P, (t + 1) * P)
                v = flip[:, :].rearrange("p (a t) -> p a t", t=P)
                if kind == "lora":
                    act.activation(cT[:, 0, cols], v[:, 0, :], ACT.Copy, scale=l_("q_a", 0, 1))
                    act.activation(cT[:, 1, cols], v[:, 1, :], ACT.Copy, scale=l_("q_a", 1, 1))
                    ins = act.activation(cT[:, 2, cols], v[:, 2, :], ACT.Copy, scale=l_("kv_a", 0, 1))
                elif kind in ("dq", "dk"):
                    g = who[0]
                    dst = (dqT if kind == "dq" else dkT)[:, 4 * g:4 * g + 4, cols]
                    ins = act.activation(dst, v[:, 0:4, :], ACT.Copy,
                                         scale=l_("dil_q" if kind == "dq" else "dil_k", g, 1))
                else:
                    half = who[0]
                    dst = (mqT if kind == "mq" else mkT)[0:MQK, 4 * half:4 * half + 4, cols]
                    ins = act.activation(dst, v[0:MQK, 0:4, :], ACT.Copy,
                                         scale=MQK ** -0.5 if kind == "mq" else 1.0)
                ins.then_inc(flip_free, 1)

            def evacuate(l, u):
                kind, _, who = UNITS[u]
                b = bank[u % BANKS]
                if kind in ("merge", "out", "ac", "ax", "ab"):
                    return
                if kind == "mkv":
                    act.wait_ge(copied, l * 4 + [x for x in range(NU) if UNITS[x][0] == "mkv"].index(u) + 1)
                    squares_of(l, NORMED.index(u), mc.rearrange("p a b -> p (a b)"), 384)
                    root(l, NORMED.index(u))
                    return
                act.wait_ge(unit_done, done(l, u))
                if kind == "lora":
                    squares_of(l, NORMED.index(u), b[:, 0:384], 384)
                elif kind in ("dq", "dk"):
                    squares_of(l, NORMED.index(u), b[:, :], W)
                elif kind == "mq":
                    squares_of(l, NORMED.index(u), b[:, 0:384], 384)
                if u in NORMED:
                    root(l, NORMED.index(u))
                elif kind == "dv":
                    g, t = who
                    act.activation(dv[:, t, g * W:(g + 1) * W], b[:, :], ACT.Copy).then_inc(bank_free[u % BANKS], 1)
                elif kind in ("z", "az"):
                    z = ZUNITS.index(u)
                    if z:
                        act.wait_ge(bank_free[ZUNITS[z - 1] % BANKS], freed(l, ZUNITS[z - 1]))
                    act.activation(tanh_z, b[:, :], ACT.Tanh, scale=0.5).then_inc(z_tanh, 1)
                elif kind == "gate":
                    n, p = who
                    for i in range(2):
                        c = 4 * n + 2 * p + i
                        ins = act.activation(gates[:, c, :], b[:, i * T:(i + 1) * T], ACT.Tanh, scale=0.5,
                                             bias=l_("b_gate", c, 1))
                    ins.then_inc(bank_free[u % BANKS], 1)

            def exp(l, j):
                job = JOBS[j]
                act.wait_ge(masked, l * NJ + j + 1)
                pr, st = probs[:, j % 2, :], stat[:, j % 2, :]
                if job[0] == "mla":
                    act.activation(pr[:, 0:P], pr[:, 0:P], ACT.Exp, bias=st[:, 2:3], accum_out=st[:, 4:5])
                    ins = act.activation(pr[:, P:384], pr[:, P:384], ACT.Exp, bias=st[:, 3:4],
                                         accum_out=st[:, 5:6])
                else:
                    n = 384 * (job[2] + 1)
                    ins = act.activation(pr[:, 0:n], pr[:, 0:n], ACT.Exp, bias=st[:, 2:3], accum_out=st[:, 4:5])
                ins.then_inc(exped, 1)

            def unflip_probs(l, j):
                for r in range(len(ROUNDS[j])):
                    rr = FIRST_ROUND[j] + r
                    act.wait_ge(flipped, l * NTR + NN + rr + 1)
                    if r == 0 and j >= 1:
                        act.wait_ge(mixed_done, l * NJ + j)
                    act.activation(turned[:, rr % 2, 0:384], flip[:, 0:384], ACT.Copy).then_inc(flip_free, 1)

            with act.Fori(0, LAYERS) as l:
                act.wait_ge(bank_free[(NU - 1) % BANKS], freed(l, NU - 1) - PER_BANK)
                act.activation(h[:], x[:], ACT.Square).then_inc(squared, 1)
                act.wait_ge(score_free, l * NS + 2)
                act.activation(rsx, varx, ACT.Sqrt).then_inc(rsx_ready, 1)
                act.wait_ge(par_ready, l + 1)
                for u in range(PREP + LAG):
                    if u < PREP:
                        evacuate(l, u)
                    if u >= LAG and u - LAG in NORMED:
                        unflip(l, NORMED.index(u - LAG))
                for j in range(NJ + 1):
                    if j < NJ:
                        exp(l, j)
                    if PREP + j < FILL:
                        evacuate(l, PREP + j)
                    if j > 0:
                        unflip_probs(l, j - 1)
            if debug != "layers":
                block_scalar(act)

        @block.vector
        def _(dve):
            steps = [0]
            base = [0]

            def link(ins):
                steps[0] += 1
                ins.then_inc(chain, 1)
                dve.wait_ge(chain, base[0] + steps[0])

            dve.wait_ge(loaded, 48)
            for s in (score_free, mixed_free, squares_used, *bank_free):
                dve.sem_inc(s, 1)
            link(dve.memset(up[:, :, 0:2], 0.0))
            link(dve.memset(var, 1.0))
            start = steps[0]
            steps[0] = 0

            def mean(dst, src, n):
                return dve.tensor_scalar(dst, src, 1.0 / n, EPS, ALU.mult, ALU.add)

            def heads(v, n):
                return v.rearrange("p (a b) -> p a b", b=n)

            def rotate(v, cos, sin, n):
                a = v.shape[1]
                r0 = rope[:, 0, 0:a * n].rearrange("p (a two n) -> p a two n", a=a, two=2)
                r1 = rope[:, 1, 0:a * n].rearrange("p (a two n) -> p a two n", a=a, two=2)
                full = [P, a, 2, n // 2]
                part = [P, a, n // 2]
                dve.tensor_tensor(r0, v, cos.broadcast_to(full), ALU.mult)
                dve.tensor_tensor(r1[:, :, 0, :], v[:, :, 1, :], sin[:, :, 0, :].broadcast_to(part), ALU.mult)
                link(dve.tensor_tensor(r1[:, :, 1, :], v[:, :, 0, :], sin[:, :, 1, :].broadcast_to(part), ALU.mult))
                return dve.tensor_tensor(v, r0, r1, ALU.add)

            def normalize(l, u):
                kind, _, who = UNITS[u]
                n = NORMED.index(u)
                t = who[-1]
                b = bank[u % BANKS]
                q = qn[:, n % 2, :]
                if kind == "mkv":
                    half = who[0]
                    dve.wait_ge(unit_done, done(l, u))
                    kv = heads(b[:, :], P)
                    mch = mc[:, :, :]
                    dve.tensor_copy(mch[:, :, 0:HALF], kv[:, :, 0:HALF])
                    dve.tensor_copy(mch[:, :, HALF:MQK], kpe[:, t:t + 1, :].broadcast_to([P, 4, MROPE])).then_inc(copied, 1)
                    dve.tensor_copy(heads(mv[:, t, half * 256:(half + 1) * 256], HALF),
                                    kv[:, :, HALF:P]).then_inc(bank_free[u % BANKS], 1)
                dve.wait_ge(squares, l * NN + n + 1)
                if kind == "lora":
                    link(dve.tensor_reduce(ssum[:, 0:1], square[:, 0:256], AX.X, ALU.add))
                    dve.tensor_reduce(ssum[:, 1:2], square[:, 256:384], AX.X, ALU.add).then_inc(squares_used, 1)
                    dve.wait_ge(squares_used, l * NN + n + 2)
                    link(mean(var[:, 0:1], ssum[:, 0:1], 256))
                    mean(var[:, 1:2], ssum[:, 1:2], 128).then_inc(var_ready, 1)
                else:
                    a, w = (8, HALF) if kind in ("dq", "dk") else (4, MQK)
                    dve.tensor_reduce(ssum[:, 0:a], heads(square[:, 0:a * w], w), AX.X,
                                      ALU.add).then_inc(squares_used, 1)
                    dve.wait_ge(squares_used, l * NN + n + 2)
                    mean(var[:, 0:a], ssum[:, 0:a], w).then_inc(var_ready, 1)
                dve.wait_ge(rs_ready, l * NN + n + 1)
                link(dve.reciprocal(rs, rs))
                if n >= 2:
                    dve.wait_ge(flipped, l * NTR + n - 1)
                if kind == "lora":
                    link(dve.tensor_copy(kpe[:, t, :], b[:, 384:416]))
                    link(dve.tensor_scalar(q[:, 0:256], b[:, 0:256], rs[:, 0:1], None, ALU.mult))
                    dve.tensor_scalar(q[:, 256:384], b[:, 256:384], rs[:, 1:2], None,
                                      ALU.mult).then_inc(bank_free[u % BANKS], 1)
                    dve.wait_ge(bank_free[u % BANKS], freed(l, u))
                    dve.sem_inc(qn_ready, 1)
                elif kind in ("dq", "dk"):
                    link(dve.tensor_tensor(heads(q, HALF), heads(b[:, :], HALF),
                                           rs[:, 0:8].unsqueeze(2).broadcast_to([P, 8, HALF]), ALU.mult))
                    dve.sem_inc(bank_free[u % BANKS], 1)
                    dve.sem_inc(qn_ready, 1)
                else:
                    src = heads(b[:, 0:384], MQK) if kind == "mq" else mc[:, :, :]
                    qh = heads(q[:, 0:384], MQK)
                    link(dve.tensor_tensor(qh, src, rs[:, 0:4].unsqueeze(2).broadcast_to([P, 4, MQK]), ALU.mult))
                    if kind == "mq":
                        dve.sem_inc(bank_free[u % BANKS], 1)
                    g = l_("mla_q" if kind == "mq" else "mla_k").unsqueeze(1).broadcast_to([P, 4, MQK])
                    link(dve.tensor_tensor(qh, qh, g, ALU.mult))
                    cs = c_("cosm")[:, t * 32:(t + 1) * 32].rearrange("p (a two n) -> p a two n", a=1, two=2)
                    sn = c_("sinm")[:, t * 32:(t + 1) * 32].rearrange("p (a two n) -> p a two n", a=1, two=2)
                    rotate(qh[:, :, HALF:MQK].rearrange("p a (two n) -> p a two n", two=2), cs, sn,
                           MROPE).then_inc(qn_ready, 1)

            def evacuate(l, u):
                kind, _, who = UNITS[u]
                b = bank[u % BANKS]
                free = bank_free[u % BANKS]
                if kind in ("dv", "gate"):
                    return
                if u in NORMED:
                    normalize(l, u)
                    return
                p = who[-1] if kind != "merge" else who[0]
                pair = slice(2 * p, 2 * p + 2)
                both = heads(b[:, :], T)
                if kind in ("z", "az"):
                    dve.wait_ge(z_tanh, l * len(ZUNITS) + ZUNITS.index(u) + 1)
                else:
                    dve.wait_ge(unit_done, done(l, u))
                if kind == "z":
                    dve.scalar_tensor_tensor(out=(yB, yC)[who[0]][:, pair, :], in0=heads(tanh_z, T), scalar=1.0,
                                             in1=both, op0=ALU.add, op1=ALU.mult).then_inc(free, 1)
                elif kind == "ac":
                    dve.tensor_copy(conv[:, pair, :], both).then_inc(free, 1)
                elif kind == "ax":
                    dve.wait_ge(bank_free[(u - 2) % BANKS], freed(l, u - 2))
                    dve.tensor_tensor(up[:, pair, 2:T + 2], conv[:, pair, :], both, ALU.mult).then_inc(free, 1)
                elif kind == "ab":
                    dve.wait_ge(bank_free[(u - 2) % BANKS], freed(l, u - 2))
                    for c in range(2 * p, 2 * p + 2):
                        link(dve.tensor_scalar(conv[:, c, :], up[:, c, 0:T], l_("conv_w", c, 1),
                                               l_("conv_b", c, 1), ALU.mult, ALU.add))
                        for tap in (1, 2):
                            link(dve.scalar_tensor_tensor(out=conv[:, c, :], in0=up[:, c, tap:tap + T],
                                                          scalar=l_("conv_w", 4 * tap + c, 1), in1=conv[:, c, :],
                                                          op0=ALU.mult, op1=ALU.add))
                    dve.tensor_tensor(conv[:, pair, :], conv[:, pair, :], both, ALU.mult).then_inc(free, 1)
                elif kind == "az":
                    dve.wait_ge(bank_free[(u - 2) % BANKS], freed(l, u - 2))
                    dve.scalar_tensor_tensor(out=heads(mtmp, T), in0=heads(tanh_z, T), scalar=1.0,
                                             in1=both, op0=ALU.add, op1=ALU.mult).then_inc(free, 1)
                    dve.wait_ge(free, freed(l, u))
                    ins = dve.scalar_tensor_tensor(out=conv[:, pair, :], in0=heads(mtmp, T), scalar=0.5,
                                                   in1=conv[:, pair, :], op0=ALU.mult, op1=ALU.mult)
                    if p == 1:
                        ins.then_inc(conv_ready, 1)
                elif kind == "merge":
                    br = who[1]
                    gsl = gates[:, DC * br + 2 * p:DC * br + 2 * p + 2, :]
                    dst = h[:, pair, :] if br == 0 else heads(mtmp, T)
                    dve.scalar_tensor_tensor(out=dst, in0=gsl, scalar=1.0, in1=both, op0=ALU.add,
                                             op1=ALU.mult).then_inc(free, 1)
                    dve.wait_ge(free, freed(l, u))
                    if br:
                        ins = dve.tensor_tensor(h[:, pair, :], h[:, pair, :], heads(mtmp, T), ALU.add)
                        if u == MERGED - 1:
                            ins.then_inc(merged, 1)
                        else:
                            link(ins)
                elif kind == "out":
                    c = 4 * who[0] + 2 * p
                    dve.scalar_tensor_tensor(out=x[:, c:c + 2, :], in0=both, scalar=0.5, in1=x[:, c:c + 2, :],
                                             op0=ALU.mult, op1=ALU.add).then_inc(free, 1)

            def mask(l, j):
                job = JOBS[j]
                dve.wait_ge(scored, l * NS + j + 2)
                pr, st = probs[:, j % 2, :], stat[:, j % 2, :]
                if job[0] == "mla":
                    dve.tensor_tensor(pr[:, 0:384], score[:, 0:384], c_("mask"), ALU.add).then_inc(score_free, 1)
                    dve.wait_ge(score_free, l * NS + j + 3)
                    dve.tensor_reduce(st[:, 0:1], pr[:, 0:P], AX.X, ALU.max)
                    link(dve.tensor_reduce(st[:, 1:2], pr[:, P:384], AX.X, ALU.max))
                    dve.tensor_scalar(st[:, 2:4], st[:, 0:2], -1.0, None, ALU.mult).then_inc(masked, 1)
                else:
                    _, hd, t = job
                    n = (t + 1) * P
                    for g in range(GROUPS):
                        bias = c_("dist")[:, 384 * g + P * t:384 * g + P * t + n]
                        ins = dve.scalar_tensor_tensor(out=pr[:, g * n:(g + 1) * n], in0=bias, scalar=slope(g, hd),
                                                       in1=score[:, g * n:(g + 1) * n], op0=ALU.mult, op1=ALU.add)
                        if g < GROUPS - 1:
                            link(ins)
                    ins.then_inc(score_free, 1)
                    dve.wait_ge(score_free, l * NS + j + 3)
                    link(dve.tensor_reduce(st[:, 0:1], pr[:, 0:3 * n], AX.X, ALU.max))
                    dve.tensor_scalar(st[:, 2:3], st[:, 0:1], -1.0, None, ALU.mult).then_inc(masked, 1)

            def divide(l, j):
                job = JOBS[j]
                pr, st = probs[:, j % 2, :], stat[:, j % 2, :]
                dve.wait_ge(exped, l * NJ + j + 1)
                if job[0] == "mla":
                    link(dve.reciprocal(st[:, 6:8], st[:, 4:6]))
                    link(dve.tensor_scalar(pr[:, 0:P], pr[:, 0:P], st[:, 6:7], None, ALU.mult))
                    dve.tensor_scalar(pr[:, P:384], pr[:, P:384], st[:, 7:8], None,
                                      ALU.mult).then_inc(probs_ready, 1)
                else:
                    n = 384 * (job[2] + 1)
                    link(dve.reciprocal(st[:, 6:7], st[:, 4:5]))
                    dve.tensor_scalar(pr[:, 0:n], pr[:, 0:n], st[:, 6:7], None, ALU.mult).then_inc(probs_ready, 1)

            def gated(l, j):
                job = JOBS[j]
                hd = job[1]
                lo = HALF * (hd % 2)
                dve.wait_ge(mixed_done, l * NJ + j + 1)
                y = yB if job[0] == "mla" else yC
                cols = slice(0, T) if job[0] == "mla" else slice(job[2] * P, (job[2] + 1) * P)
                n = T if job[0] == "mla" else P
                dst = y[lo:lo + HALF, hd // 2, cols]
                dve.scalar_tensor_tensor(out=dst, in0=mixed[lo:lo + HALF, 0:n], scalar=0.5, in1=dst,
                                         op0=ALU.mult, op1=ALU.mult).then_inc(mixed_free, 1)

            with dve.Fori(0, LAYERS) as l:
                base[0] = l * PER["layer"] + start
                link(dve.tensor_copy(par[:, :], lpar[:, bass.ds(l, 1), :].rearrange("p a n -> p (a n)")))
                link(dve.tensor_scalar(l_("dil_q"), l_("dil_q"), HALF ** -0.5, None, ALU.mult))
                dve.tensor_scalar(l_("b_gate"), l_("b_gate"), 0.5, None, ALU.mult).then_inc(par_ready, 1)
                dve.wait_ge(par_ready, l + 1)
                dve.wait_ge(scored, l * NS + 1)
                dve.tensor_scalar(varx, score[:, 0:T], 1.0 / D, EPS, ALU.mult, ALU.add).then_inc(score_free, 1)
                dve.wait_ge(rsx_ready, l + 1)
                link(dve.reciprocal(rsx, rsx))
                for c in range(DC):
                    ins = dve.scalar_tensor_tensor(out=h[:, c, :], in0=x[:, c, :], scalar=l_("norm_g", c, 1),
                                                   in1=rsx, op0=ALU.mult, op1=ALU.mult)
                ins.then_inc(hready, 1)
                for u in range(PREP):
                    evacuate(l, u)
                for j in range(NJ + 1):
                    if j < NJ:
                        mask(l, j)
                    if PREP + j < FILL:
                        evacuate(l, PREP + j)
                    if j < NJ:
                        divide(l, j)
                    if j > 0:
                        gated(l, j - 1)
                dve.wait_ge(bank_free[(FILL - 1) % BANKS], freed(l, FILL - 1))
                dve.wait_ge(bank_free[(FILL - 2) % BANKS], freed(l, FILL - 2))
                for u in range(FILL, NU):
                    evacuate(l, u)
                assert steps[0] == PER["layer"], steps[0]
            if debug != "layers":
                steps[0] += start + (LAYERS - 1) * PER["layer"]
                base[0] = 0
                block_vector(dve, link, steps, base)


def constants():
    import numpy as np
    out = {}
    p = np.arange(P)
    out["ident"] = np.eye(P)
    out["ones"] = np.ones((P, P))
    tok = np.arange(T, dtype=np.float32).reshape(TT, P).T
    inv = 10000.0 ** (-np.arange(0, MROPE, 2, dtype=np.float32) / MROPE)
    ang = tok[:, :, None] * inv.astype(np.float32)
    out["cosm"] = np.stack([np.cos(ang), np.cos(ang)], axis=2)
    out["sinm"] = np.stack([-np.sin(ang), np.sin(ang)], axis=2)
    query = np.concatenate([np.broadcast_to(p[:, None], (P, P)), np.broadcast_to(p[:, None] + P, (P, T))], axis=1)
    key = np.concatenate([np.arange(P), np.arange(T)])[None, :]
    far = query - key
    out["mask"] = np.where(far >= 0, 0.0, MASKED)
    out["dist"] = np.stack([np.where((far >= 0) & (far % d == 0) & (far // d <= w // d), -far, MASKED)
                            for w, d in ((128, 1), (512, 4), (2048, 16))], axis=1)
    out["iota"] = np.broadcast_to(np.concatenate([np.arange(SLOTS)] * 4), (P, 2 * P))
    inv = 10000.0 ** (-np.arange(16, dtype=np.float32) / 16)
    axes = np.stack([tok // 64, tok % 64], axis=2)
    ang = axes[:, :, :, None] * inv.astype(np.float32)
    out["cosx"] = np.stack([np.cos(ang), np.cos(ang)], axis=3)
    out["sinx"] = np.stack([-np.sin(ang), np.sin(ang)], axis=3)
    out["before"] = (p[:, None] < p[None, :])
    out["pick"] = p[:, None] % 32 == np.arange(2)[None, :]
    out["expert"] = np.broadcast_to(np.tile(np.arange(NEXP), 3), (P, 96))
    out["start"] = np.broadcast_to(np.repeat(np.arange(1, 4) * SLOTS, NEXP), (P, 96))
    out["job"] = np.broadcast_to(np.arange(1, MAXJOBS + 1), (P, MAXJOBS))
    return np.concatenate([out[k].reshape(P, -1).astype(np.float32) for k in CONSTS], axis=1)


def arrange(inputs):
    import numpy as np

    def f(name):
        return np.ascontiguousarray(inputs[name])

    def fm(a):
        a = a.reshape(*a.shape[:-1], -1, P)
        return np.moveaxis(a, -1, 0)

    def rows(a):
        return np.broadcast_to(a.reshape(1, -1), (P, a.size))

    x, lay, blk = f("x"), {}, {}
    lay["norm_g"] = fm(f("norm_g"))
    lay["b_gate"] = fm(f("b_gate"))
    lay["conv_w"] = fm(f("conv_w"))
    lay["conv_b"] = fm(f("conv_b"))
    lay["q_a"] = fm(f("q_a_norm_g"))
    lay["kv_a"] = fm(f("kv_a_norm_g"))
    for k in "qk":
        g = f(f"dil_{k}_norm_g")
        lay[f"dil_{k}"] = np.moveaxis(np.concatenate([g, g], axis=2), 2, 0)
        g = f(f"mla_{k}_norm_g")
        lay[f"mla_{k}"] = np.broadcast_to(g[None], (P, *g.shape))
    layer_params = np.concatenate([lay[k].reshape(P, LAYERS, -1) for k in LAYER_PARAMS], axis=2)
    blk["b_ada"] = fm(f("b_ada_2")[0])
    blk["g_attn"] = fm(f("g_attn_2")[0])
    blk["g_ffn"] = fm(f("g_ffn_2")[0])
    blk["g_final"] = fm(f("g_final_2"))
    blk["subln"] = fm(f("diff_subln_2")[0])
    blk["c"] = np.stack([fm(f("c_2")[0]), fm(f("c_ctx_2"))], axis=2)
    blk["gqa_q"] = rows(f("gqa_q_norm_2"))
    blk["gqa_k"] = rows(f("gqa_k_norm_2"))
    blk["lam"] = rows(f("diff_lambda_2"))
    blk["b_router"] = rows(f("b_router_2"))
    blk["w_router"] = np.moveaxis(f("w_router_2")[0].reshape(DC, P, NEXP), 1, 0)
    block_params = np.concatenate([blk[k].reshape(P, -1) for k in BLOCK_PARAMS], axis=1)
    return dict(
        in_x=np.ascontiguousarray(np.moveaxis(x[0].reshape(T, DC, P), (0, 1, 2), (2, 1, 0))),
        in_ctx=np.ascontiguousarray(np.moveaxis(f("ctx_2")[0].reshape(T, DC, P), (0, 1, 2), (2, 1, 0))),
        in_consts=constants(), in_layer_params=np.ascontiguousarray(layer_params),
        in_block_params=np.ascontiguousarray(block_params),
        in_w_in=f("w_in"), in_w_uq=f("w_uq"), in_w_ukv=f("w_ukv"), in_w_out_a=f("w_out_a"),
        in_w_out_b=f("w_out_b"), in_w_out_c=f("w_out_c"), in_w_o=f("w_o"), in_w_ada=f("w_ada_2")[0],
        in_w_qkv=f("w_qkv_2")[0], in_w_o2=f("w_o_2")[0], in_e_in=f("w_in_2")[0], in_eb_in=f("b_in_2")[0],
        in_e_out=f("w_out_2")[0], in_eb_out=f("b_out_2")[0])


def kernel(**inputs):
    import numpy as np
    from concourse import bacc
    from concourse.bass_utils import run_bass_kernel_spmd

    arrays = arrange(inputs)
    nc = bacc.Bacc("TRN2", target_bir_lowering=False, num_devices=1)
    args = [nc.dram_tensor(f"{name}_dram", a.shape, mybir.dt.from_np(a.dtype), kind="ExternalInput").ap()
            for name, a in arrays.items()]
    out = nc.dram_tensor("out_0_dram", (P, DC, T), F32, kind="ExternalOutput").ap()
    build(nc, *args, out)
    r = run_bass_kernel_spmd(nc, [{f"{name}_dram": a for name, a in arrays.items()}], core_ids=[0])
    got = r.results[0]["out_0_dram"]
    return np.ascontiguousarray(np.moveaxis(got, (0, 1, 2), (2, 1, 0)).reshape(1, T, D))
```

```python
from contextlib import ExitStack

import concourse.bass as bass
from concourse import mybir

F32 = mybir.dt.float32
I32 = mybir.dt.int32
ALU = mybir.AluOpType
ACT = mybir.ActivationFunctionType
AX = mybir.AxisListType

P = 128
T = 256
TT = T // P
D = 1024
DC = D // P
LAYERS = 2
EPS = 1e-6
W = 512
HALF = 64
MQK, MROPE, MHEADS = 96, 32, 8
GROUPS, DHEADS = 3, 8
NEXP = 32
TOPK = 4
SLOTS = 64
MAXJOBS = 16
MASKED = -1.0e30
RING = 4
MRING = 6
TILE = 8 * W

COL_AB, COL_AC, COL_AX, COL_AZ, COL_LORA = 0, 512, 1024, 1536, 2048
COL_BZ, COL_DQ, COL_DK, COL_DV, COL_CZ, COL_GATE = 2464, 2976, 4512, 6048, 7584, 8096
N_IN = 11168
LORA = 416
N_QKV = 2304

UNITS = [("ada", n, (n,)) for n in range(4)]
ADAS = len(UNITS)
UNITS += [("lora", 4, (t,)) for t in range(TT)]
UNITS += [("dq", 5 + g, (g, t)) for g in range(GROUPS) for t in range(TT)]
LATENT = [("mq", 8, (h, t)) for h in range(2) for t in range(TT)]
LATENT += [("mkv", 8, (h, t)) for h in range(2) for t in range(TT)]
DILK = [("dk", 9 + g, (g, t)) for g in range(GROUPS) for t in range(TT)]
for kind in "mmdmmdmmdmdmdd":
    UNITS.append((LATENT if kind == "m" else DILK).pop(0))
UNITS += [("dv", 12 + g, (g, t)) for g in range(GROUPS) for t in range(TT)]
UNITS += [("z", 15 + b, (b, p)) for b in range(2) for p in range(2)]
PREP = len(UNITS)
UNITS += [("ac", 17, (p,)) for p in range(2)]
UNITS += [("ax", 18, (p,)) for p in range(2)]
UNITS += [("ab", 19, (p,)) for p in range(2)]
UNITS += [("az", 20, (p,)) for p in range(2)]
UNITS += [("gate", 21 + n, (n, p)) for n in range(6) for p in range(2)]
FILL = len(UNITS)
UNITS += [("merge", 27 + b, (p, b)) for p in range(4) for b in range(3)]
MERGED = len(UNITS)
UNITS += [("out", 30 + n, (n, p)) for n in range(2) for p in range(2)]
NU = len(UNITS)
NT = 32
BANKS = 4
PER_BANK = NU // BANKS
assert NU % BANKS == 0 and NT % RING == 0
NORMED = [u for u, x in enumerate(UNITS) if x[0] in ("lora", "dq", "mq", "mkv", "dk")]
NN = len(NORMED)
ZUNITS = [u for u, x in enumerate(UNITS) if x[0] in ("z", "az")]
LAG = 2

JOBS = [("mla", h) for h in range(MHEADS)] + [("dil", h, t) for h in range(DHEADS) for t in range(TT)]
NJ = len(JOBS)
ROUNDS = []
for job in JOBS:
    if job[0] == "mla":
        ROUNDS.append([[0, 1, 2]])
    elif job[2] == 0:
        ROUNDS.append([[0, 1, 2]])
    else:
        ROUNDS.append([[0, 1, 2], [3, 4, 5]])
NR = sum(map(len, ROUNDS))
FIRST_ROUND = [sum(map(len, ROUNDS[:j])) for j in range(NJ + 1)]
HALVES = [2] + [len(ROUNDS[j]) + (1 if j < 6 else 0) for j in range(NJ)]
assert sum(HALVES) == 2 * (FILL - PREP)
DONE_IN = [[PREP + u for u in range(FILL - PREP) if sum(HALVES[:s]) < 2 * u + 2 <= sum(HALVES[:s + 1])]
           for s in range(NJ + 1)]
NM = NJ + 1
NTR = NN + NR
NS = NJ + 1

BUNITS = [("qa", 0, (t,)) for t in range(TT)]
BUNITS += [("ka", 1, (t,)) for t in (2, 3, 0, 1)]
BFIRST = len(BUNITS)
BUNITS += [("qb", 2, (t,)) for t in range(TT)]
BUNITS += [("kb", 3, (t,)) for t in range(2 * TT)]
BUNITS += [("vb", 4, (t,)) for t in range(2 * TT)]
BADA = len(BUNITS)
BUNITS += [("ada", 5 + n, (n,)) for n in range(4)]
BQKV = len(BUNITS)
BUNITS += [("out2", 9 + n, (n, p)) for n in range(2) for p in range(2)]
NBU = len(BUNITS)
BTURNED = [u for u, x in enumerate(BUNITS) if x[0] in ("qa", "ka", "qb", "kb")]
BNORMED = [u for u, x in enumerate(BUNITS) if x[0] in ("qa", "ka")]
AHEADS, DIFFS = 8, 4
BJOBS = [("gqa", h, t) for h in range(AHEADS) for t in range(TT)]
BJOBS += [("diff", h, t) for h in range(DIFFS) for t in range(TT)]
NBJ = len(BJOBS)
BHALVES = [4] + [1] * NBJ
assert sum(BHALVES) == 2 * (BQKV - BFIRST)
BDONE_IN = [[BFIRST + u for u in range(BQKV - BFIRST) if sum(BHALVES[:s]) < 2 * u + 2 <= sum(BHALVES[:s + 1])]
            for s in range(NBJ + 1)]
BFLIPS = [("turn", u) for u in range(BFIRST)]
for s_ in range(1, NBJ + 1):
    BFLIPS.append(("job", s_ - 1))
    BFLIPS += [("turn", u) for u in BDONE_IN[s_ - 1] if u in BTURNED]
LAMBDA_INIT = 0.8 - 0.6 * 1.0
GLU_LIMIT = 7.0
GLU_ALPHA = 1.702
PAIRS = NEXP // 2

LAYER_PARAMS = dict(norm_g=DC, b_gate=3 * DC, conv_w=12, conv_b=4, q_a=2, kv_a=1, dil_q=3, dil_k=3,
                    mla_q=MQK, mla_k=MQK)
BLOCK_PARAMS = dict(b_ada=48, g_attn=DC, g_ffn=DC, g_final=DC, subln=1, gqa_q=HALF,
                    gqa_k=HALF, lam=4 * HALF, b_router=NEXP, w_router=DC * NEXP)
CONSTS = dict(ident=P, ones=P, cosm=2 * 32, sinm=2 * 32, mask=384, dist=GROUPS * 384, iota=2 * P,
              cosx=2 * 64, sinx=2 * 64, before=P, pick=2, expert=3 * NEXP, start=3 * NEXP, job=MAXJOBS)


def places(widths):
    at, out = 0, {}
    for name, n in widths.items():
        out[name] = (at, n)
        at += n
    return out, at


LP, NLP = places(LAYER_PARAMS)
BP, NBP = places(BLOCK_PARAMS)
CP, NCP = places(CONSTS)

CHAINED = dict(layer=175, pair=2, job=2)


def slope(g, h):
    return 2.0 ** (-8.0 * (g * DHEADS + h + 1) / (GROUPS * DHEADS))


def build(nc, c_in, xT, ctxT, consts, layer_params, block_params, w_in, w_uq, w_ukv, w_out_a, w_out_b, w_out_c,
          w_o, w_ada, w_qkv, w_o2, e_in, eb_in, e_out, eb_out, out, sizes=None, debug=None):
    PER = sizes or CHAINED
    with ExitStack() as ctx:
        def sb(name, shape, dt=F32):
            return ctx.enter_context(nc.sbuf_tensor(name, shape, dt))

        def sem(name):
            return ctx.enter_context(nc.semaphore(name))

        ring = sb("ring", [P, MRING, TILE])
        cst = sb("cst", [P, NCP])
        cvec = sb("cvec", [P, DC, 2])
        silu = sb("silu", [P, DC, 32])
        mod = sb("mod", [P, 48, 2])
        par = sb("par", [P, NLP])
        x = sb("x", [P, DC, T])
        h = sb("h", [P, DC, T])
        space = sb("space", [P, 20980])
        upper = ring[:, RING:MRING, :].rearrange("p s n -> p (s n)")
        gates = upper[:, 0:3 * DC * T].rearrange("p (c t) -> p c t", t=T)
        modrow = upper[:, 0:4 * W].rearrange("p (a n) -> p a n", n=W)
        conv = upper[:, 6144:7168].rearrange("p (c t) -> p c t", t=T)
        tanh_z = upper[:, 7168:7680]
        square = upper[:, 7680:8192]
        top = [0]

        def take(*shape):
            n = 1
            for s in shape:
                n *= s
            v = space[:, top[0]:top[0] + n]
            top[0] += n
            if len(shape) == 2:
                return v.rearrange("p (a b) -> p a b", b=shape[1])
            if len(shape) == 3:
                return v.rearrange("p (a b c) -> p a b c", b=shape[1], c=shape[2])
            return v

        ssum = take(8)
        var = take(8)
        rs = take(8)
        varx, rsx = square[:, 0:T], square[:, T:2 * T]
        stat = take(2, 8)
        mc = take(4, MQK)
        probs = take(2, 1024)
        turned = take(2, W)
        qn = turned
        rope = probs[:, 0, :].rearrange("p (a n) -> p a n", a=2)
        cT = probs[:, 1, 0:3 * T].rearrange("p (a n) -> p a n", a=3)
        phase0 = top[0]
        kpe = take(TT, MROPE)
        dqT = take(12, T)
        dkT = take(12, T)
        dv = take(TT, 3 * W)
        mqT = take(MHEADS, T)
        mkT = take(MHEADS, T)
        mv = take(TT, W)
        yB = take(4, T)
        yC = take(4, T)
        up = take(4, T + 2)
        mtmp = square
        assert top[0] <= 20980, top[0]
        top[0] = phase0
        bpar = take(NBP)
        bvarx = take(T)
        brsx = take(T)
        ctx_x = take(DC, T)
        assert top[0] <= phase0 + TT * MROPE + 24 * T
        bsquare = take(W)
        bqn = take(2, W)
        brope = take(2, W)
        hc = take(DC, T)
        top_qa = top[0]
        qaT = take(4, T)
        kaT = take(2, 2 * T)
        bmodrow = space[:, top_qa:top[0]].rearrange("p (a n) -> p a n", n=W)
        qbT = take(4, T)
        kbT = take(4, 2 * T)
        va = take(4, P)
        vb = take(4, W)
        mix = ctx_x
        gs = take(2, DC)
        kdup = take(2, 2 * HALF)
        lamt = take(2, HALF)
        lam = take(8)
        assert top[0] <= 20980, top[0]
        top[0] = phase0 + NBP + 2 * T
        hTM = take(TT, D)
        bin_sb = take(2 * D)
        xs = take(DC, P)
        onehot = take(2, SLOTS)
        sel = take(TT, P)
        selg = take(2, TT, P)
        spread0 = take(2, T)
        spread1 = take(2, T)
        glu_at = top[0]
        glu = take(2, W)
        tanh_g = take(2, W)
        lin = take(2, W)
        actT = take(2, W)
        ys = take(2, W)
        bout = take(D)
        logits = take(TT, NEXP)
        best = take(TT, 8)
        fill = take(TT, 8)
        ext = take(TT, 40)
        left = take(TT, 40)
        chosen = take(TT, NEXP)
        gate = take(TT, NEXP)
        gate_half = take(TT, NEXP)
        gateT = take(T)
        pos = take(TT, 40)
        gsum = take(TT, 4)
        cnt = take(NEXP)
        cand = take(2, 96)
        cand0 = take(96)
        jt = take(MAXJOBS, 96)
        jt2 = space[:, glu_at:glu_at + MAXJOBS * 96].rearrange("p (a b) -> p a b", b=96)
        jobe = take(MAXJOBS)
        jobs_ = take(MAXJOBS)
        posb = take(TT, 1)
        jobi = take(MAXJOBS + 1).bitcast(I32)
        assert top[0] <= 20980, top[0]

        def c_(name):
            a, n = CP[name]
            return cst[:, a:a + n]

        def l_(name, i=0, n=None):
            a, m = LP[name]
            return par[:, a + i:a + i + (n or m)]

        def b_(name, i=0, n=None):
            a, m = BP[name]
            return bpar[:, a + i:a + i + (n or m)]

        ident, ones = c_("ident"), c_("ones")

        bank = [ctx.enter_context(nc.psum_tensor(f"bank{i}", [P, W], F32)) for i in range(BANKS)]
        score = ctx.enter_context(nc.psum_tensor("score", [P, 2 * W], F32))
        flip = ctx.enter_context(nc.psum_tensor("flip", [P, W], F32))
        mixed = ctx.enter_context(nc.psum_tensor("mixed", [P, W], F32))

        loaded = sem("loaded")
        par_loaded = sem("par_loaded")
        uq_loaded = sem("uq_loaded")
        par_ready = sem("par_ready")
        landed = [sem(f"landed{i}") for i in range(RING)]
        squared = sem("squared")
        hready = sem("hready")
        unit_done = sem("unit_done")
        bank_free = [sem(f"bank_free{i}") for i in range(BANKS)]
        scored = sem("scored")
        score_free = sem("score_free")
        flipped = sem("flipped")
        flip_free = sem("flip_free")
        mixed_done = sem("mixed_done")
        mixed_free = sem("mixed_free")
        squares = sem("squares")
        squares_used = sem("squares_used")
        copied = sem("copied")
        var_ready = sem("var_ready")
        rs_ready = sem("rs_ready")
        rsx_ready = sem("rsx_ready")
        qn_ready = sem("qn_ready")
        z_tanh = sem("z_tanh")
        masked = sem("masked")
        exped = sem("exped")
        probs_ready = sem("probs_ready")
        conv_ready = sem("conv_ready")
        merged = sem("merged")
        chain = sem("chain")
        stored = sem("stored")
        asked = sem("asked")
        bpar_loaded = sem("bpar_loaded")
        ctanh = sem("ctanh")
        silu_ready = sem("silu_ready")
        bsquared = sem("bsquared")
        bvar = sem("bvar")
        broot = sem("broot")
        bh_ready = sem("bh_ready")
        bsquares = sem("bsquares")
        bvaru = sem("bvaru")
        brootu = sem("brootu")
        bqn_ready = sem("bqn_ready")
        lam_in = sem("lam_in")
        lam_exp = sem("lam_exp")
        bmasked = sem("bmasked")
        bexped = sem("bexped")
        bprobs = sem("bprobs")
        mix_ready = sem("mix_ready")
        logits_done = sem("logits_done")
        gate_in = sem("gate_in")
        gate_exp = sem("gate_exp")
        chosen_ready = sem("chosen_ready")
        pos_done = sem("pos_done")
        gateT_done = sem("gateT_done")
        gateT_ready = sem("gateT_ready")
        table_ready = sem("table_ready")
        mlanded = [sem(f"mlanded{i}") for i in range(MRING)]
        mused = sem("mused")
        sel_ready = sem("sel_ready")
        onehot_ready = sem("onehot_ready")
        selg_ready = sem("selg_ready")
        glu_done = sem("glu_done")
        glu_free = sem("glu_free")
        glu_in = sem("glu_in")
        glu_tanh = sem("glu_tanh")
        lin_done = sem("lin_done")
        lin_free = sem("lin_free")
        act_ready = sem("act_ready")
        eout_done = sem("eout_done")
        eout_free = sem("eout_free")
        scattered = sem("scattered")
        final_ready = sem("final_ready")
        block = ctx.enter_context(nc.Block())

        def freed(l, u):
            return l * PER_BANK + u // BANKS + 2

        def done(l, u):
            return (l + 1) * NU + u + 1

        def slot_left(l, n):
            last = max(u for u, x in enumerate(UNITS) if x[1] == (n - RING) % NT)
            return l * NU + last + 1 if n < RING else done(l, last)

        def first_flip(j):
            return NN + FIRST_ROUND[j]


        def bdone(u):
            return (LAYERS + 1) * NU + u + 1

        def bfreed(u):
            return LAYERS * PER_BANK + u // BANKS + 2

        SCORE0, FLIP0, MIXED0 = LAYERS * NS, LAYERS * NTR, LAYERS * NM
        S_JOBS, S_SUB = 2, 2 + NBJ
        S_FFN, S_FINAL = S_SUB + 1, S_SUB + 2
        F_TOK = len(BFLIPS)
        F_MOE = F_TOK + 4
        M_ADA, M_LOGITS, M_POS, M_GATE = NBJ, 1 + NBJ, 2 + NBJ, 3 + NBJ
        M_END = M_GATE + 1

        def score_left(s):
            s1 = s - S_JOBS
            alone = not 1 <= s1 < 2 * AHEADS
            return SCORE0 + s + (1 if alone else 0)

        def half_of(j):
            return j % 2 if BJOBS[j][0] == "gqa" else 0

        def block_sync(sp):
            sp.wait_ge(mixed_free, MIXED0 + 1)
            sp.dma_start(bpar, block_params).then_inc(bpar_loaded, 16)
            sp.dma_start(ctx_x, ctxT).then_inc(bpar_loaded, 16)
            sources = [(w_qkv, 0, W), (w_qkv, W, 256), (w_qkv, 768, W), (w_qkv, 1280, W), (w_qkv, 1792, W)]
            sources += [(w_ada, (LAYERS * 4 + n) * W, W) for n in range(4)]
            sources += [(w_o2, 0, W), (w_o2, W, W)]
            for n, (src, a, width) in enumerate(sources):
                if n >= RING:
                    last = max(u for u, x_ in enumerate(BUNITS) if x_[1] == n - RING)
                    sp.wait_ge(unit_done, bdone(last))
                else:
                    last = max(u for u, x_ in enumerate(UNITS) if x_[1] == NT - RING + n)
                    sp.wait_ge(unit_done, done(LAYERS - 1, last))
                sp.dma_start(ring[:, n % RING, :].rearrange("p (c n) -> p c n", c=DC)[:, :, 0:width],
                             columns(src, a, width)).then_inc(landed[n % RING], 16)

            def expert_tile(we, wo, j):
                rows_ = slice((j % 2) * W, (j % 2 + 1) * W)
                src = wo[rows_, :] if j >= 4 else we[rows_, (j // 2) * D:(j // 2 + 1) * D]
                sp.dma_start(ring[:, j, :].rearrange("p (c n) -> p c n", c=4),
                             src.rearrange("(c p) n -> p c n", p=P)).then_inc(mlanded[j], 16)

            def expert(e, m):
                we = e_in[bass.ds(e, 1)].rearrange("a k n -> (a k) n")
                wo = e_out[bass.ds(e, 1)].rearrange("a k n -> (a k) n")
                for j in range(MRING):
                    sp.wait_ge(mused, m * MRING + j + 1)
                    sp.sem_inc(asked, 1)
                    expert_tile(we, wo, j)

            assert (len(sources) - 2) % RING == 1
            for j in (4, 5, 3, 0, 1, 2):
                if j in (0, 3):
                    sp.wait_ge(unit_done, bdone(BQKV - 1))
                elif j in (1, 2):
                    sp.wait_ge(unit_done, bdone(NBU - 1))
                expert_tile(e_in[0], e_out[0], j)
            sp.wait_ge(mix_ready, 1)
            sp.dma_start(bout[0:NEXP, :], eb_out).then_inc(bpar_loaded, 16)
            sp.wait_ge(table_ready, 1)
            sp.dma_start(bin_sb[0:NEXP, :], eb_in).then_inc(bpar_loaded, 16)
            with sp.Fori(1, NEXP) as e:
                expert(e, e)
            sp.wait_ge(table_ready, 2)
            n_jobs = sp.value_load(jobi[0:1, MAXJOBS:MAXJOBS + 1], min_val=0, max_val=MAXJOBS)
            with sp.If(n_jobs > 0):
                with sp.Fori(0, n_jobs) as i:
                    e = sp.value_load(jobi[0:1, bass.ds(i, 1)], min_val=0, max_val=NEXP - 1)
                    expert(e, i + NEXP)
            sp.wait_ge(final_ready, 1)
            sp.dma_start(out, h[:]).then_inc(stored, 16)
            sp.wait_ge(stored, 16)

        def ada_rows(pe, b, w8, parts):
            for k in parts:
                for g in range(4):
                    c = 4 * k + g
                    ins = pe.matmul(b[32 * g:32 * g + 32, :], silu[:, c, :], w8[:, c, :], start=k == 0, stop=k == 1,
                                    tile_position=(0, 32 * g))
            return ins

        def pick(pe, rows_, at):
            for m in range(4):
                ins = pe.matmul(mixed[:, at + 2 * m:at + 2 * m + 2], rows_[:, m * P:(m + 1) * P], c_("pick"),
                                start=True, stop=True)
            return ins

        def block_tensor(pe):
            pe.sem_inc(mused, MRING)

            def start(u):
                tl = BUNITS[u][1]
                pe.wait_ge(landed[tl % RING], LAYERS * 16 * NT // RING + 16 * (tl // RING + 1))
                pe.wait_ge(bank_free[u % BANKS], bfreed(u) - 1)

            def place(u):
                return bank[u % BANKS], ring[:, BUNITS[u][1] % RING, :].rearrange("p (c n) -> p c n", c=DC)

            for s, src in ((0, h[:]), (1, hc)):
                pe.wait_ge(bsquared, s + 1)
                pe.wait_ge(score_free, score_left(s))
                for c in range(DC):
                    ins = pe.matmul(score[:, 0:T], ones, src[:, c, :], start=c == 0, stop=c == DC - 1)
                ins.then_inc(scored, 1)

            def project(u, parts=(0, 1)):
                kind, _, who = BUNITS[u]
                if 0 in parts:
                    start(u)
                b, w8 = place(u)
                if kind == "ada":
                    ins = ada_rows(pe, b, w8, parts)
                    if 1 in parts:
                        ins.then_inc(unit_done, 1)
                    return
                t = who[0]
                n = 256 if kind == "ka" else W
                if kind in ("qa", "qb"):
                    src, tt = h, t
                else:
                    src, tt = (hc, t) if t < TT else (h, t - TT)
                for c in range(4 * parts[0], 4 * parts[-1] + 4):
                    ins = pe.matmul(b[:, 0:n], src[:, c, tt * P:(tt + 1) * P], w8[:, c, 0:n], start=c == 0,
                                    stop=c == DC - 1)
                if 1 in parts:
                    ins.then_inc(unit_done, 1)

            def turn(u):
                r = BTURNED.index(u)
                pe.wait_ge(bqn_ready, r + 1)
                pe.wait_ge(flip_free, FLIP0 + BFLIPS.index(("turn", u)) + 1)
                for i in range(2 if BUNITS[u][0] == "ka" else 4):
                    ins = pe.transpose(flip[:, i * P:(i + 1) * P], bqn[:, r % 2, i * P:(i + 1) * P], ident)
                ins.then_inc(flipped, 1)

            for u in range(BFIRST + LAG):
                if u < BFIRST:
                    pe.wait_ge(bh_ready, 1 if u < 4 else 2)
                    project(u)
                if u >= LAG:
                    turn(u - LAG)
            pe.wait_ge(flip_free, FLIP0 + BFIRST + 1)

            bhalves = [0]

            def bfill():
                u, part = BFIRST + bhalves[0] // 2, bhalves[0] % 2
                bhalves[0] += 1
                project(u, (part,))

            def scores(j):
                kind, hd, t = BJOBS[j]
                pe.wait_ge(score_free, score_left(S_JOBS + j))
                cols = slice(t * P, (t + 1) * P)
                if kind == "gqa":
                    lo = HALF * (hd % 2)
                    o = score[:, W * half_of(j):W * half_of(j) + W]
                    ins = pe.matmul(o, qaT[lo:lo + HALF, hd // 2, cols], kaT[lo:lo + HALF, hd // 4, :],
                                    start=True, stop=True)
                else:
                    for cp in range(2):
                        lo = HALF * cp
                        ins = pe.matmul(score[:, W * cp:W * cp + W], qbT[lo:lo + HALF, hd, cols],
                                        kbT[lo:lo + HALF, hd, :], start=True, stop=True)
                ins.then_inc(scored, 1)

            def values(j):
                kind, hd, t = BJOBS[j]
                pe.wait_ge(bprobs, j + 1)
                f = FLIP0 + BFLIPS.index(("job", j))
                pe.wait_ge(flip_free, f + 1)
                for i in range(4):
                    ins = pe.transpose(flip[:, i * P:(i + 1) * P], probs[:, j % 2, i * P:(i + 1) * P], ident)
                ins.then_inc(flipped, 1)
                bfill()
                pe.wait_ge(flip_free, f + 2)
                pe.wait_ge(mixed_free, MIXED0 + j + 1)
                for i in range(4):
                    pt = turned[:, j % 2, i * P:(i + 1) * P]
                    if kind == "gqa":
                        lo = HALF * (hd % 2)
                        kv = hd // 4
                        ins = pe.matmul(mixed[lo:lo + HALF, 0:P], va[:, i, kv * HALF:(kv + 1) * HALF], pt,
                                        start=i == 0, stop=i == 3)
                    else:
                        ins = pe.matmul(mixed[:, 0:P], vb[:, i, hd * P:(hd + 1) * P], pt, start=i == 0, stop=i == 3)
                ins.then_inc(mixed_done, 1)

            for u in range(BFIRST):
                pe.wait_ge(bank_free[u % BANKS], bfreed(u))
            for j in range(NBJ + 1):
                if j < NBJ:
                    if j == 2 * AHEADS:
                        last = max(f for f, x_ in enumerate(BFLIPS) if x_[0] == "turn")
                        pe.wait_ge(flip_free, FLIP0 + last + 2)
                    scores(j)
                if j == 2 * AHEADS + 1:
                    for u in range(BADA - 4, BADA):
                        pe.wait_ge(bank_free[u % BANKS], bfreed(u))
                if j > 0:
                    values(j - 1)
                while bhalves[0] < sum(BHALVES[:j + 1]):
                    bfill()
                for u in BDONE_IN[j - 1] if j else ():
                    if u in BTURNED:
                        turn(u)
            pe.wait_ge(bsquared, 3)
            pe.wait_ge(score_free, score_left(S_SUB))
            for i in range(2):
                ins = pe.matmul(score[:, i * W:(i + 1) * W], ones, hc[:, 2 * i:2 * i + 2, :].rearrange("p a t -> p (a t)"),
                                start=True, stop=True)
            ins.then_inc(scored, 1)
            pe.wait_ge(mixed_free, MIXED0 + M_ADA + 1)
            for n in range(4):
                pe.wait_ge(bank_free[(BADA + n) % BANKS], bfreed(BADA + n))
                ins = pick(pe, bmodrow[:, n, :], 8 * n)
            ins.then_inc(mixed_done, 1)
            for part in range(2):
                if part:
                    pe.wait_ge(mix_ready, 1)
                for u in range(BQKV, NBU):
                    if part == 0:
                        start(u)
                    b, w8 = place(u)
                    for i in range(2):
                        m = (2 * BUNITS[u][2][1] + i) * P
                        for c in range(4 * part, 4 * part + 4):
                            ins = pe.matmul(b[:, i * T:(i + 1) * T], w8[:, c, m:m + P], mix[:, c, :],
                                            start=c == 0 and i == 0, stop=c == DC - 1, skip_group_check=True)
                    if part:
                        ins.then_inc(unit_done, 1)

            pe.wait_ge(bsquared, 4)
            pe.wait_ge(score_free, score_left(S_FFN))
            for c in range(DC):
                ins = pe.matmul(score[:, 0:T], ones, h[:, c, :], start=c == 0, stop=c == DC - 1)
            ins.then_inc(scored, 1)
            pe.wait_ge(bh_ready, 3)
            pe.wait_ge(mixed_free, MIXED0 + M_LOGITS + 1)
            wr = b_("w_router").rearrange("p (c e) -> p c e", c=DC)
            for t in range(TT):
                for c in range(DC):
                    ins = pe.matmul(mixed[:, t * NEXP:(t + 1) * NEXP], h[:, c, t * P:(t + 1) * P], wr[:, c, :],
                                    start=c == 0, stop=c == DC - 1)
            ins.then_inc(mixed_done, 1)
            for r in range(4):
                t, q = r // 2, r % 2
                pe.wait_ge(flip_free, FLIP0 + F_TOK + r + 1)
                for i in range(4):
                    ins = pe.transpose(flip[:, i * P:(i + 1) * P], h[:, 4 * q + i, t * P:(t + 1) * P], ident)
                ins.then_inc(flipped, 1)
            pe.wait_ge(chosen_ready, 1)
            pe.wait_ge(mixed_free, MIXED0 + M_POS + 1)
            pe.matmul(mixed[:, 0:32], c_("before"), chosen[:, 0, :], start=True, stop=True)
            pe.matmul(mixed[:, 32:64], c_("before"), chosen[:, 1, :], start=True, stop=False)
            pe.matmul(mixed[:, 32:64], ones, chosen[:, 0, :], start=False, stop=True)
            pe.matmul(mixed[:, 64:96], ones, chosen[:, 0, :], start=True, stop=False)
            pe.matmul(mixed[:, 64:96], ones, chosen[:, 1, :], start=False, stop=True).then_inc(mixed_done, 1)
            pe.wait_ge(gate_in, 2)
            pe.wait_ge(mixed_free, MIXED0 + M_GATE + 1)
            for t in range(TT):
                ins = pe.matmul(mixed[0:NEXP, t * P:(t + 1) * P], gate[:, t, :], ident, start=True, stop=True)
            ins.then_inc(mixed_done, 1)
            pe.wait_ge(mixed_free, MIXED0 + M_END + 1)
            pe.wait_ge(bpar_loaded, 64)
            for b in range(BANKS):
                pe.wait_ge(bank_free[b], bfreed(NBU - BANKS + b))
            for c in range(DC):
                pe.matmul(bank[c // 2][:, (c % 2) * T:(c % 2 + 1) * T], bout[0:NEXP, c * P:(c + 1) * P],
                          gateT[0:NEXP, :], start=c % 2 == 0, stop=False, skip_group_check=True)

            def gather(first_sel, first_flip_):
                pe.wait_ge(sel_ready, first_sel)
                for q in range(2):
                    pe.wait_ge(flip_free, first_flip_ + q)
                    for i in range(4):
                        c = 4 * q + i
                        for t in range(TT):
                            ins = pe.matmul(flip[:, i * P:(i + 1) * P], hTM[:, t, c * P:(c + 1) * P], sel[:, t, :],
                                            start=t == 0, stop=t == TT - 1)
                    ins.then_inc(flipped, 1)

            def expert_in(m, which, hh):
                pe.wait_ge((glu_free, lin_free)[which], m + 1)
                for k in range(DC):
                    j = 2 * which + k // 4
                    if k % 4 == 0:
                        pe.wait_ge(mlanded[j], m * 16 + 16)
                    wk = ring[:, j, (k % 4) * D:(k % 4 + 1) * D]
                    for blk in range(2):
                        ins = pe.matmul(score[HALF * blk:HALF * blk + HALF, which * W:(which + 1) * W],
                                        xs[:, k, HALF * hh:HALF * hh + HALF], wk[:, blk * W:(blk + 1) * W],
                                        start=k == 0, stop=False)
                    if k % 4 == 3:
                        ins.then_inc(mused, 1)
                for blk in range(2):
                    ins = pe.matmul(score[HALF * blk:HALF * blk + HALF, which * W:(which + 1) * W],
                                    onehot[:, hh, :], bin_sb[:, which * D + blk * W:which * D + (blk + 1) * W],
                                    start=False, stop=True)
                ins.then_inc((glu_done, lin_done)[which], 1)

            def expert_out(m, hh):
                pe.wait_ge(eout_free, m + 1)
                for k in range(DC):
                    j = 4 + k // 4
                    if k % 4 == 0:
                        pe.wait_ge(mlanded[j], m * 16 + 16)
                    wk = ring[:, j, (k % 4) * D:(k % 4 + 1) * D]
                    a0 = (k % 4) * P + HALF * (k // 4)
                    for blk in range(2):
                        ins = pe.matmul(mixed[HALF * blk:HALF * blk + HALF, :], actT[:, hh, a0:a0 + HALF],
                                        wk[:, blk * W:(blk + 1) * W], start=k == 0, stop=k == DC - 1)
                    if k == 3:
                        ins.then_inc(mused, 1)
                ins.then_inc(eout_done, 1)

            def turn_act(m, hh, f):
                pe.wait_ge(act_ready, m + 1)
                pe.wait_ge(flip_free, f)
                for i in range(4):
                    ins = pe.transpose(flip[:, i * P:(i + 1) * P], lin[:, hh, i * P:(i + 1) * P], ident)
                ins.then_inc(flipped, 1)
                pe.wait_ge(flip_free, f + 1)

            def turn_sel(hh, f):
                pe.wait_ge(flip_free, f)
                for t in range(TT):
                    ins = pe.transpose(flip[:, t * P:(t + 1) * P], selg[:, hh, t, :], ident)
                ins.then_inc(flipped, 1)

            def scatter(hh):
                for c in range(DC):
                    sp_ = (spread0, spread1)[c // 4]
                    ins = pe.matmul(bank[c // 2][:, (c % 2) * T:(c % 2 + 1) * T],
                                    ys[:, hh, (c % 4) * P:(c % 4 + 1) * P], sp_[:, hh, :], start=False, stop=False,
                                    skip_group_check=True)
                return ins

            pe.wait_ge(eout_free, 1)
            gather(1, FLIP0 + F_MOE + 1)
            pe.wait_ge(flip_free, FLIP0 + F_MOE + 3)
            base_f = FLIP0 + F_MOE + 2
            with pe.Fori(0, PAIRS) as i:
                pe.wait_ge(onehot_ready, i + 1)
                expert_in(i * 2, 0, 0)
                expert_in(i * 2, 1, 0)
                pe.wait_ge(eout_free, i * 2 + 1)
                scatter(1)
                pe.wait_ge(selg_ready, i + 1)
                turn_sel(0, i * 6 + base_f + 1)
                turn_sel(1, i * 6 + base_f + 2)
                turn_act(i * 2, 0, i * 6 + base_f + 3)
                expert_out(i * 2, 0)
                pe.wait_ge(eout_done, i * 2 + 1)
                pe.sem_inc(mused, 1)
                expert_in(i * 2 + 1, 0, 1)
                expert_in(i * 2 + 1, 1, 1)
                gather(i + 2, i * 6 + base_f + 4)
                pe.wait_ge(eout_free, i * 2 + 2)
                scatter(0)
                turn_act(i * 2 + 1, 1, i * 6 + base_f + 6)
                expert_out(i * 2 + 1, 1)
                pe.wait_ge(eout_done, i * 2 + 2)
                pe.sem_inc(mused, 1)
            pe.wait_ge(eout_free, NEXP + 1)
            scatter(1).then_inc(scattered, 1)
            base_f2 = base_f + 6 * PAIRS
            n_jobs = pe.value_load(jobi[0:1, MAXJOBS:MAXJOBS + 1], min_val=0, max_val=MAXJOBS)
            with pe.If(n_jobs > 0):
                with pe.Fori(0, n_jobs) as i:
                    pe.wait_ge(selg_ready, i + PAIRS + 1)
                    gather(i + PAIRS + 2, i * 4 + base_f2 + 1)
                    turn_sel(0, i * 4 + base_f2 + 3)
                    pe.wait_ge(flip_free, i * 4 + base_f2 + 4)
                    pe.wait_ge(onehot_ready, i + PAIRS + 1)
                    expert_in(i + NEXP, 0, 0)
                    expert_in(i + NEXP, 1, 0)
                    turn_act(i + NEXP, 0, i * 4 + base_f2 + 4)
                    expert_out(i + NEXP, 0)
                    pe.wait_ge(eout_free, i + NEXP + 2)
                    pe.sem_inc(mused, 1)
                    scatter(0).then_inc(scattered, 1)
            pe.wait_ge(bsquared, 5)
            for c in range(DC):
                ins = pe.matmul(score[:, 0:T], ones, h[:, c, :], start=c == 0, stop=c == DC - 1)
            ins.then_inc(scored, 1)

        def block_scalar(act):
            act.wait_ge(bank_free[(NU - 1) % BANKS], freed(LAYERS - 1, NU - 1))
            act.activation(h[:], x[:], ACT.Square).then_inc(bsquared, 1)
            act.wait_ge(bpar_loaded, 32)
            act.activation(hc, ctx_x, ACT.Square).then_inc(bsquared, 1)
            act.wait_ge(lam_in, 1)
            act.activation(lam[:, 2:4], lam[:, 0:2], ACT.Exp).then_inc(lam_exp, 1)

            def stream_root(n, s):
                act.wait_ge(bvar, n)
                act.activation(brsx, bvarx, ACT.Sqrt).then_inc(broot, 1)

            stream_root(1, 0)
            stream_root(2, 1)
            def evacuate_block(u):
                kind, _, who = BUNITS[u]
                b = bank[u % BANKS]
                if kind in ("qa", "ka"):
                    n = BNORMED.index(u)
                    act.wait_ge(unit_done, bdone(u))
                    if n:
                        act.wait_ge(bvaru, n)
                    w = W if kind == "qa" else P
                    act.activation(bsquare[:, 0:w], b[:, 0:w], ACT.Square).then_inc(bsquares, 1)
                    act.wait_ge(bvaru, n + 1)
                    act.activation(rs, var, ACT.Sqrt).then_inc(brootu, 1)
                elif kind == "vb":
                    act.wait_ge(unit_done, bdone(u))
                    act.activation(vb[:, who[0], :], b[:, :], ACT.Copy).then_inc(bank_free[u % BANKS], 1)
                elif kind == "ada":
                    act.wait_ge(unit_done, bdone(u))
                    act.activation(bmodrow[:, who[0], :], b[:, :], ACT.Copy).then_inc(bank_free[u % BANKS], 1)

            def unturn(u):
                kind, _, who = BUNITS[u]
                t = who[0]
                act.wait_ge(flipped, FLIP0 + BFLIPS.index(("turn", u)) + 1)
                v = flip[:, :].rearrange("p (a t) -> p a t", t=P)
                n = 2 if kind == "ka" else 4
                dst = dict(qa=qaT, ka=kaT, qb=qbT, kb=kbT)[kind][:, 0:n, t * P:(t + 1) * P]
                act.activation(dst, v[:, 0:n, :], ACT.Copy,
                               scale=HALF ** -0.5 if kind in ("qa", "qb") else 1.0).then_inc(flip_free, 1)

            for u in range(BFIRST + LAG):
                if u < BFIRST:
                    evacuate_block(u)
                if u >= LAG:
                    unturn(u - LAG)
            for j in range(NBJ + 1):
                if j < NBJ:
                    kind = BJOBS[j][0]
                    act.wait_ge(bmasked, j + 1)
                    if j >= 2:
                        act.wait_ge(flipped, FLIP0 + BFLIPS.index(("job", j - 2)) + 1)
                    st = stat[:, j % 2, :]
                    a = W * half_of(j)
                    ins = act.activation(probs[:, j % 2, 0:W], score[:, a:a + W], ACT.Exp, bias=st[:, 2:3],
                                         accum_out=st[:, 4:5])
                    if kind == "diff":
                        ins = act.activation(probs[:, j % 2, W:2 * W], score[:, W:2 * W], ACT.Exp, bias=st[:, 3:4],
                                             accum_out=st[:, 5:6])
                    ins.then_inc(score_free, 1)
                if j > 0:
                    act.wait_ge(flipped, FLIP0 + BFLIPS.index(("job", j - 1)) + 1)
                    if j >= 3:
                        act.wait_ge(mixed_done, MIXED0 + j - 2)
                    act.activation(turned[:, (j - 1) % 2, :], flip[:, :], ACT.Copy).then_inc(flip_free, 1)
                for u in BDONE_IN[j]:
                    evacuate_block(u)
                for u in BDONE_IN[j - 1] if j else ():
                    if u in BTURNED:
                        unturn(u)
            act.wait_ge(mixed_free, MIXED0 + NBJ + 1)
            act.activation(hc[:, 0:4, :], mix[:, 4:8, :], ACT.Square).then_inc(bsquared, 1)
            act.wait_ge(bvar, 3)
            act.activation(hc[:, 0:4, :], hc[:, 4:8, :], ACT.Sqrt).then_inc(broot, 1)
            act.wait_ge(bank_free[(NBU - 1) % BANKS], bfreed(NBU - 1))
            act.activation(h[:], x[:], ACT.Square).then_inc(bsquared, 1)
            stream_root(4, S_FFN)
            for r in range(4):
                t, q = r // 2, r % 2
                act.wait_ge(flipped, FLIP0 + F_TOK + r + 1)
                act.activation(hTM[:, t, q * W:(q + 1) * W], flip[:, :], ACT.Copy).then_inc(flip_free, 1)
            act.wait_ge(gate_in, 1)
            for t in range(TT):
                ins = act.activation(gate[:, t, :], ext[:, t, 0:NEXP], ACT.Exp, bias=gsum[:, t, 0:1])
            ins.then_inc(gate_exp, 1)

            def gathered(f):
                for q in range(2):
                    act.wait_ge(flipped, f + q)
                    act.activation(xs[:, 4 * q:4 * q + 4, :], flip[:, :].rearrange("p (a t) -> p a t", t=P),
                                   ACT.Copy).then_inc(flip_free, 1)

            def sel_turned(hh, f):
                act.wait_ge(flipped, f)
                act.activation(spread0[0:HALF, hh, :], flip[0:HALF, 0:T], ACT.Copy)
                act.activation(spread1[HALF:P, hh, :], flip[HALF:P, 0:T], ACT.Copy).then_inc(flip_free, 1)

            def tanh(m, hh):
                act.wait_ge(glu_free, m + 2)
                act.activation(tanh_g[:, hh, :], glu[:, hh, :], ACT.Tanh, scale=GLU_ALPHA / 2).then_inc(glu_tanh, 1)

            def act_turned(hh, f):
                act.wait_ge(flipped, f)
                act.activation(actT[:, hh, :], flip[:, :], ACT.Copy).then_inc(flip_free, 1)

            base_f = FLIP0 + F_MOE + 2
            gathered(FLIP0 + F_MOE + 1)
            with act.Fori(0, PAIRS) as i:
                tanh(i * 2, 0)
                sel_turned(0, i * 6 + base_f + 1)
                sel_turned(1, i * 6 + base_f + 2)
                act_turned(0, i * 6 + base_f + 3)
                tanh(i * 2 + 1, 1)
                gathered(i * 6 + base_f + 4)
                act_turned(1, i * 6 + base_f + 6)
            base_f2 = base_f + 6 * PAIRS
            n_jobs = act.value_load(jobi[0:1, MAXJOBS:MAXJOBS + 1], min_val=0, max_val=MAXJOBS)
            with act.If(n_jobs > 0):
                with act.Fori(0, n_jobs) as i:
                    gathered(i * 4 + base_f2 + 1)
                    sel_turned(0, i * 4 + base_f2 + 3)
                    tanh(i + NEXP, 0)
                    act_turned(0, i * 4 + base_f2 + 4)
            act.wait_ge(bh_ready, 4)
            act.activation(h[:], x[:], ACT.Square).then_inc(bsquared, 1)
            stream_root(5, S_FINAL)

        def block_vector(dve, link, steps, base):
            def to(shape, v, axis=1):
                return v.unsqueeze(axis).broadcast_to(shape)

            dve.wait_ge(bpar_loaded, 32)
            lv = b_("lam").rearrange("p (a n) -> p a n", a=4)
            for k in range(2):
                link(dve.tensor_tensor(lamt[:, k, :], lv[:, 2 * k, :], lv[:, 2 * k + 1, :], ALU.mult))
            dve.tensor_reduce(lam[:, 0:2], lamt, AX.X, ALU.add).then_inc(lam_in, 1)
            DONE_ADA = LAYERS * 4 * ADAS
            link(dve.tensor_tensor(mod[:, 0:DONE_ADA, :], mod[:, 0:DONE_ADA, :],
                                   to([P, DONE_ADA, 2], b_("b_ada", 0, DONE_ADA), 2), ALU.add))
            SH1, SC1, GT1, SH2, SC2, GT2 = (DC * i for i in range(6))

            def modulated(dst, src, n, gains, shift, scale_at, which, s):
                link(dve.scalar_tensor_tensor(out=gs[:, 0, :], in0=mod[:, scale_at:scale_at + DC, which], scalar=1.0,
                                              in1=gains, op0=ALU.add, op1=ALU.mult))
                dve.wait_ge(scored, SCORE0 + s + 1)
                dve.tensor_scalar(bvarx, score[:, 0:T], 1.0 / D, EPS, ALU.mult, ALU.add).then_inc(score_free, 1)
                dve.wait_ge(score_free, SCORE0 + s + 2)
                dve.sem_inc(bvar, 1)
                dve.wait_ge(broot, n)
                link(dve.reciprocal(brsx, brsx))
                for c in range(DC):
                    ins = dve.scalar_tensor_tensor(out=dst[:, c, :], in0=src[:, c, :], scalar=gs[:, 0, c:c + 1],
                                                   in1=brsx, op0=ALU.mult, op1=ALU.mult)
                link(ins)
                for c in range(DC):
                    ins = dve.tensor_scalar(dst[:, c, :], dst[:, c, :],
                                            mod[:, shift + c:shift + c + 1, which:which + 1].rearrange("p a b -> p (a b)"),
                                            None, ALU.add)
                return ins

            modulated(h, x, 1, b_("g_attn"), SH1, SC1, 0, 0).then_inc(bh_ready, 1)
            modulated(hc, ctx_x, 2, b_("g_attn"), SH1, SC1, 1, 1).then_inc(bh_ready, 1)
            dve.wait_ge(lam_exp, 1)
            link(dve.tensor_tensor(lam[:, 4:5], lam[:, 3:4], lam[:, 2:3], ALU.subtract))
            link(dve.tensor_scalar(lam[:, 4:5], lam[:, 4:5], -LAMBDA_INIT, None, ALU.add))
            link(dve.tensor_scalar(b_("subln"), b_("subln"), 1.0 - LAMBDA_INIT, None, ALU.mult))

            def rotate(v, t):
                a = v.shape[1] // 2
                for ax in range(2):
                    def tab(name, hf):
                        at = t * 64 + ax * 32 + hf * 16
                        return c_(name)[:, at:at + 16].unsqueeze(1).broadcast_to([P, a, 16])
                    for hf in range(2):
                        s_ = v[:, ax::2, hf, :]
                        o_ = v[:, ax::2, 1 - hf, :]
                        r0 = brope[:, 0, :].rearrange("p (b n) -> p b n", n=16)[:, (2 * ax + hf) * 8:(2 * ax + hf) * 8 + a, :]
                        r1 = brope[:, 1, :].rearrange("p (b n) -> p b n", n=16)[:, (2 * ax + hf) * 8:(2 * ax + hf) * 8 + a, :]
                        dve.tensor_tensor(r0, s_, tab("cosx", hf), ALU.mult)
                        link(dve.tensor_tensor(r1, o_, tab("sinx", hf), ALU.mult))
                for ax in range(2):
                    for hf in range(2):
                        r0 = brope[:, 0, :].rearrange("p (b n) -> p b n", n=16)[:, (2 * ax + hf) * 8:(2 * ax + hf) * 8 + a, :]
                        r1 = brope[:, 1, :].rearrange("p (b n) -> p b n", n=16)[:, (2 * ax + hf) * 8:(2 * ax + hf) * 8 + a, :]
                        ins = dve.tensor_tensor(v[:, ax::2, hf, :], r0, r1, ALU.add)
                link(ins)

            def evacuate_block(u):
                kind, _, who = BUNITS[u]
                b = bank[u % BANKS]
                t = who[0]
                if kind in ("vb", "ada"):
                    return
                r = BTURNED.index(u)
                q = bqn[:, r % 2, :]
                xt = t if kind in ("qa", "qb") else t - TT
                if r >= 2:
                    dve.wait_ge(flipped, FLIP0 + BFLIPS.index(("turn", BTURNED[r - 2])) + 1)
                if kind in ("qa", "ka"):
                    n = BNORMED.index(u)
                    a = 8 if kind == "qa" else 2
                    dve.wait_ge(bsquares, n + 1)
                    link(dve.tensor_reduce(ssum[:, 0:a], bsquare[:, 0:a * HALF].rearrange("p (a b) -> p a b", b=HALF), AX.X,
                                           ALU.add))
                    dve.tensor_scalar(var[:, 0:a], ssum[:, 0:a], 1.0 / HALF, EPS, ALU.mult, ALU.add).then_inc(bvaru, 1)
                    dve.wait_ge(brootu, n + 1)
                    link(dve.reciprocal(rs, rs))
                    dst = q if kind == "qa" else kdup.rearrange("p a b -> p (a b)")[:, 0:P]
                    dv_ = dst.rearrange("p (a b) -> p a b", b=HALF)
                    if kind == "ka":
                        link(dve.tensor_copy(va[:, t, :], b[:, P:2 * P]))
                    dve.tensor_tensor(dv_, b[:, 0:a * HALF].rearrange("p (a b) -> p a b", b=HALF),
                                      to([P, a, HALF], rs[:, 0:a], 2), ALU.mult).then_inc(bank_free[u % BANKS], 1)
                    dve.wait_ge(bank_free[u % BANKS], bfreed(u))
                    g = b_("gqa_q" if kind == "qa" else "gqa_k")
                    link(dve.tensor_tensor(dv_, dv_, to([P, a, HALF], g), ALU.mult))
                else:
                    dst = q
                    dve.wait_ge(unit_done, bdone(u))
                    dve.tensor_copy(q, b[:, :]).then_inc(bank_free[u % BANKS], 1)
                    dve.wait_ge(bank_free[u % BANKS], bfreed(u))
                if xt >= 0:
                    rotate(dst.rearrange("p (a two n) -> p a two n", two=2, n=16), xt)
                if kind == "ka":
                    kd = kdup.rearrange("p a b -> p (a b)")[:, 0:P].rearrange("p (a b) -> p a b", b=HALF)
                    for cp in range(2):
                        ins = dve.tensor_copy(q[:, 0:256].rearrange("p (a two b) -> p a two b", two=2, b=HALF)[:, :, cp, :],
                                              kd)
                    link(ins)
                dve.sem_inc(bqn_ready, 1)

            for u in range(BFIRST):
                evacuate_block(u)
            for j in range(NBJ + 1):
                if j < NBJ:
                    kind, hd, t = BJOBS[j]
                    st = stat[:, j % 2, :]
                    dve.wait_ge(scored, SCORE0 + S_JOBS + j + 1)
                    a = W * half_of(j)
                    if kind == "gqa":
                        link(dve.tensor_reduce(st[:, 0:1], score[:, a:a + W], AX.X, ALU.max))
                        dve.tensor_scalar(st[:, 2:3], st[:, 0:1], -1.0, None, ALU.mult).then_inc(bmasked, 1)
                    else:
                        link(dve.tensor_reduce(st[:, 0:2], score[:, :].rearrange("p (a n) -> p a n", a=2), AX.X, ALU.max))
                        dve.tensor_scalar(st[:, 2:4], st[:, 0:2], -1.0, None, ALU.mult).then_inc(bmasked, 1)
                for u in BDONE_IN[j - 1] if j else ():
                    evacuate_block(u)
                if j < NBJ:
                    kind, hd, t = BJOBS[j]
                    pr, st = probs[:, j % 2, :], stat[:, j % 2, :]
                    dve.wait_ge(score_free, SCORE0 + S_JOBS + j + 2)
                    if kind == "gqa":
                        link(dve.reciprocal(st[:, 6:7], st[:, 4:5]))
                        dve.tensor_scalar(pr[:, 0:W], pr[:, 0:W], st[:, 6:7], None, ALU.mult).then_inc(bprobs, 1)
                    else:
                        link(dve.reciprocal(st[:, 6:8], st[:, 4:6]))
                        link(dve.tensor_tensor(st[:, 7:8], st[:, 7:8], lam[:, 4:5], ALU.mult))
                        link(dve.tensor_scalar(pr[:, 0:W], pr[:, 0:W], st[:, 6:7], None, ALU.mult))
                        dve.scalar_tensor_tensor(out=pr[:, 0:W], in0=pr[:, W:2 * W], scalar=st[:, 7:8], in1=pr[:, 0:W],
                                                 op0=ALU.mult, op1=ALU.add).then_inc(bprobs, 1)
                if j > 0:
                    kind, hd, t = BJOBS[j - 1]
                    lo = HALF * (hd % 2)
                    dve.wait_ge(mixed_done, MIXED0 + j)
                    cols = slice(t * P, (t + 1) * P)
                    if kind == "gqa":
                        dve.tensor_copy(mix[lo:lo + HALF, hd // 2, cols], mixed[lo:lo + HALF, 0:P]).then_inc(mixed_free, 1)
                    else:
                        dve.tensor_copy(mix[:, 4 + hd, cols], mixed[:, 0:P]).then_inc(mixed_free, 1)
            dve.wait_ge(scored, SCORE0 + S_SUB + 1)
            dve.tensor_scalar(hc[:, 4:8, :].rearrange("p a t -> p (a t)"), score[:, :], 1.0 / P, EPS, ALU.mult,
                              ALU.add).then_inc(score_free, 1)
            dve.wait_ge(score_free, SCORE0 + S_SUB + 2)
            dve.sem_inc(bvar, 1)
            dve.wait_ge(broot, 3)
            link(dve.reciprocal(hc[:, 0:4, :], hc[:, 0:4, :]))
            m4 = mix[:, 4:8, :].rearrange("p a t -> p (a t)")
            dve.scalar_tensor_tensor(out=m4, in0=m4, scalar=b_("subln"), in1=hc[:, 0:4, :].rearrange("p a t -> p (a t)"),
                                     op0=ALU.mult, op1=ALU.mult).then_inc(mix_ready, 1)
            dve.wait_ge(mixed_done, MIXED0 + M_ADA + 1)
            dve.tensor_tensor(mod[:, DONE_ADA:48, :], mixed[:, 0:32].rearrange("p (c b) -> p c b", b=2),
                              to([P, 16, 2], b_("b_ada", DONE_ADA, 16), 2), ALU.add).then_inc(mixed_free, 1)
            dve.wait_ge(mixed_free, MIXED0 + M_ADA + 2)
            for u in range(BQKV, NBU):
                n, p = BUNITS[u][2]
                dve.wait_ge(unit_done, bdone(u))
                for i in range(2):
                    c = 4 * n + 2 * p + i
                    ins = dve.scalar_tensor_tensor(out=x[:, c, :], in0=bank[u % BANKS][:, i * T:(i + 1) * T],
                                                   scalar=mod[:, GT1 + c, 0:1], in1=x[:, c, :], op0=ALU.mult,
                                                   op1=ALU.add)
                ins.then_inc(bank_free[u % BANKS], 1)
            if debug == "attention":
                return

            dve.wait_ge(unit_done, bdone(NBU - 1))
            for v in (bin_sb, pos, ext, ys, spread0, spread1, sel):
                ins = dve.memset(v, -1.0 if v is pos else -2.0 ** 126 if v is ext else 0.0)
            link(ins)
            dve.sem_inc(table_ready, 1)
            modulated(h, x, 4, b_("g_ffn"), SH2, SC2, 0, S_FFN).then_inc(bh_ready, 1)
            dve.wait_ge(mixed_done, MIXED0 + M_LOGITS + 1)
            dve.tensor_tensor(ext[:, :, 0:NEXP], mixed[:, 0:2 * NEXP].rearrange("p (a e) -> p a e", a=2),
                              to([P, TT, NEXP], b_("b_router")), ALU.add).then_inc(mixed_free, 1)
            dve.wait_ge(mixed_free, MIXED0 + M_LOGITS + 2)
            for t in range(TT):
                link(dve.max(best[:, t, :], ext[:, t, 0:NEXP]))
            link(dve.memset(fill, -2.0 ** 126))
            link(dve.tensor_copy(fill[:, :, 0:TOPK], best[:, :, 0:TOPK]))
            for t in range(TT):
                link(dve.match_replace(left[:, t, :], fill[:, t, :], ext[:, t, :], -2.0 ** 127))
            dve.tensor_scalar(chosen, left[:, :, 0:NEXP], -1.5 * 2.0 ** 126, None, ALU.is_lt).then_inc(chosen_ready, 1)
            dve.wait_ge(chosen_ready, 1)
            dve.tensor_scalar(gsum[:, :, 0:1], best[:, :, 0:1], -1.0, None, ALU.mult).then_inc(gate_in, 1)
            dve.wait_ge(gate_exp, 1)
            link(dve.tensor_tensor(gate, gate, chosen, ALU.mult))
            link(dve.tensor_reduce(gsum[:, :, 1], gate, AX.X, ALU.add))
            link(dve.reciprocal(gsum[:, :, 2], gsum[:, :, 1]))
            link(dve.tensor_tensor(gate, gate, to([P, TT, NEXP], gsum[:, :, 2], 2), ALU.mult))
            dve.tensor_scalar(gate_half, gate, 0.5, None, ALU.mult).then_inc(gate_in, 1)
            dve.wait_ge(mixed_done, MIXED0 + M_POS + 1)
            link(dve.tensor_copy(cnt, mixed[:, 64:96]))
            pv = pos[:, :, 0:NEXP]
            dve.scalar_tensor_tensor(out=pv, in0=mixed[:, 0:64].rearrange("p (a e) -> p a e", a=2), scalar=1.0,
                                     in1=chosen, op0=ALU.add, op1=ALU.mult).then_inc(mixed_free, 1)
            dve.wait_ge(mixed_free, MIXED0 + M_POS + 2)
            link(dve.tensor_scalar(pv, pv, -1.0, None, ALU.add))
            dve.wait_ge(mixed_done, MIXED0 + M_GATE + 1)
            dve.tensor_copy(gateT[0:NEXP, :], mixed[0:NEXP, 0:T]).then_inc(mixed_free, 1)
            dve.wait_ge(gate_in, 2)

            def column(v, t, e):
                return v[:, t, bass.ds(e, 1)]

            iota = c_("iota")

            def select(hh, e):
                for t in range(TT):
                    ins = dve.tensor_scalar(sel[:, t, HALF * hh:HALF * hh + HALF], iota[:, 0:HALF], column(pos, t, e),
                                            None, ALU.is_equal)
                return ins

            select(0, 0)
            select(1, 1).then_inc(sel_ready, 1)
            for b in range(3):
                ins = dve.tensor_scalar(cand0[:, b * NEXP:(b + 1) * NEXP], cnt, SLOTS * (b + 1) + 0.5, None, ALU.is_gt)
            link(ins)
            src, s = cand0, 1
            k = 0
            while s < 96:
                dst = cand[:, k % 2, :]
                dve.tensor_copy(dst[:, 0:s], src[:, 0:s])
                link(dve.tensor_tensor(dst[:, s:96], src[:, s:96], src[:, 0:96 - s], ALU.add))
                src, s, k = dst, 2 * s, k + 1
            link(dve.tensor_copy(jobi[:, MAXJOBS:MAXJOBS + 1], src[:, 95:96]))
            link(dve.tensor_tensor(cand0, cand0, src, ALU.mult))
            jshape = [P, MAXJOBS, 96]
            link(dve.tensor_tensor(jt, to(jshape, cand0), to(jshape, c_("job"), 2), ALU.is_equal))
            for name, dst in (("expert", jobe), ("start", jobs_)):
                link(dve.tensor_tensor(jt2, jt, to(jshape, c_(name)), ALU.mult))
                link(dve.tensor_reduce(dst, jt2, AX.X, ALU.add))
            link(dve.tensor_copy(jobi[:, 0:MAXJOBS], jobe))
            for s_ in (glu_free, lin_free, eout_free, table_ready):
                dve.sem_inc(s_, 1)
            mark = steps[0]
            dve.wait_ge(bpar_loaded, 64)

            def onehots(hh, e):
                return dve.tensor_copy(onehot[:, hh, :], ident[:, bass.ds(e, 1)].broadcast_to([P, SLOTS]))

            def gates_of(hh, e, where):
                for t in range(TT):
                    ins = dve.tensor_scalar(selg[:, hh, t, :], iota[:, 0:P], where(t), column(gate_half, t, e),
                                            ALU.is_equal, ALU.mult)
                return ins

            def activate(m, hh):
                dve.wait_ge(glu_done, m + 1)
                dve.tensor_scalar(glu[:, hh, :], score[:, 0:W], GLU_LIMIT, None, ALU.min).then_inc(glu_free, 1)
                dve.wait_ge(glu_tanh, m + 1)
                link(dve.scalar_tensor_tensor(out=glu[:, hh, :], in0=tanh_g[:, hh, :], scalar=1.0, in1=glu[:, hh, :],
                                              op0=ALU.add, op1=ALU.mult))
                dve.wait_ge(lin_done, m + 1)
                dve.tensor_scalar(lin[:, hh, :], score[:, W:2 * W], GLU_LIMIT, -GLU_LIMIT, ALU.min,
                                  ALU.max).then_inc(lin_free, 1)
                dve.wait_ge(lin_free, m + 2)
                dve.scalar_tensor_tensor(out=lin[:, hh, :], in0=lin[:, hh, :], scalar=1.0, in1=glu[:, hh, :],
                                         op0=ALU.add, op1=ALU.mult).then_inc(act_ready, 1)

            def expert_rows(m, hh):
                dve.wait_ge(eout_done, m + 1)
                dve.tensor_copy(ys[:, hh, :], mixed[:, :]).then_inc(eout_free, 1)

            with dve.Fori(0, PAIRS) as i:
                base[0] = i * PER["pair"] + mark
                steps[0] = 0
                onehots(0, i * 2)
                onehots(1, i * 2 + 1).then_inc(onehot_ready, 1)
                gates_of(0, i * 2, lambda t: column(pos, t, i * 2))
                gates_of(1, i * 2 + 1, lambda t: column(pos, t, i * 2 + 1)).then_inc(selg_ready, 1)
                activate(i * 2, 0)
                select(0, i * 2 + 2)
                select(1, i * 2 + 3).then_inc(sel_ready, 1)
                expert_rows(i * 2, 0)
                activate(i * 2 + 1, 1)
                expert_rows(i * 2 + 1, 1)
                assert steps[0] == PER["pair"], steps[0]
            mark2 = mark + PAIRS * PER["pair"]
            n_jobs = dve.value_load(jobi[0:1, MAXJOBS:MAXJOBS + 1], min_val=0, max_val=MAXJOBS)
            with dve.If(n_jobs > 0):
                with dve.Fori(0, n_jobs) as i:
                    base[0] = i * PER["job"] + mark2
                    steps[0] = 0
                    e = dve.value_load(jobi[0:1, bass.ds(i, 1)], min_val=0, max_val=NEXP - 1)
                    dve.wait_ge(scattered, i + 1)
                    for t in range(TT):
                        ins = dve.tensor_tensor(posb[:, t, :], column(pos, t, e), jobs_[:, bass.ds(i, 1)], ALU.subtract)
                    link(ins)
                    onehots(0, e).then_inc(onehot_ready, 1)
                    gates_of(0, e, lambda t: posb[:, t, 0:1]).then_inc(selg_ready, 1)
                    for t in range(TT):
                        ins = dve.tensor_scalar(sel[:, t, 0:HALF], iota[:, 0:HALF], posb[:, t, 0:1], None, ALU.is_equal)
                    ins.then_inc(sel_ready, 1)
                    activate(i + NEXP, 0)
                    expert_rows(i + NEXP, 0)
                    assert steps[0] == PER["job"], steps[0]
            dve.wait_ge(scattered, n_jobs + 1)
            for c in range(DC):
                ins = dve.scalar_tensor_tensor(out=x[:, c, :], in0=bank[c // 2][:, (c % 2) * T:(c % 2 + 1) * T],
                                               scalar=mod[:, GT2 + c, 0:1], in1=x[:, c, :], op0=ALU.mult, op1=ALU.add)
            ins.then_inc(bh_ready, 1)
            dve.wait_ge(scored, SCORE0 + S_FINAL + 1)
            dve.tensor_scalar(bvarx, score[:, 0:T], 1.0 / D, EPS, ALU.mult, ALU.add).then_inc(bvar, 1)
            dve.wait_ge(broot, 5)
            dve.reciprocal(brsx, brsx).then_inc(bh_ready, 1)
            dve.wait_ge(bh_ready, 5)
            for c in range(DC):
                ins = dve.scalar_tensor_tensor(out=h[:, c, :], in0=x[:, c, :], scalar=b_("g_final", c, 1), in1=brsx,
                                               op0=ALU.mult, op1=ALU.mult)
            ins.then_inc(final_ready, 1)

        def columns(weights, a, n):
            return weights[:, a:a + n].rearrange("(c p) n -> p c n", p=P)

        @block.sync
        def _(sp):
            for dst, src in ((cst[:], consts), (cvec[:].rearrange("p c b -> p (c b)"), c_in), (x[:], xT)):
                sp.dma_start(dst, src).then_inc(loaded, 16)

            def tile(l, n, parts):
                sp.wait_ge(unit_done, slot_left(l, n))
                sp.sem_inc(asked, 1)
                dst, src = parts
                sp.dma_start(dst, src).then_inc(landed[n % RING], 16)

            def slot(n):
                return ring[:, n % RING, :].rearrange("p (c n) -> p c n", c=DC)

            with sp.Fori(0, LAYERS) as l:
                wl = w_in[bass.ds(l, 1)].rearrange("a k n -> (a k) n")
                for n in range(4):
                    if n == 3:
                        sp.dma_start(par[:, :], layer_params[:, bass.ds(l, 1), :].rearrange("p a n -> p (a n)")).then_inc(par_loaded, 16)
                    tile(l, n, (slot(n), w_ada[:, bass.ds(l * 4 * W + n * W, W)].rearrange("(c p) n -> p c n", p=P)))
                tile(l, 4, (slot(4)[:, :, 0:LORA], columns(wl, COL_LORA, LORA)))
                for g in range(GROUPS):
                    tile(l, 5 + g, (slot(5 + g), columns(wl, COL_DQ + g * W, W)))
                sp.wait_ge(unit_done, slot_left(l, 8))
                sp.sem_inc(asked, 1)
                s8 = ring[:, 8 % RING, :]
                sp.dma_start(s8[:, 0:2 * 768].rearrange("p (c n) -> p c n", c=2),
                             w_uq[bass.ds(l, 1)].rearrange("a (c p) n -> p (a c) n", p=P)).then_inc(uq_loaded, 16)
                sp.dma_start(s8[:, 2 * 768:2 * 768 + D],
                             w_ukv[bass.ds(l, 1)].rearrange("a p n -> p (a n)")).then_inc(landed[0], 16)
                for g in range(GROUPS):
                    tile(l, 9 + g, (slot(9 + g), columns(wl, COL_DK + g * W, W)))
                for g in range(GROUPS):
                    tile(l, 12 + g, (slot(12 + g), columns(wl, COL_DV + g * W, W)))
                for n, a in ((15, COL_BZ), (16, COL_CZ), (17, COL_AC), (18, COL_AX), (19, COL_AB), (20, COL_AZ)):
                    tile(l, n, (slot(n), columns(wl, a, W)))
                for i in range(6):
                    tile(l, 21 + i, (slot(21 + i), columns(wl, COL_GATE + i * W, W)))
                for b, wb in enumerate((w_out_a, w_out_b, w_out_c)):
                    tile(l, 27 + b, (ring[:, (27 + b) % RING, :].rearrange("p (c n) -> p c n", c=4),
                                     wb[bass.ds(l, 1)].rearrange("a (c p) n -> p (a c) n", p=P)))
                wol = w_o[bass.ds(l, 1)].rearrange("a k n -> (a k) n")
                for n in range(2):
                    tile(l, 30 + n, (slot(30 + n), columns(wol, n * W, W)))
            if debug == "layers":
                for b in range(BANKS):
                    sp.wait_ge(bank_free[b], LAYERS * PER_BANK + 1)
                sp.dma_start(out, x[:]).then_inc(stored, 16)
                sp.wait_ge(stored, 16)
            else:
                block_sync(sp)

        @block.tensor
        def _(pe):
            pe.wait_ge(loaded, 48)
            pe.wait_ge(silu_ready, 1)
            pe.sem_inc(unit_done, NU)

            def norm_sum(source, n_chunks, columns):
                for c in range(n_chunks):
                    ins = pe.matmul(score[:, 0:columns], ones, source[:, c, :], start=c == 0,
                                    stop=c == n_chunks - 1)
                return ins

            def unit(l, u, parts=(0, 1)):
                kind, tl, who = UNITS[u]
                if 0 in parts:
                    pe.wait_ge(landed[tl % RING], l * (16 * NT // RING) + 16 * (tl // RING + 1))
                    pe.wait_ge(bank_free[u % BANKS], freed(l, u) - 1)
                b = bank[u % BANKS]
                w8 = ring[:, tl % RING, :].rearrange("p (c n) -> p c n", c=DC)
                w4 = ring[:, tl % RING, :].rearrange("p (c n) -> p c n", c=4)
                if kind == "ada":
                    ins = ada_rows(pe, b, w8, parts)
                elif kind in ("lora", "dq", "dk", "dv"):
                    t = who[-1]
                    n = LORA if kind == "lora" else W
                    for c in range(DC):
                        ins = pe.matmul(b[:, 0:n], h[:, c, t * P:(t + 1) * P], w8[:, c, 0:n],
                                        start=c == 0, stop=c == DC - 1)
                elif kind == "mq":
                    half, t = who
                    pe.wait_ge(uq_loaded, l * 16 + 16)
                    wq = ring[:, tl % RING, 0:1536].rearrange("p (c n) -> p c n", c=2)
                    for c in range(2):
                        ins = pe.matmul(b[:, 0:384], cT[:, c, t * P:(t + 1) * P],
                                        wq[:, c, half * 384:(half + 1) * 384], start=c == 0, stop=c == 1)
                elif kind == "mkv":
                    half, t = who
                    ins = pe.matmul(b[:, :], cT[:, 2, t * P:(t + 1) * P],
                                    ring[:, tl % RING, 1536 + half * W:1536 + (half + 1) * W],
                                    start=True, stop=True)
                elif kind == "merge":
                    p, br = who
                    y = (conv, yB, yC)[br]
                    for i in range(2):
                        m = (2 * p + i) * P
                        for c in range(4):
                            ins = pe.matmul(b[:, i * T:(i + 1) * T], w4[:, c, m:m + P], y[:, c, :],
                                            start=c == 0, stop=c == 3)
                else:
                    p = who[-1]
                    for i in parts:
                        m = (2 * p + i) * P
                        for c in range(DC):
                            ins = pe.matmul(b[:, i * T:(i + 1) * T], w8[:, c, m:m + P], h[:, c, :],
                                            start=c == 0, stop=c == DC - 1)
                return ins

            def turn(l, u):
                kind = UNITS[u][0]
                n = NORMED.index(u)
                pe.wait_ge(qn_ready, l * NN + n + 1)
                pe.wait_ge(flip_free, l * NTR + n + 1)
                src = qn[:, n % 2, :]
                if kind == "lora":
                    blocks = [(P, src[:, i * P:(i + 1) * P]) for i in range(3)]
                elif kind in ("dq", "dk"):
                    blocks = [(P, src[:, i * P:(i + 1) * P]) for i in range(4)]
                else:
                    blocks = [(MQK, src[:, i * MQK:(i + 1) * MQK]) for i in range(4)]
                for i, (m, blk) in enumerate(blocks):
                    ins = pe.transpose(flip[0:m, i * P:(i + 1) * P], blk, ident)
                ins.then_inc(flipped, 1)

            halves = [0]

            def fill(l):
                u, part = PREP + halves[0] // 2, halves[0] % 2
                halves[0] += 1
                ins = unit(l, u, (part,))
                if part:
                    ins.then_inc(unit_done, 1)

            def scores(l, j):
                pe.wait_ge(score_free, l * NS + j + 2)
                job = JOBS[j]
                if job[0] == "mla":
                    q, k = mqT[0:MQK, job[1], :], mkT[0:MQK, job[1], :]
                    pe.matmul(score[:, 0:P], q[:, 0:P], k[:, 0:P], start=True, stop=True)
                    ins = pe.matmul(score[:, P:P + T], q[:, P:T], k, start=True, stop=True)
                else:
                    _, hd, t = job
                    n = (t + 1) * P
                    lo = HALF * (hd % 2)
                    for g in range(GROUPS):
                        q = dqT[lo:lo + HALF, g * 4 + hd // 2, t * P:(t + 1) * P]
                        k = dkT[lo:lo + HALF, g * 4 + hd // 2, 0:n]
                        ins = pe.matmul(score[:, g * n:(g + 1) * n], q, k, start=True, stop=True)
                ins.then_inc(scored, 1)

            def values(l, j):
                job = JOBS[j]
                hd = job[1]
                lo = HALF * (hd % 2)
                pe.wait_ge(probs_ready, l * NJ + j + 1)
                pe.wait_ge(mixed_free, l * NM + j + 2)
                blocks = 3 if job[0] == "mla" or job[2] == 0 else 6
                for r, cols in enumerate(ROUNDS[j]):
                    fr = first_flip(j) + r
                    pe.wait_ge(flip_free, l * NTR + fr + 1)
                    for i, c in enumerate(cols):
                        ins = pe.transpose(flip[:, i * P:(i + 1) * P], probs[:, j % 2, c * P:(c + 1) * P], ident)
                    ins.then_inc(flipped, 1)
                    fill(l)
                    pe.wait_ge(flip_free, l * NTR + fr + 2)
                    pt = turned[:, (FIRST_ROUND[j] + r) % 2, :]
                    for i, c in enumerate(cols):
                        if job[0] == "mla":
                            o = mixed[lo:lo + HALF, (0, P, P)[c]:(0, P, P)[c] + P]
                            v = mv[:, (0, 0, 1)[c], hd * HALF:(hd + 1) * HALF]
                            first, last = c < 2, c != 1
                        else:
                            t = job[2]
                            g, kt = c // (t + 1), c % (t + 1)
                            o = mixed[lo:lo + HALF, 0:P]
                            v = dv[:, kt, g * W + hd * HALF:g * W + (hd + 1) * HALF]
                            first, last = c == 0, c == blocks - 1
                        ins = pe.matmul(o, v, pt[:, i * P:(i + 1) * P], start=first, stop=last)
                ins.then_inc(mixed_done, 1)

            with pe.Fori(0, LAYERS) as l:
                def step(u):
                    unit(l, u).then_inc(unit_done, 1)

                step(0)
                step(1)
                pe.wait_ge(squared, l + 1)
                pe.wait_ge(score_free, l * NS + 1)
                norm_sum(h, DC, T).then_inc(scored, 1)
                step(2)
                step(3)
                pe.wait_ge(mixed_free, l * NM + 1)
                for n in range(ADAS):
                    pe.wait_ge(bank_free[n], freed(l, n))
                    ins = pick(pe, modrow[:, n, :], 8 * n)
                ins.then_inc(mixed_done, 1)
                for u in range(ADAS, PREP + LAG):
                    if u < PREP:
                        if UNITS[u][0] == "lora":
                            pe.wait_ge(hready, l + 1)
                        if UNITS[u][0] == "mq" and UNITS[u][2] == (0, 0):
                            pe.wait_ge(flip_free, l * NTR + 2 + 1)
                        step(u)
                    if u >= LAG and u - LAG in NORMED:
                        turn(l, u - LAG)
                pe.wait_ge(flip_free, l * NTR + NN + 1)
                for b in range(BANKS):
                    pe.wait_ge(bank_free[(PREP - 1 - b) % BANKS], freed(l, PREP - 1 - b))
                halves[0] = 0
                for j in range(NJ + 1):
                    if j < NJ:
                        scores(l, j)
                    if j > 0:
                        values(l, j - 1)
                    while halves[0] < sum(HALVES[:j + 1]):
                        fill(l)
                pe.wait_ge(conv_ready, l + 1)
                pe.wait_ge(mixed_free, l * NM + NM + 1)
                for u in range(FILL, MERGED):
                    step(u)
                pe.wait_ge(merged, l + 1)
                for u in range(MERGED, NU):
                    step(u)
            if debug != "layers":
                block_tensor(pe)

        @block.scalar
        def _(act):
            act.wait_ge(loaded, 48)
            act.sem_inc(flip_free, 1)
            act.activation(tanh_z[:, 0:2 * DC], cvec[:].rearrange("p c b -> p (c b)"), ACT.Tanh,
                           scale=0.5).then_inc(ctanh, 1)

            def squares_of(l, n, src, width):
                act.wait_ge(squares_used, l * NN + n + 1)
                act.activation(square[:, 0:width], src, ACT.Square).then_inc(squares, 1)

            def root(l, n):
                act.wait_ge(var_ready, l * NN + n + 1)
                act.activation(rs, var, ACT.Sqrt).then_inc(rs_ready, 1)

            def unflip(l, n):
                kind, _, who = UNITS[NORMED[n]]
                act.wait_ge(flipped, l * NTR + n + 1)
                t = who[-1]
                cols = slice(t * P, (t + 1) * P)
                v = flip[:, :].rearrange("p (a t) -> p a t", t=P)
                if kind == "lora":
                    act.activation(cT[:, 0, cols], v[:, 0, :], ACT.Copy, scale=l_("q_a", 0, 1))
                    act.activation(cT[:, 1, cols], v[:, 1, :], ACT.Copy, scale=l_("q_a", 1, 1))
                    ins = act.activation(cT[:, 2, cols], v[:, 2, :], ACT.Copy, scale=l_("kv_a", 0, 1))
                elif kind in ("dq", "dk"):
                    g = who[0]
                    dst = (dqT if kind == "dq" else dkT)[:, 4 * g:4 * g + 4, cols]
                    ins = act.activation(dst, v[:, 0:4, :], ACT.Copy,
                                         scale=l_("dil_q" if kind == "dq" else "dil_k", g, 1))
                else:
                    half = who[0]
                    dst = (mqT if kind == "mq" else mkT)[0:MQK, 4 * half:4 * half + 4, cols]
                    ins = act.activation(dst, v[0:MQK, 0:4, :], ACT.Copy,
                                         scale=MQK ** -0.5 if kind == "mq" else 1.0)
                ins.then_inc(flip_free, 1)

            def evacuate(l, u):
                kind, _, who = UNITS[u]
                b = bank[u % BANKS]
                if kind in ("merge", "out", "ac", "ax", "ab"):
                    return
                if kind == "ada":
                    act.wait_ge(unit_done, done(l, u))
                    act.activation(modrow[:, who[0], :], b[:, :], ACT.Copy).then_inc(bank_free[u % BANKS], 1)
                    return
                if kind == "mkv":
                    act.wait_ge(copied, l * 4 + [x for x in range(NU) if UNITS[x][0] == "mkv"].index(u) + 1)
                    squares_of(l, NORMED.index(u), mc.rearrange("p a b -> p (a b)"), 384)
                    root(l, NORMED.index(u))
                    return
                act.wait_ge(unit_done, done(l, u))
                if kind == "lora":
                    squares_of(l, NORMED.index(u), b[:, 0:384], 384)
                elif kind in ("dq", "dk"):
                    squares_of(l, NORMED.index(u), b[:, :], W)
                elif kind == "mq":
                    squares_of(l, NORMED.index(u), b[:, 0:384], 384)
                if u in NORMED:
                    root(l, NORMED.index(u))
                elif kind == "dv":
                    g, t = who
                    act.activation(dv[:, t, g * W:(g + 1) * W], b[:, :], ACT.Copy).then_inc(bank_free[u % BANKS], 1)
                elif kind in ("z", "az"):
                    z = ZUNITS.index(u)
                    if z:
                        act.wait_ge(bank_free[ZUNITS[z - 1] % BANKS], freed(l, ZUNITS[z - 1]))
                    act.activation(tanh_z, b[:, :], ACT.Tanh, scale=0.5).then_inc(z_tanh, 1)
                elif kind == "gate":
                    n, p = who
                    for i in range(2):
                        c = 4 * n + 2 * p + i
                        ins = act.activation(gates[:, c, :], b[:, i * T:(i + 1) * T], ACT.Tanh, scale=0.5,
                                             bias=l_("b_gate", c, 1))
                    ins.then_inc(bank_free[u % BANKS], 1)

            def exp(l, j):
                job = JOBS[j]
                act.wait_ge(masked, l * NJ + j + 1)
                pr, st = probs[:, j % 2, :], stat[:, j % 2, :]
                if job[0] == "mla":
                    act.activation(pr[:, 0:P], pr[:, 0:P], ACT.Exp, bias=st[:, 2:3], accum_out=st[:, 4:5])
                    ins = act.activation(pr[:, P:384], pr[:, P:384], ACT.Exp, bias=st[:, 3:4],
                                         accum_out=st[:, 5:6])
                else:
                    n = 384 * (job[2] + 1)
                    ins = act.activation(pr[:, 0:n], pr[:, 0:n], ACT.Exp, bias=st[:, 2:3], accum_out=st[:, 4:5])
                ins.then_inc(exped, 1)

            def unflip_probs(l, j):
                for r in range(len(ROUNDS[j])):
                    rr = FIRST_ROUND[j] + r
                    act.wait_ge(flipped, l * NTR + NN + rr + 1)
                    if r == 0 and j >= 1:
                        act.wait_ge(mixed_done, l * NM + j + 1)
                    act.activation(turned[:, rr % 2, 0:384], flip[:, 0:384], ACT.Copy).then_inc(flip_free, 1)

            with act.Fori(0, LAYERS) as l:
                act.wait_ge(bank_free[(NU - 1) % BANKS], freed(l, NU - 1) - PER_BANK)
                act.activation(h[:], x[:], ACT.Square).then_inc(squared, 1)
                evacuate(l, 0)
                evacuate(l, 1)
                act.wait_ge(score_free, l * NS + 2)
                act.activation(rsx, varx, ACT.Sqrt).then_inc(rsx_ready, 1)
                evacuate(l, 2)
                evacuate(l, 3)
                act.wait_ge(par_ready, l + 1)
                for u in range(ADAS, PREP + LAG):
                    if u < PREP:
                        evacuate(l, u)
                    if u >= LAG and u - LAG in NORMED:
                        unflip(l, NORMED.index(u - LAG))
                for j in range(NJ + 1):
                    if j < NJ:
                        exp(l, j)
                    if j > 0:
                        unflip_probs(l, j - 1)
                    for u in DONE_IN[j]:
                        evacuate(l, u)
            if debug != "layers":
                block_scalar(act)

        @block.vector
        def _(dve):
            steps = [0]
            base = [0]

            def link(ins):
                steps[0] += 1
                ins.then_inc(chain, 1)
                dve.wait_ge(chain, base[0] + steps[0])

            dve.wait_ge(loaded, 48)
            for s in (score_free, mixed_free, squares_used, *bank_free):
                dve.sem_inc(s, 1)
            link(dve.memset(up[:, :, 0:2], 0.0))
            link(dve.memset(var, 1.0))
            link(dve.memset(silu[:], 0.0))
            dve.wait_ge(ctanh, 1)
            link(dve.scalar_tensor_tensor(out=silu[:, :, 0:2], in0=tanh_z[:, 0:2 * DC].rearrange("p (c b) -> p c b", b=2),
                                          scalar=1.0, in1=cvec[:], op0=ALU.add, op1=ALU.mult))
            dve.tensor_scalar(silu[:, :, 0:2], silu[:, :, 0:2], 0.5, None, ALU.mult).then_inc(silu_ready, 1)
            start = steps[0]
            steps[0] = 0

            def mean(dst, src, n):
                return dve.tensor_scalar(dst, src, 1.0 / n, EPS, ALU.mult, ALU.add)

            def heads(v, n):
                return v.rearrange("p (a b) -> p a b", b=n)

            def rotate(v, cos, sin, n):
                a = v.shape[1]
                r0 = rope[:, 0, 0:a * n].rearrange("p (a two n) -> p a two n", a=a, two=2)
                r1 = rope[:, 1, 0:a * n].rearrange("p (a two n) -> p a two n", a=a, two=2)
                full = [P, a, 2, n // 2]
                part = [P, a, n // 2]
                dve.tensor_tensor(r0, v, cos.broadcast_to(full), ALU.mult)
                dve.tensor_tensor(r1[:, :, 0, :], v[:, :, 1, :], sin[:, :, 0, :].broadcast_to(part), ALU.mult)
                link(dve.tensor_tensor(r1[:, :, 1, :], v[:, :, 0, :], sin[:, :, 1, :].broadcast_to(part), ALU.mult))
                return dve.tensor_tensor(v, r0, r1, ALU.add)

            def normalize(l, u):
                kind, _, who = UNITS[u]
                n = NORMED.index(u)
                t = who[-1]
                b = bank[u % BANKS]
                q = qn[:, n % 2, :]
                if kind == "mkv":
                    half = who[0]
                    dve.wait_ge(unit_done, done(l, u))
                    kv = heads(b[:, :], P)
                    mch = mc[:, :, :]
                    dve.tensor_copy(mch[:, :, 0:HALF], kv[:, :, 0:HALF])
                    dve.tensor_copy(mch[:, :, HALF:MQK], kpe[:, t:t + 1, :].broadcast_to([P, 4, MROPE])).then_inc(copied, 1)
                    dve.tensor_copy(heads(mv[:, t, half * 256:(half + 1) * 256], HALF),
                                    kv[:, :, HALF:P]).then_inc(bank_free[u % BANKS], 1)
                dve.wait_ge(squares, l * NN + n + 1)
                if kind == "lora":
                    link(dve.tensor_reduce(ssum[:, 0:1], square[:, 0:256], AX.X, ALU.add))
                    dve.tensor_reduce(ssum[:, 1:2], square[:, 256:384], AX.X, ALU.add).then_inc(squares_used, 1)
                    dve.wait_ge(squares_used, l * NN + n + 2)
                    link(mean(var[:, 0:1], ssum[:, 0:1], 256))
                    mean(var[:, 1:2], ssum[:, 1:2], 128).then_inc(var_ready, 1)
                else:
                    a, w = (8, HALF) if kind in ("dq", "dk") else (4, MQK)
                    dve.tensor_reduce(ssum[:, 0:a], heads(square[:, 0:a * w], w), AX.X,
                                      ALU.add).then_inc(squares_used, 1)
                    dve.wait_ge(squares_used, l * NN + n + 2)
                    mean(var[:, 0:a], ssum[:, 0:a], w).then_inc(var_ready, 1)
                dve.wait_ge(rs_ready, l * NN + n + 1)
                link(dve.reciprocal(rs, rs))
                if n >= 2:
                    dve.wait_ge(flipped, l * NTR + n - 1)
                if kind == "lora":
                    link(dve.tensor_copy(kpe[:, t, :], b[:, 384:416]))
                    link(dve.tensor_scalar(q[:, 0:256], b[:, 0:256], rs[:, 0:1], None, ALU.mult))
                    dve.tensor_scalar(q[:, 256:384], b[:, 256:384], rs[:, 1:2], None,
                                      ALU.mult).then_inc(bank_free[u % BANKS], 1)
                    dve.wait_ge(bank_free[u % BANKS], freed(l, u))
                    dve.sem_inc(qn_ready, 1)
                elif kind in ("dq", "dk"):
                    link(dve.tensor_tensor(heads(q, HALF), heads(b[:, :], HALF),
                                           rs[:, 0:8].unsqueeze(2).broadcast_to([P, 8, HALF]), ALU.mult))
                    dve.sem_inc(bank_free[u % BANKS], 1)
                    dve.sem_inc(qn_ready, 1)
                else:
                    src = heads(b[:, 0:384], MQK) if kind == "mq" else mc[:, :, :]
                    qh = heads(q[:, 0:384], MQK)
                    link(dve.tensor_tensor(qh, src, rs[:, 0:4].unsqueeze(2).broadcast_to([P, 4, MQK]), ALU.mult))
                    if kind == "mq":
                        dve.sem_inc(bank_free[u % BANKS], 1)
                    g = l_("mla_q" if kind == "mq" else "mla_k").unsqueeze(1).broadcast_to([P, 4, MQK])
                    link(dve.tensor_tensor(qh, qh, g, ALU.mult))
                    cs = c_("cosm")[:, t * 32:(t + 1) * 32].rearrange("p (a two n) -> p a two n", a=1, two=2)
                    sn = c_("sinm")[:, t * 32:(t + 1) * 32].rearrange("p (a two n) -> p a two n", a=1, two=2)
                    rotate(qh[:, :, HALF:MQK].rearrange("p a (two n) -> p a two n", two=2), cs, sn,
                           MROPE).then_inc(qn_ready, 1)

            def evacuate(l, u):
                kind, _, who = UNITS[u]
                b = bank[u % BANKS]
                free = bank_free[u % BANKS]
                if kind in ("dv", "gate", "ada"):
                    return
                if u in NORMED:
                    normalize(l, u)
                    return
                p = who[-1] if kind != "merge" else who[0]
                pair = slice(2 * p, 2 * p + 2)
                both = heads(b[:, :], T)
                if kind in ("z", "az"):
                    dve.wait_ge(z_tanh, l * len(ZUNITS) + ZUNITS.index(u) + 1)
                else:
                    dve.wait_ge(unit_done, done(l, u))
                if kind == "z":
                    dve.scalar_tensor_tensor(out=(yB, yC)[who[0]][:, pair, :], in0=heads(tanh_z, T), scalar=1.0,
                                             in1=both, op0=ALU.add, op1=ALU.mult).then_inc(free, 1)
                elif kind == "ac":
                    dve.tensor_copy(conv[:, pair, :], both).then_inc(free, 1)
                elif kind == "ax":
                    dve.wait_ge(bank_free[(u - 2) % BANKS], freed(l, u - 2))
                    dve.tensor_tensor(up[:, pair, 2:T + 2], conv[:, pair, :], both, ALU.mult).then_inc(free, 1)
                elif kind == "ab":
                    dve.wait_ge(bank_free[(u - 2) % BANKS], freed(l, u - 2))
                    for c in range(2 * p, 2 * p + 2):
                        link(dve.tensor_scalar(conv[:, c, :], up[:, c, 0:T], l_("conv_w", c, 1),
                                               l_("conv_b", c, 1), ALU.mult, ALU.add))
                        for tap in (1, 2):
                            link(dve.scalar_tensor_tensor(out=conv[:, c, :], in0=up[:, c, tap:tap + T],
                                                          scalar=l_("conv_w", 4 * tap + c, 1), in1=conv[:, c, :],
                                                          op0=ALU.mult, op1=ALU.add))
                    dve.tensor_tensor(conv[:, pair, :], conv[:, pair, :], both, ALU.mult).then_inc(free, 1)
                elif kind == "az":
                    dve.wait_ge(bank_free[(u - 2) % BANKS], freed(l, u - 2))
                    dve.scalar_tensor_tensor(out=heads(mtmp, T), in0=heads(tanh_z, T), scalar=1.0,
                                             in1=both, op0=ALU.add, op1=ALU.mult).then_inc(free, 1)
                    dve.wait_ge(free, freed(l, u))
                    ins = dve.scalar_tensor_tensor(out=conv[:, pair, :], in0=heads(mtmp, T), scalar=0.5,
                                                   in1=conv[:, pair, :], op0=ALU.mult, op1=ALU.mult)
                    if p == 1:
                        ins.then_inc(conv_ready, 1)
                elif kind == "merge":
                    br = who[1]
                    gsl = gates[:, DC * br + 2 * p:DC * br + 2 * p + 2, :]
                    dst = h[:, pair, :] if br == 0 else heads(mtmp, T)
                    dve.scalar_tensor_tensor(out=dst, in0=gsl, scalar=1.0, in1=both, op0=ALU.add,
                                             op1=ALU.mult).then_inc(free, 1)
                    dve.wait_ge(free, freed(l, u))
                    if br:
                        ins = dve.tensor_tensor(h[:, pair, :], h[:, pair, :], heads(mtmp, T), ALU.add)
                        if u == MERGED - 1:
                            ins.then_inc(merged, 1)
                        else:
                            link(ins)
                elif kind == "out":
                    c = 4 * who[0] + 2 * p
                    dve.scalar_tensor_tensor(out=x[:, c:c + 2, :], in0=both, scalar=0.5, in1=x[:, c:c + 2, :],
                                             op0=ALU.mult, op1=ALU.add).then_inc(free, 1)

            def mask(l, j):
                job = JOBS[j]
                dve.wait_ge(scored, l * NS + j + 2)
                pr, st = probs[:, j % 2, :], stat[:, j % 2, :]
                if job[0] == "mla":
                    dve.tensor_tensor(pr[:, 0:384], score[:, 0:384], c_("mask"), ALU.add).then_inc(score_free, 1)
                    dve.wait_ge(score_free, l * NS + j + 3)
                    dve.tensor_reduce(st[:, 0:1], pr[:, 0:P], AX.X, ALU.max)
                    link(dve.tensor_reduce(st[:, 1:2], pr[:, P:384], AX.X, ALU.max))
                    dve.tensor_scalar(st[:, 2:4], st[:, 0:2], -1.0, None, ALU.mult).then_inc(masked, 1)
                else:
                    _, hd, t = job
                    n = (t + 1) * P
                    for g in range(GROUPS):
                        bias = c_("dist")[:, 384 * g + P * t:384 * g + P * t + n]
                        ins = dve.scalar_tensor_tensor(out=pr[:, g * n:(g + 1) * n], in0=bias, scalar=slope(g, hd),
                                                       in1=score[:, g * n:(g + 1) * n], op0=ALU.mult, op1=ALU.add)
                        if g < GROUPS - 1:
                            link(ins)
                    ins.then_inc(score_free, 1)
                    dve.wait_ge(score_free, l * NS + j + 3)
                    link(dve.tensor_reduce(st[:, 0:1], pr[:, 0:3 * n], AX.X, ALU.max))
                    dve.tensor_scalar(st[:, 2:3], st[:, 0:1], -1.0, None, ALU.mult).then_inc(masked, 1)

            def divide(l, j):
                job = JOBS[j]
                pr, st = probs[:, j % 2, :], stat[:, j % 2, :]
                dve.wait_ge(exped, l * NJ + j + 1)
                if job[0] == "mla":
                    link(dve.reciprocal(st[:, 6:8], st[:, 4:6]))
                    link(dve.tensor_scalar(pr[:, 0:P], pr[:, 0:P], st[:, 6:7], None, ALU.mult))
                    dve.tensor_scalar(pr[:, P:384], pr[:, P:384], st[:, 7:8], None,
                                      ALU.mult).then_inc(probs_ready, 1)
                else:
                    n = 384 * (job[2] + 1)
                    link(dve.reciprocal(st[:, 6:7], st[:, 4:5]))
                    dve.tensor_scalar(pr[:, 0:n], pr[:, 0:n], st[:, 6:7], None, ALU.mult).then_inc(probs_ready, 1)

            def gated(l, j):
                job = JOBS[j]
                hd = job[1]
                lo = HALF * (hd % 2)
                dve.wait_ge(mixed_done, l * NM + j + 2)
                y = yB if job[0] == "mla" else yC
                cols = slice(0, T) if job[0] == "mla" else slice(job[2] * P, (job[2] + 1) * P)
                n = T if job[0] == "mla" else P
                dst = y[lo:lo + HALF, hd // 2, cols]
                dve.scalar_tensor_tensor(out=dst, in0=mixed[lo:lo + HALF, 0:n], scalar=0.5, in1=dst,
                                         op0=ALU.mult, op1=ALU.mult).then_inc(mixed_free, 1)

            with dve.Fori(0, LAYERS) as l:
                base[0] = l * PER["layer"] + start
                dve.wait_ge(par_loaded, l * 16 + 16)
                link(dve.tensor_scalar(l_("dil_q"), l_("dil_q"), HALF ** -0.5, None, ALU.mult))
                dve.tensor_scalar(l_("b_gate"), l_("b_gate"), 0.5, None, ALU.mult).then_inc(par_ready, 1)
                dve.wait_ge(par_ready, l + 1)
                dve.wait_ge(scored, l * NS + 1)
                dve.tensor_scalar(varx, score[:, 0:T], 1.0 / D, EPS, ALU.mult, ALU.add).then_inc(score_free, 1)
                dve.wait_ge(rsx_ready, l + 1)
                link(dve.reciprocal(rsx, rsx))
                for c in range(DC):
                    ins = dve.scalar_tensor_tensor(out=h[:, c, :], in0=x[:, c, :], scalar=l_("norm_g", c, 1),
                                                   in1=rsx, op0=ALU.mult, op1=ALU.mult)
                ins.then_inc(hready, 1)
                dve.wait_ge(mixed_done, l * NM + 1)
                dve.tensor_copy(mod[:, bass.ds(l * 4 * ADAS, 4 * ADAS), :],
                                mixed[:, 0:8 * ADAS].rearrange("p (c b) -> p c b", b=2)).then_inc(mixed_free, 1)
                for u in range(PREP):
                    evacuate(l, u)
                for j in range(NJ + 1):
                    if j < NJ:
                        mask(l, j)
                    for u in DONE_IN[j - 1] if j else ():
                        evacuate(l, u)
                    if j < NJ:
                        divide(l, j)
                    if j > 0:
                        gated(l, j - 1)
                for u in DONE_IN[NJ]:
                    evacuate(l, u)
                dve.wait_ge(bank_free[(FILL - 1) % BANKS], freed(l, FILL - 1))
                dve.wait_ge(bank_free[(FILL - 2) % BANKS], freed(l, FILL - 2))
                for u in range(FILL, NU):
                    evacuate(l, u)
                assert steps[0] == PER["layer"], steps[0]
            if debug != "layers":
                steps[0] += start + (LAYERS - 1) * PER["layer"]
                base[0] = 0
                block_vector(dve, link, steps, base)


def constants():
    import numpy as np
    out = {}
    p = np.arange(P)
    out["ident"] = np.eye(P)
    out["ones"] = np.ones((P, P))
    tok = np.arange(T, dtype=np.float32).reshape(TT, P).T
    inv = 10000.0 ** (-np.arange(0, MROPE, 2, dtype=np.float32) / MROPE)
    ang = tok[:, :, None] * inv.astype(np.float32)
    out["cosm"] = np.stack([np.cos(ang), np.cos(ang)], axis=2)
    out["sinm"] = np.stack([-np.sin(ang), np.sin(ang)], axis=2)
    query = np.concatenate([np.broadcast_to(p[:, None], (P, P)), np.broadcast_to(p[:, None] + P, (P, T))], axis=1)
    key = np.concatenate([np.arange(P), np.arange(T)])[None, :]
    far = query - key
    out["mask"] = np.where(far >= 0, 0.0, MASKED)
    out["dist"] = np.stack([np.where((far >= 0) & (far % d == 0) & (far // d <= w // d), -far, MASKED)
                            for w, d in ((128, 1), (512, 4), (2048, 16))], axis=1)
    out["iota"] = np.broadcast_to(np.concatenate([np.arange(SLOTS)] * 4), (P, 2 * P))
    inv = 10000.0 ** (-np.arange(16, dtype=np.float32) / 16)
    axes = np.stack([tok // 64, tok % 64], axis=2)
    ang = axes[:, :, :, None] * inv.astype(np.float32)
    out["cosx"] = np.stack([np.cos(ang), np.cos(ang)], axis=3)
    out["sinx"] = np.stack([-np.sin(ang), np.sin(ang)], axis=3)
    out["before"] = (p[:, None] < p[None, :])
    out["pick"] = p[:, None] % 32 == np.arange(2)[None, :]
    out["expert"] = np.broadcast_to(np.tile(np.arange(NEXP), 3), (P, 96))
    out["start"] = np.broadcast_to(np.repeat(np.arange(1, 4) * SLOTS, NEXP), (P, 96))
    out["job"] = np.broadcast_to(np.arange(1, MAXJOBS + 1), (P, MAXJOBS))
    return np.concatenate([out[k].reshape(P, -1).astype(np.float32) for k in CONSTS], axis=1)


def arrange(inputs):
    import numpy as np

    def f(name):
        return np.ascontiguousarray(inputs[name])

    def fm(a):
        a = a.reshape(*a.shape[:-1], -1, P)
        return np.moveaxis(a, -1, 0)

    def rows(a):
        return np.broadcast_to(a.reshape(1, -1), (P, a.size))

    x, lay, blk = f("x"), {}, {}
    lay["norm_g"] = fm(f("norm_g"))
    lay["b_gate"] = fm(f("b_gate"))
    lay["conv_w"] = fm(f("conv_w"))
    lay["conv_b"] = fm(f("conv_b"))
    lay["q_a"] = fm(f("q_a_norm_g"))
    lay["kv_a"] = fm(f("kv_a_norm_g"))
    for k in "qk":
        g = f(f"dil_{k}_norm_g")
        lay[f"dil_{k}"] = np.moveaxis(np.concatenate([g, g], axis=2), 2, 0)
        g = f(f"mla_{k}_norm_g")
        lay[f"mla_{k}"] = np.broadcast_to(g[None], (P, *g.shape))
    layer_params = np.concatenate([lay[k].reshape(P, LAYERS, -1) for k in LAYER_PARAMS], axis=2)
    blk["b_ada"] = fm(f("b_ada_2")[0])
    blk["g_attn"] = fm(f("g_attn_2")[0])
    blk["g_ffn"] = fm(f("g_ffn_2")[0])
    blk["g_final"] = fm(f("g_final_2"))
    blk["subln"] = fm(f("diff_subln_2")[0])
    cs = np.stack([fm(f("c_2")[0]), fm(f("c_ctx_2"))], axis=2)
    blk["gqa_q"] = rows(f("gqa_q_norm_2"))
    blk["gqa_k"] = rows(f("gqa_k_norm_2"))
    blk["lam"] = rows(f("diff_lambda_2"))
    blk["b_router"] = rows(f("b_router_2"))
    blk["w_router"] = np.moveaxis(f("w_router_2")[0].reshape(DC, P, NEXP), 1, 0)
    block_params = np.concatenate([blk[k].reshape(P, -1) for k in BLOCK_PARAMS], axis=1)
    return dict(
        in_c=np.ascontiguousarray(cs.reshape(P, -1)), in_x=np.ascontiguousarray(np.moveaxis(x[0].reshape(T, DC, P), (0, 1, 2), (2, 1, 0))),
        in_ctx=np.ascontiguousarray(np.moveaxis(f("ctx_2")[0].reshape(T, DC, P), (0, 1, 2), (2, 1, 0))),
        in_consts=constants(), in_layer_params=np.ascontiguousarray(layer_params),
        in_block_params=np.ascontiguousarray(block_params),
        in_w_in=f("w_in"), in_w_uq=f("w_uq"), in_w_ukv=f("w_ukv"), in_w_out_a=f("w_out_a"),
        in_w_out_b=f("w_out_b"), in_w_out_c=f("w_out_c"), in_w_o=f("w_o"), in_w_ada=f("w_ada_2")[0],
        in_w_qkv=f("w_qkv_2")[0], in_w_o2=f("w_o_2")[0], in_e_in=f("w_in_2")[0], in_eb_in=f("b_in_2")[0],
        in_e_out=f("w_out_2")[0], in_eb_out=f("b_out_2")[0])


def kernel(**inputs):
    import numpy as np
    from concourse import bacc
    from concourse.bass_utils import run_bass_kernel_spmd

    arrays = arrange(inputs)
    nc = bacc.Bacc("TRN2", target_bir_lowering=False, num_devices=1)
    args = [nc.dram_tensor(f"{name}_dram", a.shape, mybir.dt.from_np(a.dtype), kind="ExternalInput").ap()
            for name, a in arrays.items()]
    out = nc.dram_tensor("out_0_dram", (P, DC, T), F32, kind="ExternalOutput").ap()
    build(nc, *args, out)
    r = run_bass_kernel_spmd(nc, [{f"{name}_dram": a for name, a in arrays.items()}], core_ids=[0])
    got = r.results[0]["out_0_dram"]
    return np.ascontiguousarray(np.moveaxis(got, (0, 1, 2), (2, 1, 0)).reshape(1, T, D))
```

```python
from contextlib import ExitStack

import concourse.bass as bass
from concourse import mybir

F32 = mybir.dt.float32
F32R = mybir.dt.float32r
I32 = mybir.dt.int32
ALU = mybir.AluOpType
ACT = mybir.ActivationFunctionType
AX = mybir.AxisListType

P = 128
T = 256
TT = T // P
D = 1024
DC = D // P
LAYERS = 2
EPS = 1e-6
W = 512
HALF = 64
MQK, MROPE, MHEADS = 96, 32, 8
GROUPS, DHEADS = 3, 8
NEXP = 32
TOPK = 4
SLOTS = 64
MAXJOBS = 16
MASKED = -1.0e30
LRING = 2
PARTS = 3
RING = 4
MRING = 6
TILE = 8 * W

COL_AB, COL_AC, COL_AX, COL_AZ, COL_LORA = 0, 512, 1024, 1536, 2048
COL_BZ, COL_DQ, COL_DK, COL_DV, COL_CZ, COL_GATE = 2464, 2976, 4512, 6048, 7584, 8096
N_IN = 11168
LORA = 416
N_QKV = 2304

ADAS = 4
ADA_AFTER = {1: 1, 3: 2, 5: 3, 7: 4, 9: 5, 10: 6, 11: 7}
ADA_LOAD = {2: 1, 4: 2, 6: 3, 8: 4, 10: 5, 12: 6, 13: 7}
UNITS = [("ada", None, (0,))]
HEAD = len(UNITS)
LATENT = [("mq", None, (h, t)) for h in range(2) for t in range(TT)]
LATENT += [("mkv", None, (h, t)) for h in range(2) for t in range(TT)]
LONG = [("lora", ())] + [(kind, (g,)) for kind in ("dq", "dk", "dv") for g in range(GROUPS)]
LONG += [("z", (0,)), ("z", (1,))]
for n_, (kind, who) in enumerate(LONG):
    UNITS += [(kind, n_, (*who, t)) for t in range(TT)]
    if n_ >= 2 and LATENT:
        UNITS.append(LATENT.pop(0))
    if n_ in ADA_AFTER:
        UNITS.append(("ada", None, (ADA_AFTER[n_],)))
PREP = len(UNITS)
UNITS += [("ac", 12, (p,)) for p in range(2)]
UNITS += [("ax", 13, (p,)) for p in range(2)]
UNITS += [("ab", 14, (p,)) for p in range(2)]
UNITS += [("az", 15, (p,)) for p in range(2)]
UNITS += [("gate", 16 + n, (n, p)) for n in range(6) for p in range(2)]
FILL = len(UNITS)
UNITS += [("merge", 22 + b, (p, b)) for b in range(3) for p in range(4)]
MERGED = len(UNITS)
UNITS += [("out", 25 + n, (n, p)) for n in range(2) for p in range(2)]
NU = len(UNITS)
NT = 28
SPLIT = [(x[1], u) for u, x in enumerate(UNITS) if x[0] in ("lora", "dq", "dk", "dv", "z", "ac", "ax", "ab",
                                                            "az", "gate", "out") and x[2][-1] == 0]
NQ = 4 * len(SPLIT)
QUARTER = {u: 4 * i for i, (_, u) in enumerate(SPLIT)}
NQ_PREP, NQ_FILL = QUARTER[PREP], QUARTER[MERGED]
assert NQ % PARTS == 0
BANKS = 4
SHORT = [u for u, x in enumerate(UNITS) if x[0] in ("ada", "mq", "mkv")]
BANK = [BANKS + SHORT.index(u) % 2 if u in SHORT else (u - sum(v < u for v in SHORT)) % BANKS for u in range(NU)]
PER_BANK = (NU - len(SHORT)) // BANKS
assert (NU - len(SHORT)) % BANKS == 0 and len(SHORT) % 2 == 0 and NT % LRING == 0
NORMED = [u for u, x in enumerate(UNITS) if x[0] in ("lora", "dq", "mq", "mkv", "dk")]
NN = len(NORMED)
ZUNITS = [u for u, x in enumerate(UNITS) if x[0] in ("z", "az")]
TURN = {}
pending = []
for u in range(PREP):
    if u in QUARTER:
        for i_, v_ in enumerate(pending):
            TURN[u, 4 - len(pending) + i_] = v_
        pending = []
    if u in NORMED:
        pending.append(u)
assert not pending and len(TURN) == len(NORMED)
QN = 4

JOBS = [("mla", h) for h in range(MHEADS)] + [("dil", h, t) for h in range(DHEADS) for t in range(TT)]
NJ = len(JOBS)
ROUNDS = []
for job in JOBS:
    if job[0] == "mla":
        ROUNDS.append([[0, 1, 2]])
    elif job[2] == 0:
        ROUNDS.append([[0, 1, 2]])
    else:
        ROUNDS.append([[0, 1, 2], [3, 4, 5]])
NR = sum(map(len, ROUNDS))
FIRST_ROUND = [sum(map(len, ROUNDS[:j])) for j in range(NJ + 1)]
QUARTERS = [2] + [len(ROUNDS[j]) + (1 if j < 6 else 0) for j in range(NJ)]
assert sum(QUARTERS) == NQ_FILL - NQ_PREP
DONE_IN = [[PREP + u for u in range(FILL - PREP)
            if sum(QUARTERS[:s]) < 4 * (u // 2) + 4 <= sum(QUARTERS[:s + 1])] for s in range(NJ + 1)]
NM = NJ + 1
NTR = NN + NR
NS = NJ + 1

BUNITS = [("qa", 0, (t,)) for t in range(TT)]
BUNITS += [("ka", 1, (t,)) for t in (2, 3, 0, 1)]
BFIRST = len(BUNITS)
BUNITS += [("qb", 2, (t,)) for t in range(TT)]
BUNITS += [("kb", 3, (t,)) for t in range(2 * TT)]
BUNITS += [("vb", 4, (t,)) for t in range(2 * TT)]
BADA = len(BUNITS)
BUNITS += [("ada", 5 + n, (n,)) for n in range(4)]
BQKV = len(BUNITS)
BUNITS += [("out2", 9 + n, (n, p)) for n in range(2) for p in range(2)]
NBU = len(BUNITS)
LAG = 2
BTURNED = [u for u, x in enumerate(BUNITS) if x[0] in ("qa", "ka", "qb", "kb")]
BNORMED = [u for u, x in enumerate(BUNITS) if x[0] in ("qa", "ka")]
AHEADS, DIFFS = 8, 4
BJOBS = [("gqa", h, t) for h in range(AHEADS) for t in range(TT)]
BJOBS += [("diff", h, t) for h in range(DIFFS) for t in range(TT)]
NBJ = len(BJOBS)
BHALVES = [4] + [1] * NBJ
assert sum(BHALVES) == 2 * (BQKV - BFIRST)
BDONE_IN = [[BFIRST + u for u in range(BQKV - BFIRST) if sum(BHALVES[:s]) < 2 * u + 2 <= sum(BHALVES[:s + 1])]
            for s in range(NBJ + 1)]
BFLIPS = [("turn", u) for u in range(BFIRST)]
for s_ in range(1, NBJ + 1):
    BFLIPS.append(("job", s_ - 1))
    BFLIPS += [("turn", u) for u in BDONE_IN[s_ - 1] if u in BTURNED]
LAMBDA_INIT = 0.8 - 0.6 * 1.0
GLU_LIMIT = 7.0
GLU_ALPHA = 1.702
PAIRS = NEXP // 2

LAYER_PARAMS = dict(norm_g=DC, b_gate=3 * DC, conv_w=12, conv_b=4, q_a=2, kv_a=1, dil_q=3, dil_k=3,
                    mla_q=MQK, mla_k=MQK)
BLOCK_PARAMS = dict(b_ada=48, g_attn=DC, g_ffn=DC, g_final=DC, subln=1, gqa_q=HALF,
                    gqa_k=HALF, lam=4 * HALF, b_router=NEXP, w_router=DC * NEXP)
CONSTS = dict(ident=P, ones=P, cosm=2 * 32, sinm=2 * 32, mask=384, dist=GROUPS * 384, iota=2 * P,
              cosx=2 * 64, sinx=2 * 64, before=P, pick=2, expert=3 * NEXP, start=3 * NEXP, job=MAXJOBS)


def places(widths):
    at, out = 0, {}
    for name, n in widths.items():
        out[name] = (at, n)
        at += n
    return out, at


LP, NLP = places(LAYER_PARAMS)
BP, NBP = places(BLOCK_PARAMS)
CP, NCP = places(CONSTS)

CHAINED = dict(layer=177, pair=2, job=2)


def slope(g, h):
    return 2.0 ** (-8.0 * (g * DHEADS + h + 1) / (GROUPS * DHEADS))


def build(nc, c_in, xT, ctxT, consts, layer_params, block_params, w_in, w_uq, w_ukv, w_out_a, w_out_b, w_out_c,
          w_o, w_ada, w_qkv, w_o2, e_in, eb_in, e_out, eb_out, out, sizes=None, debug=None):
    PER = sizes or CHAINED
    with ExitStack() as ctx:
        def sb(name, shape, dt=F32):
            return ctx.enter_context(nc.sbuf_tensor(name, shape, dt))

        def sem(name):
            return ctx.enter_context(nc.semaphore(name))

        with ExitStack() as before_block:
            def early(name, shape, dt):
                return before_block.enter_context(nc.sbuf_tensor(name, shape, dt))

            early("loaded_tiles", [P, LRING * TILE], F32)
            w_hi = early("w_hi", [P, PARTS, 2, W], F32R)
            w_lo = early("w_lo", [P, PARTS, 2, W], F32R)
            h_lo = early("h_lo", [P, DC, T], F32R)
        assert 2 * PARTS * 2 * W + DC * T <= (RING - LRING) * TILE
        ring = sb("ring", [P, MRING, TILE])
        cst = sb("cst", [P, NCP])
        cvec = sb("cvec", [P, DC, 2])
        silu = sb("silu", [P, DC, 32])
        mod = sb("mod", [P, 48, 2])
        par = sb("par", [P, NLP])
        x = sb("x", [P, DC, T])
        with nc.sbuf_tensor("h_hi", [P, DC, T], F32R) as h_hi:
            pass
        h = sb("h", [P, DC, T])
        space = sb("space", [P, 20980])
        upper = ring[:, RING:MRING, :].rearrange("p s n -> p (s n)")
        gates = upper[:, 0:3 * DC * T].rearrange("p (c t) -> p c t", t=T)
        modrow = upper[:, 0:4 * W].rearrange("p (a n) -> p a n", n=W)
        w_uq_sb = upper[:, 4 * W:4 * W + 2 * 768].rearrange("p (c n) -> p c n", c=2)
        w_ukv_sb = upper[:, 4 * W + 2 * 768:4 * W + 2 * 768 + D]
        ada_sb = upper[:, 4608:4608 + DC * T].rearrange("p (c n) -> p c n", c=DC)
        conv = upper[:, 6144:7168].rearrange("p (c t) -> p c t", t=T)
        tanh_z = upper[:, 7168:7680]
        square = upper[:, 7680:8192]
        top = [0]

        def take(*shape):
            n = 1
            for s in shape:
                n *= s
            v = space[:, top[0]:top[0] + n]
            top[0] += n
            if len(shape) == 2:
                return v.rearrange("p (a b) -> p a b", b=shape[1])
            if len(shape) == 3:
                return v.rearrange("p (a b c) -> p a b c", b=shape[1], c=shape[2])
            return v

        ssum = take(8)
        var = take(8)
        rs = take(8)
        varx, rsx = square[:, 0:T], square[:, T:2 * T]
        stat = take(2, 8)
        mc = take(4, MQK)
        probs = take(2, 1024)
        turned = take(2, W)
        rope = probs[:, 0, :].rearrange("p (a n) -> p a n", a=2)
        cT = probs[:, 1, 0:3 * T].rearrange("p (a n) -> p a n", a=3)
        phase0 = top[0]
        kpe = take(TT, MROPE)
        dqT = take(12, T)
        dkT = take(12, T)
        dv = take(TT, 3 * W)
        mqT = take(MHEADS, T)
        mkT = take(MHEADS, T)
        mv = take(TT, W)
        at_y = top[0]
        yB = take(4, T)
        yC = take(4, T)
        up = take(4, T + 2)
        qn = space[:, at_y:at_y + QN * W].rearrange("p (a n) -> p a n", n=W)
        mtmp = square
        squares_x = merged_x = dv.rearrange("p a b -> p (a b)")[:, 0:DC * T].rearrange("p (c t) -> p c t", t=T)
        normed_x = dkT[:, 0:DC, :]
        assert top[0] <= 20980, top[0]
        top[0] = phase0
        bpar = take(NBP)
        bvarx = take(T)
        brsx = take(T)
        ctx_x = take(DC, T)
        assert top[0] <= phase0 + TT * MROPE + 24 * T
        bsquare = take(W)
        bqn = take(2, W)
        brope = take(2, W)
        hc = take(DC, T)
        top_qa = top[0]
        qaT = take(4, T)
        kaT = take(2, 2 * T)
        bmodrow = space[:, top_qa:top[0]].rearrange("p (a n) -> p a n", n=W)
        qbT = take(4, T)
        kbT = take(4, 2 * T)
        va = take(4, P)
        vb = take(4, W)
        mix = ctx_x
        gs = take(2, DC)
        kdup = take(2, 2 * HALF)
        lamt = take(2, HALF)
        lam = take(8)
        assert top[0] <= 20980, top[0]
        top[0] = phase0 + NBP + 2 * T
        hTM = take(TT, D)
        bin_sb = take(2 * D)
        xs = take(DC, P)
        onehot = take(2, SLOTS)
        sel = take(TT, P)
        selg = take(2, TT, P)
        spread0 = take(2, T)
        spread1 = take(2, T)
        glu = take(2, W)
        tanh_g = take(2, W)
        jt_at = top[0]
        lin = take(2, W)
        actT = take(2, W)
        ys = take(2, W)
        bout = take(D)
        logits = take(TT, NEXP)
        best = take(TT, 8)
        fill = take(TT, 8)
        ext = take(TT, 40)
        left = take(TT, 40)
        chosen = take(TT, NEXP)
        gate = take(TT, NEXP)
        gate_half = take(TT, NEXP)
        gateT = take(T)
        pos = take(TT, 40)
        gsum = take(TT, 4)
        cnt = take(NEXP)
        cand = take(2, 96)
        cand0 = take(96)
        jt = take(MAXJOBS, 96)
        jt2 = space[:, jt_at:jt_at + MAXJOBS * 96].rearrange("p (a b) -> p a b", b=96)
        jobe = take(MAXJOBS)
        jobs_ = take(MAXJOBS)
        posb = take(TT, 1)
        jobi = take(MAXJOBS + 1).bitcast(I32)
        assert top[0] <= 20980, top[0]

        def c_(name):
            a, n = CP[name]
            return cst[:, a:a + n]

        def l_(name, i=0, n=None):
            a, m = LP[name]
            return par[:, a + i:a + i + (n or m)]

        def b_(name, i=0, n=None):
            a, m = BP[name]
            return bpar[:, a + i:a + i + (n or m)]

        ident, ones = c_("ident"), c_("ones")

        bank = [ctx.enter_context(nc.psum_tensor(f"bank{i}", [P, W], F32)) for i in range(BANKS)]
        score = ctx.enter_context(nc.psum_tensor("score", [P, 2 * W], F32))
        flip = ctx.enter_context(nc.psum_tensor("flip", [P, W], F32))
        mixed = ctx.enter_context(nc.psum_tensor("mixed", [P, W], F32))

        loaded = sem("loaded")
        par_loaded = sem("par_loaded")
        uq_loaded = sem("uq_loaded")
        ada_landed = sem("ada_landed")
        par_ready = sem("par_ready")
        hi_done = sem("hi_done")
        lo_done = sem("lo_done")
        quarter_used = sem("quarter_used")
        stream_ready = sem("stream_ready")
        stream_hi = sem("stream_hi")
        landed = [sem(f"landed{i}") for i in range(RING)]
        squared = sem("squared")
        hready = sem("hready")
        unit_done = sem("unit_done")
        bank_free = [sem(f"bank_free{i}") for i in range(BANKS + 2)]
        scored = sem("scored")
        score_free = sem("score_free")
        flipped = sem("flipped")
        flip_free = sem("flip_free")
        mixed_done = sem("mixed_done")
        mixed_free = sem("mixed_free")
        squares = sem("squares")
        squares_used = sem("squares_used")
        copied = sem("copied")
        var_ready = sem("var_ready")
        rs_ready = sem("rs_ready")
        rsx_ready = sem("rsx_ready")
        qn_ready = sem("qn_ready")
        z_tanh = sem("z_tanh")
        masked = sem("masked")
        exped = sem("exped")
        probs_ready = sem("probs_ready")
        conv_ready = sem("conv_ready")
        chain = sem("chain")
        stored = sem("stored")
        asked = sem("asked")
        bpar_loaded = sem("bpar_loaded")
        ctanh = sem("ctanh")
        silu_ready = sem("silu_ready")
        bsquared = sem("bsquared")
        bvar = sem("bvar")
        broot = sem("broot")
        bh_ready = sem("bh_ready")
        bsquares = sem("bsquares")
        bvaru = sem("bvaru")
        brootu = sem("brootu")
        bqn_ready = sem("bqn_ready")
        lam_in = sem("lam_in")
        lam_exp = sem("lam_exp")
        bmasked = sem("bmasked")
        bexped = sem("bexped")
        bprobs = sem("bprobs")
        mix_ready = sem("mix_ready")
        logits_done = sem("logits_done")
        logitsT_ready = sem("logitsT_ready")
        chunk_ready = sem("chunk_ready")
        gate_in = sem("gate_in")
        gate_exp = sem("gate_exp")
        chosen_ready = sem("chosen_ready")
        pos_done = sem("pos_done")
        gateT_done = sem("gateT_done")
        gateT_ready = sem("gateT_ready")
        table_ready = sem("table_ready")
        mlanded = [sem(f"mlanded{i}") for i in range(MRING)]
        mused = sem("mused")
        sel_ready = sem("sel_ready")
        onehot_ready = sem("onehot_ready")
        selg_ready = sem("selg_ready")
        glu_done = sem("glu_done")
        glu_free = sem("glu_free")
        glu_in = sem("glu_in")
        glu_tanh = sem("glu_tanh")
        lin_done = sem("lin_done")
        lin_free = sem("lin_free")
        act_ready = sem("act_ready")
        eout_done = sem("eout_done")
        eout_free = sem("eout_free")
        scattered = sem("scattered")
        x_ready = sem("x_ready")
        final_ready = sem("final_ready")
        block = ctx.enter_context(nc.Block())

        def bank_of(u):
            return bank[BANK[u]] if BANK[u] < BANKS else (mixed, score[:, W:2 * W])[BANK[u] - BANKS]

        def free_of(u):
            return bank_free[BANK[u]]

        def freed(l, u):
            return l * sum(b == BANK[u] for b in BANK) + sum(b == BANK[u] for b in BANK[:u]) + 2

        def done(l, u):
            return (l + 1) * NU + u + 1

        def split_count(l, k):
            return (l + 1) * NQ + k + 1

        def used_count(l, k):
            return (l + 1) * (3 * NQ // 4) + 3 * (k // 4) + k % 4 + 1

        def first_flip(j):
            return NN + FIRST_ROUND[j]


        def bdone(u):
            return (LAYERS + 1) * NU + u + 1

        def bfreed(u):
            return LAYERS * PER_BANK + u // BANKS + 2

        SCORE0, FLIP0, MIXED0 = LAYERS * NS, LAYERS * NTR, LAYERS * NM
        S_JOBS, S_SUB = 2, 2 + NBJ
        S_FFN, S_FINAL = S_SUB + 1, S_SUB + 2
        F_TOK = len(BFLIPS)
        F_MOE = F_TOK + 4
        M_ADA, M_LOGITS, M_POS, M_GATE = NBJ, 1 + NBJ, 2 + NBJ, 3 + NBJ
        M_END = M_GATE + 1

        def score_left(s):
            s1 = s - S_JOBS
            alone = not 1 <= s1 < 2 * AHEADS
            return SCORE0 + s + (1 if alone else 0)

        def half_of(j):
            return j % 2 if BJOBS[j][0] == "gqa" else 0

        def block_sync(sp):
            sp.wait_ge(mixed_free, MIXED0 + 1)
            sp.dma_start(bpar, block_params).then_inc(bpar_loaded, 16)
            sp.dma_start(ctx_x, ctxT).then_inc(bpar_loaded, 16)
            sources = [(w_qkv, 0, W), (w_qkv, W, 256), (w_qkv, 768, W), (w_qkv, 1280, W), (w_qkv, 1792, W)]
            sources += [(w_ada, (LAYERS * 4 + n) * W, W) for n in range(4)]
            sources += [(w_o2, 0, W), (w_o2, W, W)]
            for n, (src, a, width) in enumerate(sources):
                if n >= RING:
                    last = max(u for u, x_ in enumerate(BUNITS) if x_[1] == n - RING)
                    sp.wait_ge(unit_done, bdone(last))
                else:
                    if n < LRING:
                        sp.wait_ge(lo_done, split_count(LAYERS - 1, NQ - 1))
                    else:
                        sp.wait_ge(unit_done, done(LAYERS - 1, NU - 1))
                sp.dma_start(ring[:, n % RING, :].rearrange("p (c n) -> p c n", c=DC)[:, :, 0:width],
                             columns(src, a, width)).then_inc(landed[n % RING], 16)

            def expert_tile(we, wo, j):
                rows_ = slice((j % 2) * W, (j % 2 + 1) * W)
                src = wo[rows_, :] if j >= 4 else we[rows_, (j // 2) * D:(j // 2 + 1) * D]
                sp.dma_start(ring[:, j, :].rearrange("p (c n) -> p c n", c=4),
                             src.rearrange("(c p) n -> p c n", p=P)).then_inc(mlanded[j], 16)

            def expert(e, m):
                we = e_in[bass.ds(e, 1)].rearrange("a k n -> (a k) n")
                wo = e_out[bass.ds(e, 1)].rearrange("a k n -> (a k) n")
                for j in range(MRING):
                    sp.wait_ge(mused, m * MRING + j + 1)
                    sp.sem_inc(asked, 1)
                    expert_tile(we, wo, j)

            assert (len(sources) - 2) % RING == 1
            for j in (4, 5, 3, 0, 1, 2):
                if j in (0, 3):
                    sp.wait_ge(unit_done, bdone(BQKV - 1))
                elif j in (1, 2):
                    sp.wait_ge(unit_done, bdone(NBU - 1))
                expert_tile(e_in[0], e_out[0], j)
            sp.wait_ge(mix_ready, 1)
            sp.dma_start(bout[0:NEXP, :], eb_out).then_inc(bpar_loaded, 16)
            sp.wait_ge(table_ready, 1)
            sp.dma_start(bin_sb[0:NEXP, :], eb_in).then_inc(bpar_loaded, 16)
            with sp.Fori(1, NEXP) as e:
                expert(e, e)
            sp.wait_ge(table_ready, 2)
            n_jobs = sp.value_load(jobi[0:1, MAXJOBS:MAXJOBS + 1], min_val=0, max_val=MAXJOBS)
            with sp.If(n_jobs > 0):
                with sp.Fori(0, n_jobs) as i:
                    e = sp.value_load(jobi[0:1, bass.ds(i, 1)], min_val=0, max_val=NEXP - 1)
                    expert(e, i + NEXP)
            for i in range(DC // 2):
                sp.wait_ge(final_ready, i + 1)
                sp.dma_start(out[:, 2 * i:2 * i + 2, :], h[:, 2 * i:2 * i + 2, :]).then_inc(stored, 16)
            sp.wait_ge(stored, 16 * (DC // 2))

        def ada_rows(pe, b, w8, parts):
            for k in parts:
                for g in range(4):
                    c = 4 * k + g
                    ins = pe.matmul(b[32 * g:32 * g + 32, :], silu[:, c, :], w8[:, c, :], start=k == 0, stop=k == 1,
                                    tile_position=(0, 32 * g))
            return ins

        def pick(pe, rows_, at):
            for m in range(4):
                ins = pe.matmul(mixed[:, at + 2 * m:at + 2 * m + 2], rows_[:, m * P:(m + 1) * P], c_("pick"),
                                start=True, stop=True)
            return ins

        def block_tensor(pe):
            pe.sem_inc(mused, MRING)

            def start(u):
                tl = BUNITS[u][1]
                before = LAYERS * 16 * NT // LRING if tl % RING < LRING else 0
                pe.wait_ge(landed[tl % RING], before + 16 * (tl // RING + 1))
                pe.wait_ge(bank_free[u % BANKS], bfreed(u) - 1)

            def place(u):
                return bank[u % BANKS], ring[:, BUNITS[u][1] % RING, :].rearrange("p (c n) -> p c n", c=DC)

            for s, src in ((0, h[:]), (1, hc)):
                pe.wait_ge(bsquared, s + 1)
                pe.wait_ge(score_free, score_left(s))
                for c in range(DC):
                    ins = pe.matmul(score[:, 0:T], ones, src[:, c, :], start=c == 0, stop=c == DC - 1)
                ins.then_inc(scored, 1)

            def project(u, parts=(0, 1)):
                kind, _, who = BUNITS[u]
                if 0 in parts:
                    start(u)
                b, w8 = place(u)
                if kind == "ada":
                    ins = ada_rows(pe, b, w8, parts)
                    if 1 in parts:
                        ins.then_inc(unit_done, 1)
                    return
                t = who[0]
                n = 256 if kind == "ka" else W
                if kind in ("qa", "qb"):
                    src, tt = h, t
                else:
                    src, tt = (hc, t) if t < TT else (h, t - TT)
                for c in range(4 * parts[0], 4 * parts[-1] + 4):
                    ins = pe.matmul(b[:, 0:n], src[:, c, tt * P:(tt + 1) * P], w8[:, c, 0:n], start=c == 0,
                                    stop=c == DC - 1)
                if 1 in parts:
                    ins.then_inc(unit_done, 1)

            def turn(u):
                r = BTURNED.index(u)
                pe.wait_ge(bqn_ready, r + 1)
                pe.wait_ge(flip_free, FLIP0 + BFLIPS.index(("turn", u)) + 1)
                for i in range(2 if BUNITS[u][0] == "ka" else 4):
                    ins = pe.transpose(flip[:, i * P:(i + 1) * P], bqn[:, r % 2, i * P:(i + 1) * P], ident)
                ins.then_inc(flipped, 1)

            for u in range(BFIRST + LAG):
                if u < BFIRST:
                    pe.wait_ge(bh_ready, 1 if u < 4 else 2)
                    project(u)
                if u >= LAG:
                    turn(u - LAG)
            pe.wait_ge(flip_free, FLIP0 + BFIRST + 1)

            bhalves = [0]

            def bfill():
                u, part = BFIRST + bhalves[0] // 2, bhalves[0] % 2
                bhalves[0] += 1
                project(u, (part,))

            def scores(j):
                kind, hd, t = BJOBS[j]
                pe.wait_ge(score_free, score_left(S_JOBS + j))
                cols = slice(t * P, (t + 1) * P)
                if kind == "gqa":
                    lo = HALF * (hd % 2)
                    o = score[:, W * half_of(j):W * half_of(j) + W]
                    ins = pe.matmul(o, qaT[lo:lo + HALF, hd // 2, cols], kaT[lo:lo + HALF, hd // 4, :],
                                    start=True, stop=True)
                else:
                    for cp in range(2):
                        lo = HALF * cp
                        ins = pe.matmul(score[:, W * cp:W * cp + W], qbT[lo:lo + HALF, hd, cols],
                                        kbT[lo:lo + HALF, hd, :], start=True, stop=True)
                ins.then_inc(scored, 1)

            def values(j):
                kind, hd, t = BJOBS[j]
                pe.wait_ge(bprobs, j + 1)
                f = FLIP0 + BFLIPS.index(("job", j))
                pe.wait_ge(flip_free, f + 1)
                for i in range(4):
                    ins = pe.transpose(flip[:, i * P:(i + 1) * P], probs[:, j % 2, i * P:(i + 1) * P], ident)
                ins.then_inc(flipped, 1)
                bfill()
                pe.wait_ge(flip_free, f + 2)
                pe.wait_ge(mixed_free, MIXED0 + j + 1)
                for i in range(4):
                    pt = turned[:, j % 2, i * P:(i + 1) * P]
                    if kind == "gqa":
                        lo = HALF * (hd % 2)
                        kv = hd // 4
                        ins = pe.matmul(mixed[lo:lo + HALF, 0:P], va[:, i, kv * HALF:(kv + 1) * HALF], pt,
                                        start=i == 0, stop=i == 3)
                    else:
                        ins = pe.matmul(mixed[:, 0:P], vb[:, i, hd * P:(hd + 1) * P], pt, start=i == 0, stop=i == 3)
                ins.then_inc(mixed_done, 1)

            for u in range(BFIRST):
                pe.wait_ge(bank_free[u % BANKS], bfreed(u))
            for j in range(NBJ + 1):
                if j < NBJ:
                    if j == 2 * AHEADS:
                        last = max(f for f, x_ in enumerate(BFLIPS) if x_[0] == "turn")
                        pe.wait_ge(flip_free, FLIP0 + last + 2)
                    scores(j)
                if j == 2 * AHEADS + 1:
                    for u in range(BADA - 4, BADA):
                        pe.wait_ge(bank_free[u % BANKS], bfreed(u))
                if j > 0:
                    values(j - 1)
                while bhalves[0] < sum(BHALVES[:j + 1]):
                    bfill()
                for u in BDONE_IN[j - 1] if j else ():
                    if u in BTURNED:
                        turn(u)
            pe.wait_ge(bsquared, 3)
            pe.wait_ge(score_free, score_left(S_SUB))
            for i in range(2):
                ins = pe.matmul(score[:, i * W:(i + 1) * W], ones, hc[:, 2 * i:2 * i + 2, :].rearrange("p a t -> p (a t)"),
                                start=True, stop=True)
            ins.then_inc(scored, 1)
            pe.wait_ge(mixed_free, MIXED0 + M_ADA + 1)
            for n in range(4):
                pe.wait_ge(bank_free[(BADA + n) % BANKS], bfreed(BADA + n))
                ins = pick(pe, bmodrow[:, n, :], 8 * n)
            ins.then_inc(mixed_done, 1)
            for part in range(2):
                if part:
                    pe.wait_ge(mix_ready, 1)
                for u in range(BQKV, NBU):
                    if part == 0:
                        start(u)
                    b, w8 = place(u)
                    for i in range(2):
                        m = (2 * BUNITS[u][2][1] + i) * P
                        for c in range(4 * part, 4 * part + 4):
                            ins = pe.matmul(b[:, i * T:(i + 1) * T], w8[:, c, m:m + P], mix[:, c, :],
                                            start=c == 0 and i == 0, stop=c == DC - 1, skip_group_check=True)
                    if part:
                        ins.then_inc(unit_done, 1)

            pe.wait_ge(score_free, score_left(S_FFN))
            for c in range(DC):
                if c % 2 == 0:
                    pe.wait_ge(bsquared, 4 + c // 2)
                ins = pe.matmul(score[:, 0:T], ones, h[:, c, :], start=c == 0, stop=c == DC - 1)
            ins.then_inc(scored, 1)
            pe.wait_ge(mixed_free, MIXED0 + M_LOGITS + 1)
            wr = b_("w_router").rearrange("p (c e) -> p c e", c=DC)
            for c in range(DC):
                pe.wait_ge(chunk_ready, c + 1)
                ins = pe.matmul(mixed[0:NEXP, 0:T], wr[:, c, :], h[:, c, :], start=c == 0, stop=c == DC - 1)
            ins.then_inc(mixed_done, 1)
            pe.wait_ge(logitsT_ready, 1)
            for t in range(TT):
                ins = pe.matmul(mixed[:, T + t * NEXP:T + (t + 1) * NEXP], gateT[0:NEXP, t * P:(t + 1) * P],
                                ident[0:NEXP, 0:NEXP], start=True, stop=True)
            ins.then_inc(logits_done, 1)
            for r in range(4):
                t, q = r // 2, r % 2
                pe.wait_ge(flip_free, FLIP0 + F_TOK + r + 1)
                for i in range(4):
                    ins = pe.transpose(flip[:, i * P:(i + 1) * P], h[:, 4 * q + i, t * P:(t + 1) * P], ident)
                ins.then_inc(flipped, 1)
            pe.wait_ge(chosen_ready, 1)
            pe.wait_ge(mixed_free, MIXED0 + M_POS + 1)
            pe.matmul(mixed[:, 0:32], c_("before"), chosen[:, 0, :], start=True, stop=True)
            pe.matmul(mixed[:, 32:64], c_("before"), chosen[:, 1, :], start=True, stop=False)
            pe.matmul(mixed[:, 32:64], ones, chosen[:, 0, :], start=False, stop=True)
            pe.matmul(mixed[:, 64:96], ones, chosen[:, 0, :], start=True, stop=False)
            pe.matmul(mixed[:, 64:96], ones, chosen[:, 1, :], start=False, stop=True).then_inc(mixed_done, 1)
            pe.wait_ge(gate_in, 2)
            pe.wait_ge(mixed_free, MIXED0 + M_GATE + 1)
            for t in range(TT):
                ins = pe.matmul(mixed[0:NEXP, t * P:(t + 1) * P], gate[:, t, :], ident, start=True, stop=True)
            ins.then_inc(mixed_done, 1)
            pe.wait_ge(mixed_free, MIXED0 + M_END + 1)
            pe.wait_ge(bpar_loaded, 64)
            for b in range(BANKS):
                pe.wait_ge(bank_free[b], bfreed(NBU - BANKS + b))
            for c in range(DC):
                pe.matmul(bank[c // 2][:, (c % 2) * T:(c % 2 + 1) * T], bout[0:NEXP, c * P:(c + 1) * P],
                          gateT[0:NEXP, :], start=c % 2 == 0, stop=False, skip_group_check=True)

            def gather(first_sel, first_flip_):
                pe.wait_ge(sel_ready, first_sel)
                for q in range(2):
                    pe.wait_ge(flip_free, first_flip_ + q)
                    for i in range(4):
                        c = 4 * q + i
                        for t in range(TT):
                            ins = pe.matmul(flip[:, i * P:(i + 1) * P], hTM[:, t, c * P:(c + 1) * P], sel[:, t, :],
                                            start=t == 0, stop=t == TT - 1)
                    ins.then_inc(flipped, 1)

            def expert_in(m, which, hh, biased=None):
                pe.wait_ge((glu_free, lin_free)[which], m + 1)
                for k in range(DC):
                    j = 2 * which + k // 4
                    if k % 4 == 0:
                        pe.wait_ge(mlanded[j], m * 16 + 16)
                    wk = ring[:, j, (k % 4) * D:(k % 4 + 1) * D]
                    for blk in range(2):
                        ins = pe.matmul(score[HALF * blk:HALF * blk + HALF, which * W:(which + 1) * W],
                                        xs[:, k, HALF * hh:HALF * hh + HALF], wk[:, blk * W:(blk + 1) * W],
                                        start=k == 0, stop=False)
                    if k % 4 == 3:
                        ins.then_inc(mused, 1)
                if biased is not None:
                    pe.wait_ge(onehot_ready, biased)
                for blk in range(2):
                    ins = pe.matmul(score[HALF * blk:HALF * blk + HALF, which * W:(which + 1) * W],
                                    onehot[:, hh, :], bin_sb[:, which * D + blk * W:which * D + (blk + 1) * W],
                                    start=False, stop=True)
                ins.then_inc((glu_done, lin_done)[which], 1)

            def expert_out(m, hh):
                pe.wait_ge(eout_free, m + 1)
                for k in range(DC):
                    j = 4 + k // 4
                    if k % 4 == 0:
                        pe.wait_ge(mlanded[j], m * 16 + 16)
                    wk = ring[:, j, (k % 4) * D:(k % 4 + 1) * D]
                    a0 = (k % 4) * P + HALF * (k // 4)
                    for blk in range(2):
                        ins = pe.matmul(mixed[HALF * blk:HALF * blk + HALF, :], actT[:, hh, a0:a0 + HALF],
                                        wk[:, blk * W:(blk + 1) * W], start=k == 0, stop=k == DC - 1)
                    if k == 3:
                        ins.then_inc(mused, 1)
                ins.then_inc(eout_done, 1)

            def turn_act(m, hh, f):
                pe.wait_ge(act_ready, m + 1)
                pe.wait_ge(flip_free, f)
                for i in range(4):
                    ins = pe.transpose(flip[:, i * P:(i + 1) * P], lin[:, hh, i * P:(i + 1) * P], ident)
                ins.then_inc(flipped, 1)
                pe.wait_ge(flip_free, f + 1)

            def turn_sel(hh, f):
                pe.wait_ge(flip_free, f)
                for t in range(TT):
                    ins = pe.transpose(flip[:, t * P:(t + 1) * P], selg[:, hh, t, :], ident)
                ins.then_inc(flipped, 1)

            def scatter(hh):
                for c in range(DC):
                    sp_ = (spread0, spread1)[c // 4]
                    ins = pe.matmul(bank[c // 2][:, (c % 2) * T:(c % 2 + 1) * T],
                                    ys[:, hh, (c % 4) * P:(c % 4 + 1) * P], sp_[:, hh, :], start=False, stop=False,
                                    skip_group_check=True)
                return ins

            pe.wait_ge(eout_free, 1)
            gather(1, FLIP0 + F_MOE + 1)
            pe.wait_ge(flip_free, FLIP0 + F_MOE + 3)
            base_f = FLIP0 + F_MOE + 2
            with pe.Fori(0, PAIRS) as i:
                expert_in(i * 2, 0, 0, i + 1)
                expert_in(i * 2, 1, 0)
                pe.wait_ge(eout_free, i * 2 + 1)
                scatter(1)
                pe.wait_ge(selg_ready, i + 1)
                turn_sel(0, i * 6 + base_f + 1)
                turn_sel(1, i * 6 + base_f + 2)
                turn_act(i * 2, 0, i * 6 + base_f + 3)
                expert_out(i * 2, 0)
                pe.wait_ge(eout_done, i * 2 + 1)
                pe.sem_inc(mused, 1)
                expert_in(i * 2 + 1, 0, 1)
                expert_in(i * 2 + 1, 1, 1)
                gather(i + 2, i * 6 + base_f + 4)
                pe.wait_ge(eout_free, i * 2 + 2)
                scatter(0)
                turn_act(i * 2 + 1, 1, i * 6 + base_f + 6)
                expert_out(i * 2 + 1, 1)
                pe.wait_ge(eout_done, i * 2 + 2)
                pe.sem_inc(mused, 1)
            pe.wait_ge(eout_free, NEXP + 1)
            scatter(1).then_inc(scattered, 1)
            base_f2 = base_f + 6 * PAIRS
            n_jobs = pe.value_load(jobi[0:1, MAXJOBS:MAXJOBS + 1], min_val=0, max_val=MAXJOBS)
            with pe.If(n_jobs > 0):
                with pe.Fori(0, n_jobs) as i:
                    pe.wait_ge(selg_ready, i + PAIRS + 1)
                    gather(i + PAIRS + 2, i * 4 + base_f2 + 1)
                    turn_sel(0, i * 4 + base_f2 + 3)
                    pe.wait_ge(flip_free, i * 4 + base_f2 + 4)
                    expert_in(i + NEXP, 0, 0, i + PAIRS + 1)
                    expert_in(i + NEXP, 1, 0)
                    turn_act(i + NEXP, 0, i * 4 + base_f2 + 4)
                    expert_out(i + NEXP, 0)
                    pe.wait_ge(eout_free, i + NEXP + 2)
                    pe.sem_inc(mused, 1)
                    scatter(0).then_inc(scattered, 1)
            for c in range(DC):
                if c % 2 == 0:
                    pe.wait_ge(bsquared, 8 + c // 2)
                ins = pe.matmul(score[:, 0:T], ones, h[:, c, :], start=c == 0, stop=c == DC - 1)
            ins.then_inc(scored, 1)

        def block_scalar(act):
            act.wait_ge(free_of(NU - 1), freed(LAYERS - 1, NU - 1))
            act.activation(h[:], x[:], ACT.Square).then_inc(bsquared, 1)
            act.wait_ge(bpar_loaded, 32)
            act.activation(hc, ctx_x, ACT.Square).then_inc(bsquared, 1)
            act.wait_ge(lam_in, 1)
            act.activation(lam[:, 2:4], lam[:, 0:2], ACT.Exp).then_inc(lam_exp, 1)

            def stream_root(n, s):
                act.wait_ge(bvar, n)
                act.activation(brsx, bvarx, ACT.Sqrt).then_inc(broot, 1)

            stream_root(1, 0)
            stream_root(2, 1)
            def evacuate_block(u):
                kind, _, who = BUNITS[u]
                b = bank[u % BANKS]
                if kind in ("qa", "ka"):
                    n = BNORMED.index(u)
                    act.wait_ge(unit_done, bdone(u))
                    if n:
                        act.wait_ge(bvaru, n)
                    w = W if kind == "qa" else P
                    act.activation(bsquare[:, 0:w], b[:, 0:w], ACT.Square).then_inc(bsquares, 1)
                    act.wait_ge(bvaru, n + 1)
                    act.activation(rs, var, ACT.Sqrt).then_inc(brootu, 1)
                elif kind == "vb":
                    act.wait_ge(unit_done, bdone(u))
                    act.activation(vb[:, who[0], :], b[:, :], ACT.Copy).then_inc(bank_free[u % BANKS], 1)
                elif kind == "ada":
                    act.wait_ge(unit_done, bdone(u))
                    act.activation(bmodrow[:, who[0], :], b[:, :], ACT.Copy).then_inc(bank_free[u % BANKS], 1)

            def unturn(u):
                kind, _, who = BUNITS[u]
                t = who[0]
                act.wait_ge(flipped, FLIP0 + BFLIPS.index(("turn", u)) + 1)
                v = flip[:, :].rearrange("p (a t) -> p a t", t=P)
                n = 2 if kind == "ka" else 4
                dst = dict(qa=qaT, ka=kaT, qb=qbT, kb=kbT)[kind][:, 0:n, t * P:(t + 1) * P]
                act.activation(dst, v[:, 0:n, :], ACT.Copy,
                               scale=HALF ** -0.5 if kind in ("qa", "qb") else 1.0).then_inc(flip_free, 1)

            for u in range(BFIRST + LAG):
                if u < BFIRST:
                    evacuate_block(u)
                if u >= LAG:
                    unturn(u - LAG)
            for j in range(NBJ + 1):
                if j > 0:
                    act.wait_ge(flipped, FLIP0 + BFLIPS.index(("job", j - 1)) + 1)
                    if j >= 3:
                        act.wait_ge(mixed_done, MIXED0 + j - 2)
                    act.activation(turned[:, (j - 1) % 2, :], flip[:, :], ACT.Copy).then_inc(flip_free, 1)
                if j < NBJ:
                    kind = BJOBS[j][0]
                    act.wait_ge(bmasked, j + 1)
                    if j >= 2:
                        act.wait_ge(flipped, FLIP0 + BFLIPS.index(("job", j - 2)) + 1)
                    st = stat[:, j % 2, :]
                    a = W * half_of(j)
                    ins = act.activation(probs[:, j % 2, 0:W], score[:, a:a + W], ACT.Exp, bias=st[:, 2:3],
                                         accum_out=st[:, 4:5])
                    if kind == "diff":
                        ins = act.activation(probs[:, j % 2, W:2 * W], score[:, W:2 * W], ACT.Exp, bias=st[:, 3:4],
                                             accum_out=st[:, 5:6])
                    ins.then_inc(score_free, 1)
                for u in BDONE_IN[j]:
                    evacuate_block(u)
                for u in BDONE_IN[j - 1] if j else ():
                    if u in BTURNED:
                        unturn(u)
            act.wait_ge(mixed_free, MIXED0 + NBJ + 1)
            act.activation(hc[:, 0:4, :], mix[:, 4:8, :], ACT.Square).then_inc(bsquared, 1)
            act.wait_ge(bvar, 3)
            act.activation(hc[:, 0:4, :], hc[:, 4:8, :], ACT.Sqrt).then_inc(broot, 1)
            for i, u in enumerate(range(BQKV, NBU)):
                act.wait_ge(bank_free[u % BANKS], bfreed(u))
                act.activation(h[:, 2 * i:2 * i + 2, :], x[:, 2 * i:2 * i + 2, :], ACT.Square).then_inc(bsquared, 1)
            stream_root(4, S_FFN)
            for r in range(4):
                t, q = r // 2, r % 2
                act.wait_ge(flipped, FLIP0 + F_TOK + r + 1)
                act.activation(hTM[:, t, q * W:(q + 1) * W], flip[:, :], ACT.Copy).then_inc(flip_free, 1)
            act.wait_ge(gate_in, 1)
            for t in range(TT):
                ins = act.activation(gate[:, t, :], ext[:, t, 0:NEXP], ACT.Exp, bias=gsum[:, t, 0:1])
            ins.then_inc(gate_exp, 1)

            def gathered(f):
                for q in range(2):
                    act.wait_ge(flipped, f + q)
                    act.activation(xs[:, 4 * q:4 * q + 4, :], flip[:, :].rearrange("p (a t) -> p a t", t=P),
                                   ACT.Copy).then_inc(flip_free, 1)

            def sel_turned(hh, f):
                act.wait_ge(flipped, f)
                act.activation(spread0[0:HALF, hh, :], flip[0:HALF, 0:T], ACT.Copy)
                act.activation(spread1[HALF:P, hh, :], flip[HALF:P, 0:T], ACT.Copy).then_inc(flip_free, 1)

            def tanh(m, hh):
                act.wait_ge(glu_free, m + 2)
                act.activation(tanh_g[:, hh, :], glu[:, hh, :], ACT.Tanh, scale=GLU_ALPHA / 2).then_inc(glu_tanh, 1)

            def act_turned(hh, f):
                act.wait_ge(flipped, f)
                act.activation(actT[:, hh, :], flip[:, :], ACT.Copy).then_inc(flip_free, 1)

            base_f = FLIP0 + F_MOE + 2
            gathered(FLIP0 + F_MOE + 1)
            with act.Fori(0, PAIRS) as i:
                tanh(i * 2, 0)
                sel_turned(0, i * 6 + base_f + 1)
                sel_turned(1, i * 6 + base_f + 2)
                act_turned(0, i * 6 + base_f + 3)
                tanh(i * 2 + 1, 1)
                gathered(i * 6 + base_f + 4)
                act_turned(1, i * 6 + base_f + 6)
            base_f2 = base_f + 6 * PAIRS
            n_jobs = act.value_load(jobi[0:1, MAXJOBS:MAXJOBS + 1], min_val=0, max_val=MAXJOBS)
            with act.If(n_jobs > 0):
                with act.Fori(0, n_jobs) as i:
                    gathered(i * 4 + base_f2 + 1)
                    sel_turned(0, i * 4 + base_f2 + 3)
                    tanh(i + NEXP, 0)
                    act_turned(0, i * 4 + base_f2 + 4)
            for i in range(DC // 2):
                act.wait_ge(x_ready, i + 1)
                act.activation(h[:, 2 * i:2 * i + 2, :], x[:, 2 * i:2 * i + 2, :], ACT.Square).then_inc(bsquared, 1)
            stream_root(5, S_FINAL)

        def block_vector(dve, link, steps, base):
            def to(shape, v, axis=1):
                return v.unsqueeze(axis).broadcast_to(shape)

            dve.wait_ge(bpar_loaded, 32)
            lv = b_("lam").rearrange("p (a n) -> p a n", a=4)
            for k in range(2):
                link(dve.tensor_tensor(lamt[:, k, :], lv[:, 2 * k, :], lv[:, 2 * k + 1, :], ALU.mult))
            dve.tensor_reduce(lam[:, 0:2], lamt, AX.X, ALU.add).then_inc(lam_in, 1)
            DONE_ADA = LAYERS * 4 * ADAS
            link(dve.tensor_tensor(mod[:, 0:DONE_ADA, :], mod[:, 0:DONE_ADA, :],
                                   to([P, DONE_ADA, 2], b_("b_ada", 0, DONE_ADA), 2), ALU.add))
            SH1, SC1, GT1, SH2, SC2, GT2 = (DC * i for i in range(6))

            def modulated(dst, src, n, gains, shift, scale_at, which, s, each=None):
                link(dve.scalar_tensor_tensor(out=gs[:, 0, :], in0=mod[:, scale_at:scale_at + DC, which], scalar=1.0,
                                              in1=gains, op0=ALU.add, op1=ALU.mult))
                dve.wait_ge(scored, SCORE0 + s + 1)
                dve.tensor_scalar(bvarx, score[:, 0:T], 1.0 / D, EPS, ALU.mult, ALU.add).then_inc(score_free, 1)
                dve.wait_ge(score_free, SCORE0 + s + 2)
                dve.sem_inc(bvar, 1)
                dve.wait_ge(broot, n)
                link(dve.reciprocal(brsx, brsx))
                groups = 1 if each is None else 2
                for g in range(groups):
                    chunks = range(g * DC // groups, (g + 1) * DC // groups)
                    for c in chunks:
                        ins = dve.scalar_tensor_tensor(out=dst[:, c, :], in0=src[:, c, :], scalar=gs[:, 0, c:c + 1],
                                                       in1=brsx, op0=ALU.mult, op1=ALU.mult)
                    link(ins)
                    for c in chunks:
                        ins = dve.tensor_scalar(dst[:, c, :], dst[:, c, :],
                                                mod[:, shift + c:shift + c + 1, which:which + 1].rearrange("p a b -> p (a b)"),
                                                None, ALU.add)
                        if each is not None:
                            ins.then_inc(each, 1)
                return ins

            modulated(h, x, 1, b_("g_attn"), SH1, SC1, 0, 0).then_inc(bh_ready, 1)
            modulated(hc, ctx_x, 2, b_("g_attn"), SH1, SC1, 1, 1).then_inc(bh_ready, 1)
            dve.wait_ge(lam_exp, 1)
            link(dve.tensor_tensor(lam[:, 4:5], lam[:, 3:4], lam[:, 2:3], ALU.subtract))
            link(dve.tensor_scalar(lam[:, 4:5], lam[:, 4:5], -LAMBDA_INIT, None, ALU.add))
            link(dve.tensor_scalar(b_("subln"), b_("subln"), 1.0 - LAMBDA_INIT, None, ALU.mult))

            def rotate(v, t):
                a = v.shape[1] // 2
                for ax in range(2):
                    def tab(name, hf):
                        at = t * 64 + ax * 32 + hf * 16
                        return c_(name)[:, at:at + 16].unsqueeze(1).broadcast_to([P, a, 16])
                    for hf in range(2):
                        s_ = v[:, ax::2, hf, :]
                        o_ = v[:, ax::2, 1 - hf, :]
                        r0 = brope[:, 0, :].rearrange("p (b n) -> p b n", n=16)[:, (2 * ax + hf) * 8:(2 * ax + hf) * 8 + a, :]
                        r1 = brope[:, 1, :].rearrange("p (b n) -> p b n", n=16)[:, (2 * ax + hf) * 8:(2 * ax + hf) * 8 + a, :]
                        dve.tensor_tensor(r0, s_, tab("cosx", hf), ALU.mult)
                        link(dve.tensor_tensor(r1, o_, tab("sinx", hf), ALU.mult))
                for ax in range(2):
                    for hf in range(2):
                        r0 = brope[:, 0, :].rearrange("p (b n) -> p b n", n=16)[:, (2 * ax + hf) * 8:(2 * ax + hf) * 8 + a, :]
                        r1 = brope[:, 1, :].rearrange("p (b n) -> p b n", n=16)[:, (2 * ax + hf) * 8:(2 * ax + hf) * 8 + a, :]
                        ins = dve.tensor_tensor(v[:, ax::2, hf, :], r0, r1, ALU.add)
                link(ins)

            def evacuate_block(u):
                kind, _, who = BUNITS[u]
                b = bank[u % BANKS]
                t = who[0]
                if kind in ("vb", "ada"):
                    return
                r = BTURNED.index(u)
                q = bqn[:, r % 2, :]
                xt = t if kind in ("qa", "qb") else t - TT
                if r >= 2:
                    dve.wait_ge(flipped, FLIP0 + BFLIPS.index(("turn", BTURNED[r - 2])) + 1)
                if kind in ("qa", "ka"):
                    n = BNORMED.index(u)
                    a = 8 if kind == "qa" else 2
                    dve.wait_ge(bsquares, n + 1)
                    link(dve.tensor_reduce(ssum[:, 0:a], bsquare[:, 0:a * HALF].rearrange("p (a b) -> p a b", b=HALF), AX.X,
                                           ALU.add))
                    dve.tensor_scalar(var[:, 0:a], ssum[:, 0:a], 1.0 / HALF, EPS, ALU.mult, ALU.add).then_inc(bvaru, 1)
                    dve.wait_ge(brootu, n + 1)
                    link(dve.reciprocal(rs, rs))
                    dst = q if kind == "qa" else kdup.rearrange("p a b -> p (a b)")[:, 0:P]
                    dv_ = dst.rearrange("p (a b) -> p a b", b=HALF)
                    if kind == "ka":
                        link(dve.tensor_copy(va[:, t, :], b[:, P:2 * P]))
                    dve.tensor_tensor(dv_, b[:, 0:a * HALF].rearrange("p (a b) -> p a b", b=HALF),
                                      to([P, a, HALF], rs[:, 0:a], 2), ALU.mult).then_inc(bank_free[u % BANKS], 1)
                    dve.wait_ge(bank_free[u % BANKS], bfreed(u))
                    g = b_("gqa_q" if kind == "qa" else "gqa_k")
                    link(dve.tensor_tensor(dv_, dv_, to([P, a, HALF], g), ALU.mult))
                else:
                    dst = q
                    dve.wait_ge(unit_done, bdone(u))
                    dve.tensor_copy(q, b[:, :]).then_inc(bank_free[u % BANKS], 1)
                    dve.wait_ge(bank_free[u % BANKS], bfreed(u))
                if xt >= 0:
                    rotate(dst.rearrange("p (a two n) -> p a two n", two=2, n=16), xt)
                if kind == "ka":
                    kd = kdup.rearrange("p a b -> p (a b)")[:, 0:P].rearrange("p (a b) -> p a b", b=HALF)
                    for cp in range(2):
                        ins = dve.tensor_copy(q[:, 0:256].rearrange("p (a two b) -> p a two b", two=2, b=HALF)[:, :, cp, :],
                                              kd)
                    link(ins)
                dve.sem_inc(bqn_ready, 1)

            for u in range(BFIRST):
                evacuate_block(u)
            for j in range(NBJ + 1):
                if j < NBJ:
                    kind, hd, t = BJOBS[j]
                    st = stat[:, j % 2, :]
                    dve.wait_ge(scored, SCORE0 + S_JOBS + j + 1)
                    a = W * half_of(j)
                    if kind == "gqa":
                        link(dve.tensor_reduce(st[:, 0:1], score[:, a:a + W], AX.X, ALU.max))
                        dve.tensor_scalar(st[:, 2:3], st[:, 0:1], -1.0, None, ALU.mult).then_inc(bmasked, 1)
                    else:
                        link(dve.tensor_reduce(st[:, 0:2], score[:, :].rearrange("p (a n) -> p a n", a=2), AX.X, ALU.max))
                        dve.tensor_scalar(st[:, 2:4], st[:, 0:2], -1.0, None, ALU.mult).then_inc(bmasked, 1)
                for u in BDONE_IN[j - 1] if j else ():
                    evacuate_block(u)
                if j < NBJ:
                    kind, hd, t = BJOBS[j]
                    pr, st = probs[:, j % 2, :], stat[:, j % 2, :]
                    dve.wait_ge(score_free, SCORE0 + S_JOBS + j + 2)
                    if kind == "gqa":
                        link(dve.reciprocal(st[:, 6:7], st[:, 4:5]))
                        dve.tensor_scalar(pr[:, 0:W], pr[:, 0:W], st[:, 6:7], None, ALU.mult).then_inc(bprobs, 1)
                    else:
                        link(dve.reciprocal(st[:, 6:8], st[:, 4:6]))
                        link(dve.tensor_tensor(st[:, 7:8], st[:, 7:8], lam[:, 4:5], ALU.mult))
                        link(dve.tensor_scalar(pr[:, 0:W], pr[:, 0:W], st[:, 6:7], None, ALU.mult))
                        dve.scalar_tensor_tensor(out=pr[:, 0:W], in0=pr[:, W:2 * W], scalar=st[:, 7:8], in1=pr[:, 0:W],
                                                 op0=ALU.mult, op1=ALU.add).then_inc(bprobs, 1)
                if j > 0:
                    kind, hd, t = BJOBS[j - 1]
                    lo = HALF * (hd % 2)
                    dve.wait_ge(mixed_done, MIXED0 + j)
                    cols = slice(t * P, (t + 1) * P)
                    if kind == "gqa":
                        dve.tensor_copy(mix[lo:lo + HALF, hd // 2, cols], mixed[lo:lo + HALF, 0:P]).then_inc(mixed_free, 1)
                    else:
                        dve.tensor_copy(mix[:, 4 + hd, cols], mixed[:, 0:P]).then_inc(mixed_free, 1)
            dve.wait_ge(scored, SCORE0 + S_SUB + 1)
            dve.tensor_scalar(hc[:, 4:8, :].rearrange("p a t -> p (a t)"), score[:, :], 1.0 / P, EPS, ALU.mult,
                              ALU.add).then_inc(score_free, 1)
            dve.wait_ge(score_free, SCORE0 + S_SUB + 2)
            dve.sem_inc(bvar, 1)
            dve.wait_ge(broot, 3)
            link(dve.reciprocal(hc[:, 0:4, :], hc[:, 0:4, :]))
            m4 = mix[:, 4:8, :].rearrange("p a t -> p (a t)")
            dve.scalar_tensor_tensor(out=m4, in0=m4, scalar=b_("subln"), in1=hc[:, 0:4, :].rearrange("p a t -> p (a t)"),
                                     op0=ALU.mult, op1=ALU.mult).then_inc(mix_ready, 1)
            dve.wait_ge(mixed_done, MIXED0 + M_ADA + 1)
            dve.tensor_tensor(mod[:, DONE_ADA:48, :], mixed[:, 0:32].rearrange("p (c b) -> p c b", b=2),
                              to([P, 16, 2], b_("b_ada", DONE_ADA, 16), 2), ALU.add).then_inc(mixed_free, 1)
            dve.wait_ge(mixed_free, MIXED0 + M_ADA + 2)
            for u in range(BQKV, NBU):
                n, p = BUNITS[u][2]
                dve.wait_ge(unit_done, bdone(u))
                for i in range(2):
                    c = 4 * n + 2 * p + i
                    ins = dve.scalar_tensor_tensor(out=x[:, c, :], in0=bank[u % BANKS][:, i * T:(i + 1) * T],
                                                   scalar=mod[:, GT1 + c, 0:1], in1=x[:, c, :], op0=ALU.mult,
                                                   op1=ALU.add)
                ins.then_inc(bank_free[u % BANKS], 1)
            if debug == "attention":
                return

            dve.wait_ge(unit_done, bdone(NBU - 1))
            for v in (bin_sb, pos, ext, ys, spread0, spread1, sel):
                ins = dve.memset(v, -1.0 if v is pos else -2.0 ** 126 if v is ext else 0.0)
            link(ins)
            dve.sem_inc(table_ready, 1)
            modulated(h, x, 4, b_("g_ffn"), SH2, SC2, 0, S_FFN, chunk_ready)
            dve.wait_ge(mixed_done, MIXED0 + M_LOGITS + 1)
            dve.tensor_copy(gateT[0:NEXP, :], mixed[0:NEXP, 0:T]).then_inc(logitsT_ready, 1)
            dve.wait_ge(logits_done, 1)
            dve.tensor_tensor(ext[:, :, 0:NEXP], mixed[:, T:T + 2 * NEXP].rearrange("p (a e) -> p a e", a=2),
                              to([P, TT, NEXP], b_("b_router")), ALU.add).then_inc(mixed_free, 1)
            dve.wait_ge(mixed_free, MIXED0 + M_LOGITS + 2)
            for t in range(TT):
                link(dve.max(best[:, t, :], ext[:, t, 0:NEXP]))
            link(dve.memset(fill, -2.0 ** 126))
            link(dve.tensor_copy(fill[:, :, 0:TOPK], best[:, :, 0:TOPK]))
            for t in range(TT):
                link(dve.match_replace(left[:, t, :], fill[:, t, :], ext[:, t, :], -2.0 ** 127))
            dve.tensor_scalar(chosen, left[:, :, 0:NEXP], -1.5 * 2.0 ** 126, None, ALU.is_lt).then_inc(chosen_ready, 1)
            dve.wait_ge(chosen_ready, 1)
            dve.tensor_scalar(gsum[:, :, 0:1], best[:, :, 0:1], -1.0, None, ALU.mult).then_inc(gate_in, 1)
            dve.wait_ge(gate_exp, 1)
            link(dve.tensor_tensor(gate, gate, chosen, ALU.mult))
            link(dve.tensor_reduce(gsum[:, :, 1], gate, AX.X, ALU.add))
            link(dve.reciprocal(gsum[:, :, 2], gsum[:, :, 1]))
            link(dve.tensor_tensor(gate, gate, to([P, TT, NEXP], gsum[:, :, 2], 2), ALU.mult))
            dve.tensor_scalar(gate_half, gate, 0.5, None, ALU.mult).then_inc(gate_in, 1)
            dve.wait_ge(mixed_done, MIXED0 + M_POS + 1)
            link(dve.tensor_copy(cnt, mixed[:, 64:96]))
            pv = pos[:, :, 0:NEXP]
            dve.scalar_tensor_tensor(out=pv, in0=mixed[:, 0:64].rearrange("p (a e) -> p a e", a=2), scalar=1.0,
                                     in1=chosen, op0=ALU.add, op1=ALU.mult).then_inc(mixed_free, 1)
            dve.wait_ge(mixed_free, MIXED0 + M_POS + 2)
            link(dve.tensor_scalar(pv, pv, -1.0, None, ALU.add))
            dve.wait_ge(mixed_done, MIXED0 + M_GATE + 1)
            dve.tensor_copy(gateT[0:NEXP, :], mixed[0:NEXP, 0:T]).then_inc(mixed_free, 1)
            dve.wait_ge(gate_in, 2)

            def column(v, t, e):
                return v[:, t, bass.ds(e, 1)]

            iota = c_("iota")

            def select(hh, e):
                for t in range(TT):
                    ins = dve.tensor_scalar(sel[:, t, HALF * hh:HALF * hh + HALF], iota[:, 0:HALF], column(pos, t, e),
                                            None, ALU.is_equal)
                return ins

            select(0, 0)
            select(1, 1).then_inc(sel_ready, 1)
            for s_ in (glu_free, lin_free, eout_free):
                dve.sem_inc(s_, 1)
            for b in range(3):
                ins = dve.tensor_scalar(cand0[:, b * NEXP:(b + 1) * NEXP], cnt, SLOTS * (b + 1) + 0.5, None, ALU.is_gt)
            link(ins)
            src, s = cand0, 1
            k = 0
            while s < 96:
                dst = cand[:, k % 2, :]
                dve.tensor_copy(dst[:, 0:s], src[:, 0:s])
                link(dve.tensor_tensor(dst[:, s:96], src[:, s:96], src[:, 0:96 - s], ALU.add))
                src, s, k = dst, 2 * s, k + 1
            link(dve.tensor_copy(jobi[:, MAXJOBS:MAXJOBS + 1], src[:, 95:96]))
            link(dve.tensor_tensor(cand0, cand0, src, ALU.mult))
            jshape = [P, MAXJOBS, 96]
            link(dve.tensor_tensor(jt, to(jshape, cand0), to(jshape, c_("job"), 2), ALU.is_equal))
            for name, dst in (("expert", jobe), ("start", jobs_)):
                link(dve.tensor_tensor(jt2, jt, to(jshape, c_(name)), ALU.mult))
                link(dve.tensor_reduce(dst, jt2, AX.X, ALU.add))
            link(dve.tensor_copy(jobi[:, 0:MAXJOBS], jobe))
            dve.sem_inc(table_ready, 1)
            mark = steps[0]
            dve.wait_ge(bpar_loaded, 64)

            def onehots(hh, e):
                return dve.tensor_copy(onehot[:, hh, :], ident[:, bass.ds(e, 1)].broadcast_to([P, SLOTS]))

            def gates_of(hh, e, where):
                for t in range(TT):
                    ins = dve.tensor_scalar(selg[:, hh, t, :], iota[:, 0:P], where(t), column(gate_half, t, e),
                                            ALU.is_equal, ALU.mult)
                return ins

            def activate(m, hh):
                dve.wait_ge(glu_done, m + 1)
                dve.tensor_scalar(glu[:, hh, :], score[:, 0:W], GLU_LIMIT, None, ALU.min).then_inc(glu_free, 1)
                dve.wait_ge(glu_tanh, m + 1)
                link(dve.scalar_tensor_tensor(out=glu[:, hh, :], in0=tanh_g[:, hh, :], scalar=1.0, in1=glu[:, hh, :],
                                              op0=ALU.add, op1=ALU.mult))
                dve.wait_ge(lin_done, m + 1)
                dve.tensor_scalar(lin[:, hh, :], score[:, W:2 * W], GLU_LIMIT, -GLU_LIMIT, ALU.min,
                                  ALU.max).then_inc(lin_free, 1)
                dve.wait_ge(lin_free, m + 2)
                dve.scalar_tensor_tensor(out=lin[:, hh, :], in0=lin[:, hh, :], scalar=1.0, in1=glu[:, hh, :],
                                         op0=ALU.add, op1=ALU.mult).then_inc(act_ready, 1)

            def expert_rows(m, hh):
                dve.wait_ge(eout_done, m + 1)
                dve.tensor_copy(ys[:, hh, :], mixed[:, :]).then_inc(eout_free, 1)

            with dve.Fori(0, PAIRS) as i:
                base[0] = i * PER["pair"] + mark
                steps[0] = 0
                onehots(0, i * 2)
                onehots(1, i * 2 + 1).then_inc(onehot_ready, 1)
                gates_of(0, i * 2, lambda t: column(pos, t, i * 2))
                gates_of(1, i * 2 + 1, lambda t: column(pos, t, i * 2 + 1)).then_inc(selg_ready, 1)
                activate(i * 2, 0)
                select(0, i * 2 + 2)
                select(1, i * 2 + 3).then_inc(sel_ready, 1)
                expert_rows(i * 2, 0)
                activate(i * 2 + 1, 1)
                expert_rows(i * 2 + 1, 1)
                assert steps[0] == PER["pair"], steps[0]
            mark2 = mark + PAIRS * PER["pair"]
            n_jobs = dve.value_load(jobi[0:1, MAXJOBS:MAXJOBS + 1], min_val=0, max_val=MAXJOBS)
            with dve.If(n_jobs > 0):
                with dve.Fori(0, n_jobs) as i:
                    base[0] = i * PER["job"] + mark2
                    steps[0] = 0
                    e = dve.value_load(jobi[0:1, bass.ds(i, 1)], min_val=0, max_val=NEXP - 1)
                    dve.wait_ge(scattered, i + 1)
                    for t in range(TT):
                        ins = dve.tensor_tensor(posb[:, t, :], column(pos, t, e), jobs_[:, bass.ds(i, 1)], ALU.subtract)
                    link(ins)
                    onehots(0, e).then_inc(onehot_ready, 1)
                    gates_of(0, e, lambda t: posb[:, t, 0:1]).then_inc(selg_ready, 1)
                    for t in range(TT):
                        ins = dve.tensor_scalar(sel[:, t, 0:HALF], iota[:, 0:HALF], posb[:, t, 0:1], None, ALU.is_equal)
                    ins.then_inc(sel_ready, 1)
                    activate(i + NEXP, 0)
                    expert_rows(i + NEXP, 0)
                    assert steps[0] == PER["job"], steps[0]
            dve.wait_ge(scattered, n_jobs + 1)
            for c in range(DC):
                ins = dve.scalar_tensor_tensor(out=x[:, c, :], in0=bank[c // 2][:, (c % 2) * T:(c % 2 + 1) * T],
                                               scalar=mod[:, GT2 + c, 0:1], in1=x[:, c, :], op0=ALU.mult, op1=ALU.add)
                if c % 2 == 1:
                    ins.then_inc(x_ready, 1)
            dve.wait_ge(scored, SCORE0 + S_FINAL + 1)
            dve.tensor_scalar(bvarx, score[:, 0:T], 1.0 / D, EPS, ALU.mult, ALU.add).then_inc(bvar, 1)
            dve.wait_ge(broot, 5)
            dve.reciprocal(brsx, brsx).then_inc(bh_ready, 1)
            dve.wait_ge(bh_ready, 3)
            for c in range(DC):
                ins = dve.scalar_tensor_tensor(out=h[:, c, :], in0=x[:, c, :], scalar=b_("g_final", c, 1), in1=brsx,
                                               op0=ALU.mult, op1=ALU.mult)
                if c % 2 == 1:
                    ins.then_inc(final_ready, 1)

        def columns(weights, a, n):
            return weights[:, a:a + n].rearrange("(c p) n -> p c n", p=P)

        @block.sync
        def _(sp):
            for dst, src in ((cst[:], consts), (cvec[:].rearrange("p c b -> p (c b)"), c_in), (x[:], xT)):
                sp.dma_start(dst, src).then_inc(loaded, 16)

            def slot_free(l, n):
                m = (n - LRING) % NT
                if m == NT - 1:
                    m -= LRING
                layer = l - 1 if n < LRING else l
                split = [u for tl, u in SPLIT if tl == m]
                if split:
                    sp.wait_ge(lo_done, split_count(layer, QUARTER[split[0]] + 3))
                else:
                    sp.wait_ge(unit_done, done(layer, max(u for u, x_ in enumerate(UNITS) if x_[1] == m)))
                sp.sem_inc(asked, 1)

            def tile(l, n, dst, src):
                slot_free(l, n)
                sp.dma_start(dst, src).then_inc(landed[n % LRING], 16)

            def slot(n):
                return ring[:, n % LRING, :].rearrange("p (c n) -> p c n", c=DC)

            with sp.Fori(0, LAYERS) as l:
                wl = w_in[bass.ds(l, 1)].rearrange("a k n -> (a k) n")
                starts = [COL_LORA] + [a + g * W for a in (COL_DQ, COL_DK, COL_DV) for g in range(GROUPS)]
                starts += [COL_BZ, COL_CZ, COL_AC, COL_AX, COL_AB, COL_AZ] + [COL_GATE + i * W for i in range(6)]

                def ada_half(n):
                    before = done(l, UNITS.index(("ada", None, (n - 1,)))) if n else done(l - 1, NU - 1)
                    sp.wait_ge(unit_done, before)
                    sp.sem_inc(asked, 1)
                    sp.dma_start(ada_sb, w_ada[:, bass.ds(l * 4 * W + n * T, T)].rearrange("(c p) n -> p c n", p=P)
                                 ).then_inc(ada_landed, 16)

                for n, a in enumerate(starts):
                    if n in ADA_LOAD:
                        ada_half(ADA_LOAD[n])
                    width = W if n else LORA
                    tile(l, n, slot(n)[:, :, 0:width], columns(wl, a, width))
                    if n == 1:
                        sp.wait_ge(unit_done, done(l - 1, NU - 1))
                        sp.sem_inc(asked, 1)
                        sp.dma_start(par[:, :], layer_params[:, bass.ds(l, 1), :].rearrange("p a n -> p (a n)")).then_inc(par_loaded, 16)
                        ada_half(0)
                        sp.dma_start(w_uq_sb, w_uq[bass.ds(l, 1)].rearrange("a (c p) n -> p (a c) n", p=P)).then_inc(uq_loaded, 16)
                        sp.dma_start(w_ukv_sb, w_ukv[bass.ds(l, 1)].rearrange("a p n -> p (a n)")).then_inc(uq_loaded, 16)
                for b, wb in enumerate((w_out_a, w_out_b, w_out_c)):
                    tile(l, 22 + b, ring[:, (22 + b) % LRING, :].rearrange("p (c n) -> p c n", c=4),
                         wb[bass.ds(l, 1)].rearrange("a (c p) n -> p (a c) n", p=P))
                wol = w_o[bass.ds(l, 1)].rearrange("a k n -> (a k) n")
                for n in range(2):
                    tile(l, 25 + n, slot(25 + n), columns(wol, n * W, W))
                slot_free(l, NT - 1)
                sp.sem_inc(landed[(NT - 1) % LRING], 16)
            if debug == "layers":
                for b in range(BANKS):
                    sp.wait_ge(bank_free[b], LAYERS * PER_BANK + 1)
                sp.dma_start(out, x[:]).then_inc(stored, 16)
                sp.wait_ge(stored, 16)
            else:
                block_sync(sp)

        @block.tensor
        def _(pe):
            pe.wait_ge(loaded, 48)
            pe.wait_ge(silu_ready, 1)
            pe.sem_inc(unit_done, NU)
            pe.sem_inc(quarter_used, 3 * NQ // 4)

            def bank_left(l, u):
                pe.wait_ge(free_of(u), freed(l, u) - 1)

            def unit(l, u):
                kind, tl, who = UNITS[u]
                bank_left(l, u)
                b = bank_of(u)
                if tl is not None:
                    pe.wait_ge(landed[tl % LRING], l * (16 * NT // LRING) + 16 * (tl // LRING + 1))
                    w4 = ring[:, tl % LRING, :].rearrange("p (c n) -> p c n", c=4)
                if kind == "ada":
                    pe.wait_ge(ada_landed, l * (32 * ADAS) + 16 * (who[0] + 1))
                    ins = ada_rows(pe, b[:, 0:T], ada_sb, (0, 1))
                elif kind == "mq":
                    half, t = who
                    pe.wait_ge(uq_loaded, l * 32 + 32)
                    for c in range(2):
                        ins = pe.matmul(b[:, 0:384], cT[:, c, t * P:(t + 1) * P],
                                        w_uq_sb[:, c, half * 384:(half + 1) * 384], start=c == 0, stop=c == 1)
                elif kind == "mkv":
                    half, t = who
                    ins = pe.matmul(b[:, :], cT[:, 2, t * P:(t + 1) * P], w_ukv_sb[:, half * W:(half + 1) * W],
                                    start=True, stop=True)
                else:
                    p, br = who
                    y = (conv, yB, yC)[br]
                    for i in range(2):
                        m = (2 * p + i) * P
                        for c in range(4):
                            ins = pe.matmul(b[:, i * T:(i + 1) * T], w4[:, c, m:m + P], y[:, c, :],
                                            start=c == 0, stop=c == 3)
                ins.then_inc(unit_done, 1)

            def quarter(l, u, q):
                kind = UNITS[u][0]
                k = QUARTER[u] + q
                if q == 0:
                    bank_left(l, u)
                    bank_left(l, u + 1)
                pe.wait_ge(lo_done, split_count(l, k))
                if kind in ("lora", "out") and q % 2 == 0:
                    pe.wait_ge(hready, l * 4 + (0 if kind == "lora" else 2) + q // 2 + 1)
                n = LORA if kind == "lora" else W
                for who in range(2):
                    b = bank_of(u + who)
                    if kind in ("lora", "dq", "dk", "dv"):
                        t = slice(who * P, (who + 1) * P)
                        for i in range(2):
                            c = 2 * q + i
                            for x_, w_ in ((h_hi, w_hi), (h_hi, w_lo), (h_lo, w_hi)):
                                ins = pe.matmul(b[:, 0:n], x_[:, c, t], w_[:, k % PARTS, i, 0:n],
                                                start=c == 0 and x_ is h_hi and w_ is w_hi,
                                                stop=c == DC - 1 and x_ is h_lo)
                    else:
                        for half in range(2):
                            m = (2 * who + half) * P
                            for i in range(2):
                                c = 2 * q + i
                                for x_, w_ in ((h_hi, w_hi), (h_lo, w_hi), (h_hi, w_lo)):
                                    ins = pe.matmul(b[:, half * T:(half + 1) * T], w_[:, k % PARTS, i, m:m + P],
                                                    x_[:, c, :],
                                                    start=c == 0 and half == 0 and x_ is h_hi and w_ is w_hi,
                                                    stop=c == DC - 1 and w_ is w_lo, skip_group_check=True)
                    if q == 3:
                        ins.then_inc(unit_done, 1)
                if q < 3:
                    ins.then_inc(quarter_used, 1)

            def turn(l, u):
                kind = UNITS[u][0]
                n = NORMED.index(u)
                pe.wait_ge(qn_ready, l * NN + n + 1)
                pe.wait_ge(flip_free, l * NTR + n + 1)
                src = qn[:, n % QN, :]
                if kind == "lora":
                    blocks = [(P, src[:, i * P:(i + 1) * P]) for i in range(3)]
                elif kind in ("dq", "dk"):
                    blocks = [(P, src[:, i * P:(i + 1) * P]) for i in range(4)]
                else:
                    blocks = [(MQK, src[:, i * MQK:(i + 1) * MQK]) for i in range(4)]
                for i, (m, blk) in enumerate(blocks):
                    ins = pe.transpose(flip[0:m, i * P:(i + 1) * P], blk, ident)
                ins.then_inc(flipped, 1)

            taken = [0]

            def fill(l):
                quarter(l, PREP + 2 * (taken[0] // 4), taken[0] % 4)
                taken[0] += 1

            def scores(l, j):
                pe.wait_ge(score_free, l * NS + j + 2)
                job = JOBS[j]
                if job[0] == "mla":
                    q, k = mqT[0:MQK, job[1], :], mkT[0:MQK, job[1], :]
                    pe.matmul(score[:, 0:P], q[:, 0:P], k[:, 0:P], start=True, stop=True)
                    ins = pe.matmul(score[:, P:P + T], q[:, P:T], k, start=True, stop=True)
                else:
                    _, hd, t = job
                    n = (t + 1) * P
                    lo = HALF * (hd % 2)
                    for g in range(GROUPS):
                        q = dqT[lo:lo + HALF, g * 4 + hd // 2, t * P:(t + 1) * P]
                        k = dkT[lo:lo + HALF, g * 4 + hd // 2, 0:n]
                        ins = pe.matmul(score[:, g * n:(g + 1) * n], q, k, start=True, stop=True)
                ins.then_inc(scored, 1)

            def values(l, j):
                job = JOBS[j]
                hd = job[1]
                lo = HALF * (hd % 2)
                pe.wait_ge(probs_ready, l * NJ + j + 1)
                pe.wait_ge(mixed_free, l * NM + j + 2)
                blocks = 3 if job[0] == "mla" or job[2] == 0 else 6
                for r, cols in enumerate(ROUNDS[j]):
                    fr = first_flip(j) + r
                    pe.wait_ge(flip_free, l * NTR + fr + 1)
                    for i, c in enumerate(cols):
                        ins = pe.transpose(flip[:, i * P:(i + 1) * P], probs[:, j % 2, c * P:(c + 1) * P], ident)
                    ins.then_inc(flipped, 1)
                    fill(l)
                    pe.wait_ge(flip_free, l * NTR + fr + 2)
                    pt = turned[:, (FIRST_ROUND[j] + r) % 2, :]
                    for i, c in enumerate(cols):
                        if job[0] == "mla":
                            o = mixed[lo:lo + HALF, (0, P, P)[c]:(0, P, P)[c] + P]
                            v = mv[:, (0, 0, 1)[c], hd * HALF:(hd + 1) * HALF]
                            first, last = c < 2, c != 1
                        else:
                            t = job[2]
                            g, kt = c // (t + 1), c % (t + 1)
                            o = mixed[lo:lo + HALF, 0:P]
                            v = dv[:, kt, g * W + hd * HALF:g * W + (hd + 1) * HALF]
                            first, last = c == 0, c == blocks - 1
                        ins = pe.matmul(o, v, pt[:, i * P:(i + 1) * P], start=first, stop=last)
                ins.then_inc(mixed_done, 1)

            with pe.Fori(0, LAYERS) as l:
                pe.wait_ge(score_free, l * NS + 1)
                for c in range(DC):
                    if c % 4 == 0:
                        pe.wait_ge(squared, l * 2 + c // 4 + 1)
                    ins = pe.matmul(score[:, 0:T], ones, squares_x[:, c, :], start=c == 0, stop=c == DC - 1)
                ins.then_inc(scored, 1)
                unit(l, 0)
                for u in range(HEAD, PREP):
                    if u in QUARTER:
                        for q in range(4):
                            quarter(l, u, q)
                            if (u, q) in TURN:
                                turn(l, TURN[u, q])
                    elif u - 1 not in QUARTER:
                        if UNITS[u][0] == "mq" and UNITS[u][2] == (0, 0):
                            pe.wait_ge(flip_free, l * NTR + 2 + 1)
                        unit(l, u)
                pe.wait_ge(flip_free, l * NTR + NN + 1)
                for b in range(BANKS + 2):
                    last = max(u for u in range(PREP) if BANK[u] == b)
                    pe.wait_ge(free_of(last), freed(l, last))
                pe.wait_ge(mixed_free, l * NM + 1)
                for n in range(ADAS):
                    ins = pick(pe, modrow[:, n, :], 8 * n)
                ins.then_inc(mixed_done, 1)
                taken[0] = 0
                for j in range(NJ + 1):
                    if j < NJ:
                        scores(l, j)
                    if j > 0:
                        values(l, j - 1)
                    while taken[0] < sum(QUARTERS[:j + 1]):
                        fill(l)
                pe.wait_ge(conv_ready, l + 1)
                pe.wait_ge(mixed_free, l * NM + NM + 1)
                for u in range(FILL, MERGED):
                    unit(l, u)
                for u in range(MERGED, NU, 2):
                    for q in range(4):
                        quarter(l, u, q)
            if debug != "layers":
                block_tensor(pe)

        @block.scalar
        def _(act):
            act.wait_ge(loaded, 48)
            act.sem_inc(flip_free, 1)
            act.activation(tanh_z[:, 0:2 * DC], cvec[:].rearrange("p c b -> p (c b)"), ACT.Tanh,
                           scale=0.5).then_inc(ctanh, 1)

            def squares_of(l, n, src, width):
                act.wait_ge(squares_used, l * NN + n + 1)
                act.activation(square[:, 0:width], src, ACT.Square).then_inc(squares, 1)

            def root(l, n):
                act.wait_ge(var_ready, l * NN + n + 1)
                act.activation(rs, var, ACT.Sqrt).then_inc(rs_ready, 1)

            def unflip(l, n):
                kind, _, who = UNITS[NORMED[n]]
                act.wait_ge(flipped, l * NTR + n + 1)
                t = who[-1]
                cols = slice(t * P, (t + 1) * P)
                v = flip[:, :].rearrange("p (a t) -> p a t", t=P)
                if kind == "lora":
                    act.activation(cT[:, 0, cols], v[:, 0, :], ACT.Copy, scale=l_("q_a", 0, 1))
                    act.activation(cT[:, 1, cols], v[:, 1, :], ACT.Copy, scale=l_("q_a", 1, 1))
                    ins = act.activation(cT[:, 2, cols], v[:, 2, :], ACT.Copy, scale=l_("kv_a", 0, 1))
                elif kind in ("dq", "dk"):
                    g = who[0]
                    dst = (dqT if kind == "dq" else dkT)[:, 4 * g:4 * g + 4, cols]
                    ins = act.activation(dst, v[:, 0:4, :], ACT.Copy,
                                         scale=l_("dil_q" if kind == "dq" else "dil_k", g, 1))
                else:
                    half = who[0]
                    dst = (mqT if kind == "mq" else mkT)[0:MQK, 4 * half:4 * half + 4, cols]
                    ins = act.activation(dst, v[0:MQK, 0:4, :], ACT.Copy,
                                         scale=MQK ** -0.5 if kind == "mq" else 1.0)
                ins.then_inc(flip_free, 1)

            def evacuate(l, u):
                kind, _, who = UNITS[u]
                b = bank_of(u)
                if kind in ("merge", "out", "ac", "ax", "ab"):
                    return
                if kind == "ada":
                    act.wait_ge(unit_done, done(l, u))
                    half = slice(T * (who[0] % 2), T * (who[0] % 2) + T)
                    act.activation(modrow[:, who[0] // 2, half], b[:, 0:T], ACT.Copy).then_inc(free_of(u), 1)
                    return
                if kind == "mkv":
                    act.wait_ge(copied, l * 4 + [x for x in range(NU) if UNITS[x][0] == "mkv"].index(u) + 1)
                    squares_of(l, NORMED.index(u), mc.rearrange("p a b -> p (a b)"), 384)
                    root(l, NORMED.index(u))
                    return
                act.wait_ge(unit_done, done(l, u))
                if kind == "lora":
                    squares_of(l, NORMED.index(u), b[:, 0:384], 384)
                elif kind in ("dq", "dk"):
                    squares_of(l, NORMED.index(u), b[:, :], W)
                elif kind == "mq":
                    squares_of(l, NORMED.index(u), b[:, 0:384], 384)
                if u in NORMED:
                    root(l, NORMED.index(u))
                elif kind == "dv":
                    g, t = who
                    act.activation(dv[:, t, g * W:(g + 1) * W], b[:, :], ACT.Copy).then_inc(free_of(u), 1)
                elif kind in ("z", "az"):
                    z = ZUNITS.index(u)
                    if z:
                        act.wait_ge(free_of(ZUNITS[z - 1]), freed(l, ZUNITS[z - 1]))
                    act.activation(tanh_z, b[:, :], ACT.Tanh, scale=0.5).then_inc(z_tanh, 1)
                elif kind == "gate":
                    n, p = who
                    for i in range(2):
                        c = 4 * n + 2 * p + i
                        ins = act.activation(gates[:, c, :], b[:, i * T:(i + 1) * T], ACT.Tanh, scale=0.5,
                                             bias=l_("b_gate", c, 1))
                    ins.then_inc(free_of(u), 1)

            def exp(l, j):
                job = JOBS[j]
                act.wait_ge(masked, l * NJ + j + 1)
                pr, st = probs[:, j % 2, :], stat[:, j % 2, :]
                if job[0] == "mla":
                    act.activation(pr[:, 0:P], pr[:, 0:P], ACT.Exp, bias=st[:, 2:3], accum_out=st[:, 4:5])
                    ins = act.activation(pr[:, P:384], pr[:, P:384], ACT.Exp, bias=st[:, 3:4],
                                         accum_out=st[:, 5:6])
                else:
                    n = 384 * (job[2] + 1)
                    ins = act.activation(pr[:, 0:n], pr[:, 0:n], ACT.Exp, bias=st[:, 2:3], accum_out=st[:, 4:5])
                ins.then_inc(exped, 1)

            def unflip_probs(l, j, r):
                rr = FIRST_ROUND[j] + r
                act.wait_ge(flipped, l * NTR + NN + rr + 1)
                if r == 0 and j >= 1:
                    act.wait_ge(mixed_done, l * NM + j + 1)
                act.activation(turned[:, rr % 2, 0:384], flip[:, 0:384], ACT.Copy).then_inc(flip_free, 1)

            split = [0]

            def split_to(l, k_end):
                while split[0] < k_end:
                    k = split[0]
                    split[0] += 1
                    m, layer = (k - PARTS, l) if k >= PARTS else (k - PARTS + NQ, l - 1)
                    if m % 4 == 3:
                        act.wait_ge(unit_done, done(layer, SPLIT[m // 4][1] + 1))
                    else:
                        act.wait_ge(quarter_used, used_count(layer, m))
                    tl = SPLIT[k // 4][0]
                    q = k % 4
                    if q == 0:
                        act.wait_ge(landed[tl % LRING], l * (16 * NT // LRING) + 16 * (tl // LRING + 1))
                    n = LORA if k < 4 else W
                    act.activation(w_hi[:, k % PARTS, :, 0:n],
                                   ring[:, tl % LRING, :].rearrange("p (c n) -> p c n", c=DC)[:, 2 * q:2 * q + 2, 0:n],
                                   ACT.Copy).then_inc(hi_done, 1)

            def stream_high(l, n, src):
                half = slice(4 * (n % 2), 4 * (n % 2) + 4)
                act.wait_ge(stream_ready, l * 4 + n + 1)
                act.activation(h_hi[:, half, :], src[:, half, :], ACT.Copy).then_inc(stream_hi, 1)

            with act.Fori(0, LAYERS) as l:
                for i in range(2):
                    u = NU - 3 + 2 * i
                    act.wait_ge(free_of(u), freed(l, u) - PER_BANK)
                    act.activation(squares_x[:, 4 * i:4 * i + 4, :], x[:, 4 * i:4 * i + 4, :],
                                   ACT.Square).then_inc(squared, 1)
                split[0] = 0
                split_to(l, PARTS)
                act.wait_ge(score_free, l * NS + 2)
                act.activation(rsx, varx, ACT.Sqrt).then_inc(rsx_ready, 1)
                act.wait_ge(par_ready, l + 1)
                stream_high(l, 0, normed_x)
                stream_high(l, 1, normed_x)
                evacuate(l, 0)
                for u in range(HEAD, PREP):
                    if u in QUARTER:
                        k = QUARTER[u]
                        for q in range(4):
                            split_to(l, k + q + 1 + PARTS)
                            if (u, q) in TURN:
                                unflip(l, NORMED.index(TURN[u, q]))
                        evacuate(l, u)
                        if k + 5 <= NQ_PREP:
                            split_to(l, k + 5 + PARTS)
                    else:
                        evacuate(l, u)
                for j in range(NJ + 1):
                    if j > 0:
                        unflip_probs(l, j - 1, 0)
                    if j < NJ:
                        exp(l, j)
                    for r in range(len(ROUNDS[j - 1]) if j else 0):
                        if r:
                            unflip_probs(l, j - 1, r)
                        split_to(l, min(NQ_PREP + sum(QUARTERS[:j]) + r + 1 + PARTS, NQ_FILL))
                    for u in DONE_IN[j]:
                        evacuate(l, u)
                    split_to(l, min(NQ_PREP + sum(QUARTERS[:j + 1]) + PARTS, NQ_FILL))
                split_to(l, NQ_FILL + PARTS)
                stream_high(l, 2, merged_x)
                stream_high(l, 3, merged_x)
                split_to(l, NQ)
            if debug != "layers":
                block_scalar(act)

        @block.gpsimd
        def _(pool):
            pool.sem_inc(lo_done, NQ)
            with pool.Fori(0, LAYERS) as l:
                for k in range(NQ):
                    tl = SPLIT[k // 4][0]
                    q = k % 4
                    n = LORA if k < 4 else W
                    pool.wait_ge(hi_done, l * NQ + k + 1)
                    pool.tensor_tensor(w_lo[:, k % PARTS, :, 0:n],
                                       ring[:, tl % LRING, :].rearrange("p (c n) -> p c n", c=DC)[:, 2 * q:2 * q + 2, 0:n],
                                       w_hi[:, k % PARTS, :, 0:n], ALU.subtract).then_inc(lo_done, 1)

        @block.vector
        def _(dve):
            steps = [0]
            base = [0]

            def link(ins):
                steps[0] += 1
                ins.then_inc(chain, 1)
                dve.wait_ge(chain, base[0] + steps[0])

            dve.wait_ge(loaded, 48)
            for s in (score_free, mixed_free, squares_used, *bank_free):
                dve.sem_inc(s, 1)
            link(dve.memset(up[:, :, 0:2], 0.0))
            link(dve.memset(var, 1.0))
            link(dve.memset(silu[:], 0.0))
            dve.wait_ge(ctanh, 1)
            link(dve.scalar_tensor_tensor(out=silu[:, :, 0:2], in0=tanh_z[:, 0:2 * DC].rearrange("p (c b) -> p c b", b=2),
                                          scalar=1.0, in1=cvec[:], op0=ALU.add, op1=ALU.mult))
            dve.tensor_scalar(silu[:, :, 0:2], silu[:, :, 0:2], 0.5, None, ALU.mult).then_inc(silu_ready, 1)
            start = steps[0]
            steps[0] = 0

            def mean(dst, src, n):
                return dve.tensor_scalar(dst, src, 1.0 / n, EPS, ALU.mult, ALU.add)

            def heads(v, n):
                return v.rearrange("p (a b) -> p a b", b=n)

            def rotate(v, cos, sin, n):
                a = v.shape[1]
                r0 = rope[:, 0, 0:a * n].rearrange("p (a two n) -> p a two n", a=a, two=2)
                r1 = rope[:, 1, 0:a * n].rearrange("p (a two n) -> p a two n", a=a, two=2)
                full = [P, a, 2, n // 2]
                part = [P, a, n // 2]
                dve.tensor_tensor(r0, v, cos.broadcast_to(full), ALU.mult)
                dve.tensor_tensor(r1[:, :, 0, :], v[:, :, 1, :], sin[:, :, 0, :].broadcast_to(part), ALU.mult)
                link(dve.tensor_tensor(r1[:, :, 1, :], v[:, :, 0, :], sin[:, :, 1, :].broadcast_to(part), ALU.mult))
                return dve.tensor_tensor(v, r0, r1, ALU.add)

            def stream_low(l, n, src):
                half = slice(4 * (n % 2), 4 * (n % 2) + 4)
                dve.wait_ge(stream_hi, l * 4 + n + 1)
                dve.tensor_tensor(h_lo[:, half, :], src[:, half, :], h_hi[:, half, :],
                                  ALU.subtract).then_inc(hready, 1)

            def normalize(l, u):
                kind, _, who = UNITS[u]
                n = NORMED.index(u)
                t = who[-1]
                b = bank_of(u)
                q = qn[:, n % QN, :]
                if kind == "mkv":
                    half = who[0]
                    dve.wait_ge(unit_done, done(l, u))
                    kv = heads(b[:, :], P)
                    mch = mc[:, :, :]
                    dve.tensor_copy(mch[:, :, 0:HALF], kv[:, :, 0:HALF])
                    dve.tensor_copy(mch[:, :, HALF:MQK], kpe[:, t:t + 1, :].broadcast_to([P, 4, MROPE])).then_inc(copied, 1)
                    dve.tensor_copy(heads(mv[:, t, half * 256:(half + 1) * 256], HALF),
                                    kv[:, :, HALF:P]).then_inc(free_of(u), 1)
                dve.wait_ge(squares, l * NN + n + 1)
                if kind == "lora":
                    link(dve.tensor_reduce(ssum[:, 0:1], square[:, 0:256], AX.X, ALU.add))
                    dve.tensor_reduce(ssum[:, 1:2], square[:, 256:384], AX.X, ALU.add).then_inc(squares_used, 1)
                    dve.wait_ge(squares_used, l * NN + n + 2)
                    link(mean(var[:, 0:1], ssum[:, 0:1], 256))
                    mean(var[:, 1:2], ssum[:, 1:2], 128).then_inc(var_ready, 1)
                else:
                    a, w = (8, HALF) if kind in ("dq", "dk") else (4, MQK)
                    dve.tensor_reduce(ssum[:, 0:a], heads(square[:, 0:a * w], w), AX.X,
                                      ALU.add).then_inc(squares_used, 1)
                    dve.wait_ge(squares_used, l * NN + n + 2)
                    mean(var[:, 0:a], ssum[:, 0:a], w).then_inc(var_ready, 1)
                dve.wait_ge(rs_ready, l * NN + n + 1)
                link(dve.reciprocal(rs, rs))
                if n >= QN:
                    dve.wait_ge(flipped, l * NTR + n - QN + 1)
                if kind == "lora":
                    link(dve.tensor_copy(kpe[:, t, :], b[:, 384:416]))
                    link(dve.tensor_scalar(q[:, 0:256], b[:, 0:256], rs[:, 0:1], None, ALU.mult))
                    dve.tensor_scalar(q[:, 256:384], b[:, 256:384], rs[:, 1:2], None,
                                      ALU.mult).then_inc(free_of(u), 1)
                    dve.wait_ge(free_of(u), freed(l, u))
                    dve.sem_inc(qn_ready, 1)
                elif kind in ("dq", "dk"):
                    link(dve.tensor_tensor(heads(q, HALF), heads(b[:, :], HALF),
                                           rs[:, 0:8].unsqueeze(2).broadcast_to([P, 8, HALF]), ALU.mult))
                    dve.sem_inc(free_of(u), 1)
                    dve.sem_inc(qn_ready, 1)
                else:
                    src = heads(b[:, 0:384], MQK) if kind == "mq" else mc[:, :, :]
                    qh = heads(q[:, 0:384], MQK)
                    link(dve.tensor_tensor(qh, src, rs[:, 0:4].unsqueeze(2).broadcast_to([P, 4, MQK]), ALU.mult))
                    if kind == "mq":
                        dve.sem_inc(free_of(u), 1)
                    g = l_("mla_q" if kind == "mq" else "mla_k").unsqueeze(1).broadcast_to([P, 4, MQK])
                    link(dve.tensor_tensor(qh, qh, g, ALU.mult))
                    cs = c_("cosm")[:, t * 32:(t + 1) * 32].rearrange("p (a two n) -> p a two n", a=1, two=2)
                    sn = c_("sinm")[:, t * 32:(t + 1) * 32].rearrange("p (a two n) -> p a two n", a=1, two=2)
                    rotate(qh[:, :, HALF:MQK].rearrange("p a (two n) -> p a two n", two=2), cs, sn,
                           MROPE).then_inc(qn_ready, 1)

            def evacuate(l, u):
                kind, _, who = UNITS[u]
                b = bank_of(u)
                free = free_of(u)
                if kind in ("dv", "gate", "ada"):
                    return
                if u in NORMED:
                    normalize(l, u)
                    return
                p = who[0] if kind == "merge" else who[-1]
                pair = slice(2 * p, 2 * p + 2)
                both = heads(b[:, :], T)
                if kind in ("z", "az"):
                    dve.wait_ge(z_tanh, l * len(ZUNITS) + ZUNITS.index(u) + 1)
                else:
                    dve.wait_ge(unit_done, done(l, u))
                if kind == "z":
                    dve.scalar_tensor_tensor(out=(yB, yC)[who[0]][:, pair, :], in0=heads(tanh_z, T), scalar=1.0,
                                             in1=both, op0=ALU.add, op1=ALU.mult).then_inc(free, 1)
                elif kind == "ac":
                    dve.tensor_copy(conv[:, pair, :], both).then_inc(free, 1)
                elif kind == "ax":
                    dve.wait_ge(free_of(u - 2), freed(l, u - 2))
                    dve.tensor_tensor(up[:, pair, 2:T + 2], conv[:, pair, :], both, ALU.mult).then_inc(free, 1)
                elif kind == "ab":
                    dve.wait_ge(free_of(u - 2), freed(l, u - 2))
                    for c in range(2 * p, 2 * p + 2):
                        link(dve.tensor_scalar(conv[:, c, :], up[:, c, 0:T], l_("conv_w", c, 1),
                                               l_("conv_b", c, 1), ALU.mult, ALU.add))
                        for tap in (1, 2):
                            link(dve.scalar_tensor_tensor(out=conv[:, c, :], in0=up[:, c, tap:tap + T],
                                                          scalar=l_("conv_w", 4 * tap + c, 1), in1=conv[:, c, :],
                                                          op0=ALU.mult, op1=ALU.add))
                    dve.tensor_tensor(conv[:, pair, :], conv[:, pair, :], both, ALU.mult).then_inc(free, 1)
                elif kind == "az":
                    dve.wait_ge(free_of(u - 2), freed(l, u - 2))
                    dve.scalar_tensor_tensor(out=heads(mtmp, T), in0=heads(tanh_z, T), scalar=1.0,
                                             in1=both, op0=ALU.add, op1=ALU.mult).then_inc(free, 1)
                    dve.wait_ge(free, freed(l, u))
                    ins = dve.scalar_tensor_tensor(out=conv[:, pair, :], in0=heads(mtmp, T), scalar=0.5,
                                                   in1=conv[:, pair, :], op0=ALU.mult, op1=ALU.mult)
                    if p == 1:
                        ins.then_inc(conv_ready, 1)
                    else:
                        link(ins)
                elif kind == "merge":
                    br = who[1]
                    gsl = gates[:, DC * br + 2 * p:DC * br + 2 * p + 2, :]
                    dst = merged_x[:, pair, :] if br == 0 else heads(mtmp, T)
                    dve.scalar_tensor_tensor(out=dst, in0=gsl, scalar=1.0, in1=both, op0=ALU.add,
                                             op1=ALU.mult).then_inc(free, 1)
                    dve.wait_ge(free, freed(l, u))
                    if br:
                        link(dve.tensor_tensor(merged_x[:, pair, :], merged_x[:, pair, :], heads(mtmp, T), ALU.add))
                    if br == 2 and p % 2 == 1:
                        dve.sem_inc(stream_ready, 1)
                    if u == MERGED - 1:
                        stream_low(l, 2, merged_x)
                        stream_low(l, 3, merged_x)
                elif kind == "out":
                    c = 4 * who[0] + 2 * p
                    dve.scalar_tensor_tensor(out=x[:, c:c + 2, :], in0=both, scalar=0.5, in1=x[:, c:c + 2, :],
                                             op0=ALU.mult, op1=ALU.add).then_inc(free, 1)

            def mask(l, j):
                job = JOBS[j]
                dve.wait_ge(scored, l * NS + j + 2)
                pr, st = probs[:, j % 2, :], stat[:, j % 2, :]
                if job[0] == "mla":
                    dve.tensor_tensor(pr[:, 0:384], score[:, 0:384], c_("mask"), ALU.add).then_inc(score_free, 1)
                    dve.wait_ge(score_free, l * NS + j + 3)
                    dve.tensor_reduce(st[:, 0:1], pr[:, 0:P], AX.X, ALU.max)
                    link(dve.tensor_reduce(st[:, 1:2], pr[:, P:384], AX.X, ALU.max))
                    dve.tensor_scalar(st[:, 2:4], st[:, 0:2], -1.0, None, ALU.mult).then_inc(masked, 1)
                else:
                    _, hd, t = job
                    n = (t + 1) * P
                    for g in range(GROUPS):
                        bias = c_("dist")[:, 384 * g + P * t:384 * g + P * t + n]
                        ins = dve.scalar_tensor_tensor(out=pr[:, g * n:(g + 1) * n], in0=bias, scalar=slope(g, hd),
                                                       in1=score[:, g * n:(g + 1) * n], op0=ALU.mult, op1=ALU.add)
                        if g < GROUPS - 1:
                            link(ins)
                    ins.then_inc(score_free, 1)
                    dve.wait_ge(score_free, l * NS + j + 3)
                    link(dve.tensor_reduce(st[:, 0:1], pr[:, 0:3 * n], AX.X, ALU.max))
                    dve.tensor_scalar(st[:, 2:3], st[:, 0:1], -1.0, None, ALU.mult).then_inc(masked, 1)

            def divide(l, j):
                job = JOBS[j]
                pr, st = probs[:, j % 2, :], stat[:, j % 2, :]
                dve.wait_ge(exped, l * NJ + j + 1)
                if job[0] == "mla":
                    link(dve.reciprocal(st[:, 6:8], st[:, 4:6]))
                    link(dve.tensor_scalar(pr[:, 0:P], pr[:, 0:P], st[:, 6:7], None, ALU.mult))
                    dve.tensor_scalar(pr[:, P:384], pr[:, P:384], st[:, 7:8], None,
                                      ALU.mult).then_inc(probs_ready, 1)
                else:
                    n = 384 * (job[2] + 1)
                    link(dve.reciprocal(st[:, 6:7], st[:, 4:5]))
                    dve.tensor_scalar(pr[:, 0:n], pr[:, 0:n], st[:, 6:7], None, ALU.mult).then_inc(probs_ready, 1)

            def gated(l, j):
                job = JOBS[j]
                hd = job[1]
                lo = HALF * (hd % 2)
                dve.wait_ge(mixed_done, l * NM + j + 2)
                y = yB if job[0] == "mla" else yC
                cols = slice(0, T) if job[0] == "mla" else slice(job[2] * P, (job[2] + 1) * P)
                n = T if job[0] == "mla" else P
                dst = y[lo:lo + HALF, hd // 2, cols]
                dve.scalar_tensor_tensor(out=dst, in0=mixed[lo:lo + HALF, 0:n], scalar=0.5, in1=dst,
                                         op0=ALU.mult, op1=ALU.mult).then_inc(mixed_free, 1)

            with dve.Fori(0, LAYERS) as l:
                base[0] = l * PER["layer"] + start
                dve.wait_ge(par_loaded, l * 16 + 16)
                link(dve.tensor_scalar(l_("dil_q"), l_("dil_q"), HALF ** -0.5, None, ALU.mult))
                dve.tensor_scalar(l_("b_gate"), l_("b_gate"), 0.5, None, ALU.mult).then_inc(par_ready, 1)
                dve.wait_ge(par_ready, l + 1)
                dve.wait_ge(scored, l * NS + 1)
                dve.tensor_scalar(varx, score[:, 0:T], 1.0 / D, EPS, ALU.mult, ALU.add).then_inc(score_free, 1)
                dve.wait_ge(rsx_ready, l + 1)
                link(dve.reciprocal(rsx, rsx))
                for c in range(DC):
                    ins = dve.scalar_tensor_tensor(out=normed_x[:, c, :], in0=x[:, c, :], scalar=l_("norm_g", c, 1),
                                                   in1=rsx, op0=ALU.mult, op1=ALU.mult)
                    if c % 4 == 3:
                        ins.then_inc(stream_ready, 1)
                stream_low(l, 0, normed_x)
                stream_low(l, 1, normed_x)
                for u in range(PREP):
                    evacuate(l, u)
                dve.wait_ge(mixed_done, l * NM + 1)
                dve.tensor_copy(mod[:, bass.ds(l * 4 * ADAS, 4 * ADAS), :],
                                mixed[:, 0:8 * ADAS].rearrange("p (c b) -> p c b", b=2)).then_inc(mixed_free, 1)
                for j in range(NJ + 1):
                    if j < NJ:
                        mask(l, j)
                    for u in DONE_IN[j - 1] if j else ():
                        evacuate(l, u)
                    if j < NJ:
                        divide(l, j)
                    if j > 0:
                        gated(l, j - 1)
                for u in DONE_IN[NJ]:
                    evacuate(l, u)
                dve.wait_ge(free_of(FILL - 1), freed(l, FILL - 1))
                dve.wait_ge(free_of(FILL - 2), freed(l, FILL - 2))
                for u in range(FILL, NU):
                    evacuate(l, u)
                assert steps[0] == PER["layer"], steps[0]
            if debug != "layers":
                steps[0] += start + (LAYERS - 1) * PER["layer"]
                base[0] = 0
                block_vector(dve, link, steps, base)


def constants():
    import numpy as np
    out = {}
    p = np.arange(P)
    out["ident"] = np.eye(P)
    out["ones"] = np.ones((P, P))
    tok = np.arange(T, dtype=np.float32).reshape(TT, P).T
    inv = 10000.0 ** (-np.arange(0, MROPE, 2, dtype=np.float32) / MROPE)
    ang = tok[:, :, None] * inv.astype(np.float32)
    out["cosm"] = np.stack([np.cos(ang), np.cos(ang)], axis=2)
    out["sinm"] = np.stack([-np.sin(ang), np.sin(ang)], axis=2)
    query = np.concatenate([np.broadcast_to(p[:, None], (P, P)), np.broadcast_to(p[:, None] + P, (P, T))], axis=1)
    key = np.concatenate([np.arange(P), np.arange(T)])[None, :]
    far = query - key
    out["mask"] = np.where(far >= 0, 0.0, MASKED)
    out["dist"] = np.stack([np.where((far >= 0) & (far % d == 0) & (far // d <= w // d), -far, MASKED)
                            for w, d in ((128, 1), (512, 4), (2048, 16))], axis=1)
    out["iota"] = np.broadcast_to(np.concatenate([np.arange(SLOTS)] * 4), (P, 2 * P))
    inv = 10000.0 ** (-np.arange(16, dtype=np.float32) / 16)
    axes = np.stack([tok // 64, tok % 64], axis=2)
    ang = axes[:, :, :, None] * inv.astype(np.float32)
    out["cosx"] = np.stack([np.cos(ang), np.cos(ang)], axis=3)
    out["sinx"] = np.stack([-np.sin(ang), np.sin(ang)], axis=3)
    out["before"] = (p[:, None] < p[None, :])
    out["pick"] = p[:, None] % 32 == np.arange(2)[None, :]
    out["expert"] = np.broadcast_to(np.tile(np.arange(NEXP), 3), (P, 96))
    out["start"] = np.broadcast_to(np.repeat(np.arange(1, 4) * SLOTS, NEXP), (P, 96))
    out["job"] = np.broadcast_to(np.arange(1, MAXJOBS + 1), (P, MAXJOBS))
    return np.concatenate([out[k].reshape(P, -1).astype(np.float32) for k in CONSTS], axis=1)


def arrange(inputs):
    import numpy as np

    def f(name):
        return np.ascontiguousarray(inputs[name])

    def fm(a):
        a = a.reshape(*a.shape[:-1], -1, P)
        return np.moveaxis(a, -1, 0)

    def rows(a):
        return np.broadcast_to(a.reshape(1, -1), (P, a.size))

    x, lay, blk = f("x"), {}, {}
    lay["norm_g"] = fm(f("norm_g"))
    lay["b_gate"] = fm(f("b_gate"))
    lay["conv_w"] = fm(f("conv_w"))
    lay["conv_b"] = fm(f("conv_b"))
    lay["q_a"] = fm(f("q_a_norm_g"))
    lay["kv_a"] = fm(f("kv_a_norm_g"))
    for k in "qk":
        g = f(f"dil_{k}_norm_g")
        lay[f"dil_{k}"] = np.moveaxis(np.concatenate([g, g], axis=2), 2, 0)
        g = f(f"mla_{k}_norm_g")
        lay[f"mla_{k}"] = np.broadcast_to(g[None], (P, *g.shape))
    layer_params = np.concatenate([lay[k].reshape(P, LAYERS, -1) for k in LAYER_PARAMS], axis=2)
    blk["b_ada"] = fm(f("b_ada_2")[0])
    blk["g_attn"] = fm(f("g_attn_2")[0])
    blk["g_ffn"] = fm(f("g_ffn_2")[0])
    blk["g_final"] = fm(f("g_final_2"))
    blk["subln"] = fm(f("diff_subln_2")[0])
    cs = np.stack([fm(f("c_2")[0]), fm(f("c_ctx_2"))], axis=2)
    blk["gqa_q"] = rows(f("gqa_q_norm_2"))
    blk["gqa_k"] = rows(f("gqa_k_norm_2"))
    blk["lam"] = rows(f("diff_lambda_2"))
    blk["b_router"] = rows(f("b_router_2"))
    blk["w_router"] = np.moveaxis(f("w_router_2")[0].reshape(DC, P, NEXP), 1, 0)
    block_params = np.concatenate([blk[k].reshape(P, -1) for k in BLOCK_PARAMS], axis=1)
    return dict(
        in_c=np.ascontiguousarray(cs.reshape(P, -1)), in_x=np.ascontiguousarray(np.moveaxis(x[0].reshape(T, DC, P), (0, 1, 2), (2, 1, 0))),
        in_ctx=np.ascontiguousarray(np.moveaxis(f("ctx_2")[0].reshape(T, DC, P), (0, 1, 2), (2, 1, 0))),
        in_consts=constants(), in_layer_params=np.ascontiguousarray(layer_params),
        in_block_params=np.ascontiguousarray(block_params),
        in_w_in=f("w_in"), in_w_uq=f("w_uq"), in_w_ukv=f("w_ukv"), in_w_out_a=f("w_out_a"),
        in_w_out_b=f("w_out_b"), in_w_out_c=f("w_out_c"), in_w_o=f("w_o"), in_w_ada=f("w_ada_2")[0],
        in_w_qkv=f("w_qkv_2")[0], in_w_o2=f("w_o_2")[0], in_e_in=f("w_in_2")[0], in_eb_in=f("b_in_2")[0],
        in_e_out=f("w_out_2")[0], in_eb_out=f("b_out_2")[0])


def kernel(**inputs):
    import numpy as np
    from concourse import bacc
    from concourse.bass_utils import run_bass_kernel_spmd

    arrays = arrange(inputs)
    nc = bacc.Bacc("TRN2", target_bir_lowering=False, num_devices=1)
    args = [nc.dram_tensor(f"{name}_dram", a.shape, mybir.dt.from_np(a.dtype), kind="ExternalInput").ap()
            for name, a in arrays.items()]
    out = nc.dram_tensor("out_0_dram", (P, DC, T), F32, kind="ExternalOutput").ap()
    build(nc, *args, out)
    r = run_bass_kernel_spmd(nc, [{f"{name}_dram": a for name, a in arrays.items()}], core_ids=[0])
    got = r.results[0]["out_0_dram"]
    return np.ascontiguousarray(np.moveaxis(got, (0, 1, 2), (2, 1, 0)).reshape(1, T, D))
```
